# Optimizing a Trainium2 kernel written in Bass

```python
import jax
import jax.numpy as jnp
from jax import lax
import numpy as np
import math
import jax, jax.numpy as jnp

D_MODEL = 1024
BATCH = 1
SEQ = 512
DEPTH = 2

GRID_W = 64
CTX_LEN = 256
N_MIXERS = 2
N_ATT = (DEPTH + 1) // 2
N_RWKV = DEPTH // 2
HEAD_DIM = 64
ATT_Q_HEADS = D_MODEL // HEAD_DIM
ATT_KV_HEADS = ATT_Q_HEADS // 4
ATT_GROUP = ATT_Q_HEADS // ATT_KV_HEADS
WINDOW = 128
BLOCK = 128
ROPE_BASE = 10000.0
RWKV_HEADS = D_MODEL // HEAD_DIM
DECAY_LORA = 64
ICLR_LORA = 64
GATE_LORA = 128
D_FF = 4 * D_MODEL
NORM_EPS = 1e-6
GN_EPS = 64e-5
NEG_INF = -1e30
F32 = jnp.float32


def rmsnorm(x, g):
    x32 = x.astype(F32)
    y = x32 * lax.rsqrt(jnp.mean(x32 * x32, axis=-1, keepdims=True) + NORM_EPS)
    return (y * g.astype(F32)).astype(x.dtype)

def rope_1d(t, pos):
    half = t.shape[-1] // 2
    freqs = ROPE_BASE ** (-jnp.arange(half, dtype=F32) / half)
    ang = pos.astype(F32)[:, None, None] * freqs
    cos, sin = jnp.cos(ang), jnp.sin(ang)
    t1, t2 = t[..., :half].astype(F32), t[..., half:].astype(F32)
    return jnp.concatenate([t1 * cos - t2 * sin, t1 * sin + t2 * cos], axis=-1).astype(t.dtype)

def rope_2d(t, rows, cols):
    r = HEAD_DIM // 2
    return jnp.concatenate([rope_1d(t[..., :r], rows), rope_1d(t[..., r:], cols)], axis=-1)

def sq_relu_mlp(h, w1, w2):
    return jnp.square(jax.nn.relu(h @ w1)) @ w2

def attention_mixer(h, hc, w_qkv, q_gain, k_gain, sink, w_o, rows, cols, ctx_out):
    B, S, _ = h.shape
    L = hc.shape[1]
    nq, nk = ATT_Q_HEADS * HEAD_DIM, ATT_KV_HEADS * HEAD_DIM

    def project(t):
        T = t.shape[1]
        qkv = t @ w_qkv
        q = rmsnorm(qkv[..., :nq].reshape(B, T, ATT_Q_HEADS, HEAD_DIM), q_gain)
        k = rmsnorm(qkv[..., nq:nq + nk].reshape(B, T, ATT_KV_HEADS, HEAD_DIM), k_gain)
        v = qkv[..., nq + nk:].reshape(B, T, ATT_KV_HEADS, HEAD_DIM)
        return q, k, v

    q, k, v = project(h)
    q, k = rope_2d(q, rows, cols), rope_2d(k, rows, cols)
    qc, kc, vc = project(hc)
    scale = HEAD_DIM ** -0.5
    sink_logit = sink.astype(F32).reshape(ATT_KV_HEADS, ATT_GROUP, 1, 1)

    nb = S // BLOCK
    qb = q.reshape(B, nb, BLOCK, ATT_KV_HEADS, ATT_GROUP, HEAD_DIM)

    def band(t):
        tp = jnp.pad(t, ((0, 0), (BLOCK, BLOCK), (0, 0), (0, 0))).reshape(B, nb + 2, BLOCK, ATT_KV_HEADS, HEAD_DIM)
        return jnp.concatenate([tp[:, :-2], tp[:, 1:-1], tp[:, 2:]], axis=2)

    kw, vw = band(k), band(v)
    s_win = jnp.einsum('bnqhgd,bnkhd->bnhgqk', qb, kw).astype(F32) * scale
    s_ctx = jnp.einsum('bnqhgd,blhd->bnhgql', qb, kc).astype(F32) * scale
    blk = jnp.arange(nb)[:, None, None] * BLOCK
    qpos = blk + jnp.arange(BLOCK)[None, :, None]
    kpos = blk - BLOCK + jnp.arange(3 * BLOCK)[None, None, :]
    mask = (jnp.abs(kpos - qpos) <= WINDOW) & (kpos >= 0) & (kpos < S)
    s_win = jnp.where(mask[None, :, None, None], s_win, NEG_INF)
    sinks = jnp.broadcast_to(sink_logit, s_win.shape[:-1] + (1,))
    p = jax.nn.softmax(jnp.concatenate([s_win, s_ctx, sinks], axis=-1), axis=-1)
    p_win = p[..., :3 * BLOCK].astype(v.dtype)
    p_ctx = p[..., 3 * BLOCK:3 * BLOCK + L].astype(v.dtype)
    o = jnp.einsum('bnhgqk,bnkhd->bnqhgd', p_win, vw) + jnp.einsum('bnhgql,blhd->bnqhgd', p_ctx, vc)
    y = o.reshape(B, S, D_MODEL) @ w_o
    if not ctx_out:
        return y, None

    qcg = qc.reshape(B, L, ATT_KV_HEADS, ATT_GROUP, HEAD_DIM)
    s_cc = jnp.einsum('blhgd,bmhd->bhglm', qcg, kc).astype(F32) * scale
    sinks_c = jnp.broadcast_to(sink_logit, s_cc.shape[:-1] + (1,))
    pc = jax.nn.softmax(jnp.concatenate([s_cc, sinks_c], axis=-1), axis=-1)[..., :L].astype(vc.dtype)
    yc = jnp.einsum('bhglm,bmhd->blhgd', pc, vc).reshape(B, L, D_MODEL) @ w_o
    return y, yc

def wkv_scan(r, w, k, v, a, b, s0, reverse):
    def step(s, inp):
        r_t, w_t, k_t, v_t, a_t, b_t = inp
        sa = jnp.einsum('bhvk,bhk->bhv', s, a_t)
        s = s * w_t[:, :, None, :] + sa[..., None] * b_t[:, :, None, :] + v_t[..., None] * k_t[:, :, None, :]
        return s, jnp.einsum('bhvk,bhk->bhv', s, r_t)

    xs = tuple(jnp.moveaxis(t, 1, 0) for t in (r, w, k, v, a, b))
    s_final, ys = lax.scan(step, s0, xs, reverse=reverse)
    return s_final, jnp.moveaxis(ys, 0, 1)

def rwkv_features(h, mu, w_rkv, w0, w1, w2, a0, a1, a2, k_k, k_a):
    B, T, _ = h.shape
    hn = (RWKV_HEADS, HEAD_DIM)
    hp = jnp.pad(h, ((0, 0), (1, 1), (0, 0)))
    xx = 0.5 * (hp[:, :-2] + hp[:, 2:]) - h
    xr, xw, xk, xv, xa, xg = [h + xx * mu[m] for m in range(6)]

    def heads(t):
        return t.astype(F32).reshape(B, T, *hn)

    r = heads(xr @ w_rkv[0])
    k = heads(xk @ w_rkv[1])
    v = heads(xv @ w_rkv[2])
    decay = tuple(
        heads(jnp.exp(-jnp.exp(-jax.nn.softplus(-(w0[d] + jnp.tanh(xw @ w1[d]) @ w2[d]).astype(F32)) - 0.5)))
        for d in range(2))
    a = heads(jax.nn.sigmoid((a0 + (xa @ a1) @ a2).astype(F32)))
    kk = k * k_k.astype(F32).reshape(hn)
    kk = kk / jnp.maximum(jnp.sqrt(jnp.sum(kk * kk, axis=-1, keepdims=True)), 1e-12)
    k = k * (1.0 + (a - 1.0) * k_a.astype(F32).reshape(hn))
    return r, k, v, -kk, kk * a, decay, xg

def group_norm(y, g, b):
    hn = (RWKV_HEADS, HEAD_DIM)
    mean = jnp.mean(y, axis=-1, keepdims=True)
    var = jnp.mean(jnp.square(y - mean), axis=-1, keepdims=True)
    return (y - mean) * lax.rsqrt(var + GN_EPS) * g.astype(F32).reshape(hn) + b.astype(F32).reshape(hn)

def rwkv_readout(y_fwd, y_bwd, r, k, v, xg, g1, g2, r_k, gn_g, gn_b, w_o):
    B, T = xg.shape[:2]
    bonus = jnp.sum(r * k * r_k.astype(F32), axis=-1, keepdims=True) * v

    def gate(d):
        return (jax.nn.sigmoid(xg @ g1[d]) @ g2[d]).astype(F32).reshape(B, T, RWKV_HEADS, HEAD_DIM)

    o = (group_norm(y_fwd, gn_g, gn_b) + bonus) * gate(0) + (group_norm(y_bwd, gn_g, gn_b) + bonus) * gate(1)
    return o.reshape(B, T, D_MODEL).astype(xg.dtype) @ w_o

def rwkv_mixer(h, hc, mu, w_rkv, w0, w1, w2, a0, a1, a2, g1, g2, k_k, k_a, r_k, gn_g, gn_b, w_o, ctx_out):
    feat = (mu, w_rkv, w0, w1, w2, a0, a1, a2, k_k, k_a)
    rc, kc, vc, nac, bc, decc, xgc = rwkv_features(hc, *feat)
    r, k, v, na, b, dec, xg = rwkv_features(h, *feat)
    zero = jnp.zeros((h.shape[0], RWKV_HEADS, HEAD_DIM, HEAD_DIM), F32)
    s_fwd, yc_fwd = wkv_scan(rc, decc[0], kc, vc, nac, bc, zero, False)
    s_bwd, yc_bwd = wkv_scan(rc, decc[1], kc, vc, nac, bc, zero, True)
    _, y_fwd = wkv_scan(r, dec[0], k, v, na, b, s_fwd, False)
    _, y_bwd = wkv_scan(r, dec[1], k, v, na, b, s_bwd, True)
    ro = (g1, g2, r_k, gn_g, gn_b, w_o)
    y = rwkv_readout(y_fwd, y_bwd, r, k, v, xg, *ro)
    if not ctx_out:
        return y, None
    return y, rwkv_readout(yc_fwd, yc_bwd, rc, kc, vc, xgc, *ro)

def first_inputs(seed: int = 0) -> dict:
    key = jax.random.key(seed)
    ks = iter(jax.random.split(key, 40))
    D = D_MODEL

    def nrm(shape, s):
        return jax.random.normal(next(ks), shape, F32) * s

    def unif(shape, lo, hi):
        return jax.random.uniform(next(ks), shape, F32, lo, hi)

    qkv_cols = (ATT_Q_HEADS + 2 * ATT_KV_HEADS) * HEAD_DIM
    return {
        'x': nrm((BATCH, SEQ, D), 1.0),
        'c': nrm((BATCH, D), 1.0),
        'ctx': nrm((BATCH, CTX_LEN, D), 1.0),
        'c_ctx': nrm((D,), 1.0),
        'ada_w': nrm((DEPTH, D, 6 * D), 0.5 * D ** -0.5),
        'ada_b': nrm((DEPTH, 6 * D), 0.01),
        'norm1_g': 1.0 + nrm((DEPTH, D), 0.1),
        'norm2_g': 1.0 + nrm((DEPTH, D), 0.1),
        'mlp_w1': nrm((DEPTH, D, D_FF), D ** -0.5),
        'mlp_w2': nrm((DEPTH, D_FF, D), D_FF ** -0.5),
        'att_w_qkv': nrm((N_ATT, D, qkv_cols), D ** -0.5),
        'att_q_gain': 1.0 + nrm((N_ATT, HEAD_DIM), 0.1),
        'att_k_gain': 1.0 + nrm((N_ATT, HEAD_DIM), 0.1),
        'att_sink': nrm((N_ATT, ATT_Q_HEADS), 1.0),
        'att_w_o': nrm((N_ATT, D, D), D ** -0.5),
        'rwkv_mu': unif((N_RWKV, 6, D), 0.0, 1.0),
        'rwkv_w_rkv': nrm((N_RWKV, 3, D, D), D ** -0.5),
        'rwkv_w0': unif((N_RWKV, 2, D), -6.0, 1.0),
        'rwkv_w1': nrm((N_RWKV, 2, D, DECAY_LORA), D ** -0.5),
        'rwkv_w2': nrm((N_RWKV, 2, DECAY_LORA, D), 0.5 * DECAY_LORA ** -0.5),
        'rwkv_a0': nrm((N_RWKV, D), 0.5),
        'rwkv_a1': nrm((N_RWKV, D, ICLR_LORA), D ** -0.5),
        'rwkv_a2': nrm((N_RWKV, ICLR_LORA, D), ICLR_LORA ** -0.5),
        'rwkv_g1': nrm((N_RWKV, 2, D, GATE_LORA), D ** -0.5),
        'rwkv_g2': nrm((N_RWKV, 2, GATE_LORA, D), GATE_LORA ** -0.5),
        'rwkv_k_k': 0.85 + nrm((N_RWKV, D), 0.05),
        'rwkv_k_a': 1.0 + nrm((N_RWKV, D), 0.05),
        'rwkv_r_k': nrm((N_RWKV, RWKV_HEADS, HEAD_DIM), 0.1),
        'rwkv_gn_g': 1.0 + nrm((N_RWKV, D), 0.1),
        'rwkv_gn_b': nrm((N_RWKV, D), 0.01),
        'rwkv_w_o': nrm((N_RWKV, D, D), D ** -0.5),
    }

def first_block(x, c, ctx, c_ctx, ada_w, ada_b, norm1_g, norm2_g, mlp_w1, mlp_w2,
              att_w_qkv, att_q_gain, att_k_gain, att_sink, att_w_o,
              rwkv_mu, rwkv_w_rkv, rwkv_w0, rwkv_w1, rwkv_w2, rwkv_a0, rwkv_a1, rwkv_a2,
              rwkv_g1, rwkv_g2, rwkv_k_k, rwkv_k_a, rwkv_r_k, rwkv_gn_g, rwkv_gn_b, rwkv_w_o):
    S = x.shape[1]
    n_rows = S // GRID_W
    rows = jnp.repeat(jnp.arange(n_rows), GRID_W)
    cols = jnp.tile(jnp.arange(GRID_W), n_rows)
    silu_c = jax.nn.silu(c)[:, None, :]
    silu_cc = jax.nn.silu(c_ctx)[None, None, :]
    xc = ctx
    for i in range(DEPTH):
        ctx_out = i < DEPTH - 1
        j = i // N_MIXERS
        sh1, sc1, gt1, sh2, sc2, gt2 = jnp.split(silu_c @ ada_w[i] + ada_b[i], 6, axis=-1)
        csh1, csc1, cgt1, csh2, csc2, cgt2 = jnp.split(silu_cc @ ada_w[i] + ada_b[i], 6, axis=-1)
        h = rmsnorm(x, norm1_g[i]) * (1.0 + sc1) + sh1
        hc = rmsnorm(xc, norm1_g[i]) * (1.0 + csc1) + csh1
        if i % N_MIXERS == 0:
            y, yc = attention_mixer(h, hc, att_w_qkv[j], att_q_gain[j], att_k_gain[j], att_sink[j],
                                    att_w_o[j], rows, cols, ctx_out)
        else:
            y, yc = rwkv_mixer(h, hc, rwkv_mu[j], rwkv_w_rkv[j], rwkv_w0[j], rwkv_w1[j], rwkv_w2[j],
                               rwkv_a0[j], rwkv_a1[j], rwkv_a2[j], rwkv_g1[j], rwkv_g2[j],
                               rwkv_k_k[j], rwkv_k_a[j], rwkv_r_k[j], rwkv_gn_g[j], rwkv_gn_b[j],
                               rwkv_w_o[j], ctx_out)
        x = x + gt1 * y
        x = x + gt2 * sq_relu_mlp(rmsnorm(x, norm2_g[i]) * (1.0 + sc2) + sh2, mlp_w1[i], mlp_w2[i])
        if ctx_out:
            xc = xc + cgt1 * yc
            xc = xc + cgt2 * sq_relu_mlp(rmsnorm(xc, norm2_g[i]) * (1.0 + csc2) + csh2, mlp_w1[i], mlp_w2[i])
    return x


PLE_DIM = 256
N_EVEN = (DEPTH + 1) // 2
N_ODD = DEPTH // 2

DA_HEADS = 4
DA_HEAD_DIM = 64
DA_V_DIM = 2 * DA_HEAD_DIM
DA_QK_WIDTH = DA_HEADS * 2 * DA_HEAD_DIM
DA_WIDTH = DA_HEADS * DA_V_DIM

HG_HEADS = 4
HG_KDIM = 128
HG_VDIM = 128
HG_KWIDTH = HG_HEADS * HG_KDIM
HG_WIDTH = HG_HEADS * HG_VDIM
HG_CHUNK = 64

DL_HEADS = 16
DL_HEAD_DIM = D_MODEL // DL_HEADS
DL_PAIRS = ((128, 1), (512, 4), (2048, 16))

FFN_DIM = 4 * D_MODEL
ROPE_THETA = 500000.0
ROT_DIM = 64 // 4
ALPHA = (2 * DEPTH) ** 0.25
BETA = (8 * DEPTH) ** -0.25
LN_EPS = 1e-5
Q_BLOCK = 128


def layer_norm(x, g, b):
    xf = x.astype(jnp.float32)
    mu = jnp.mean(xf, -1, keepdims=True)
    var = jnp.mean(jnp.square(xf - mu), -1, keepdims=True)
    return ((xf - mu) * lax.rsqrt(var + LN_EPS) * g + b).astype(x.dtype)

def rms_norm(x, g):
    xf = x.astype(jnp.float32)
    return (xf * lax.rsqrt(jnp.mean(xf * xf, -1, keepdims=True) + LN_EPS) * g).astype(x.dtype)

def rope_tables(seq):
    inv = ROPE_THETA ** (-jnp.arange(0, ROT_DIM, 2, dtype=jnp.float32) / ROT_DIM)
    ang = jnp.arange(seq, dtype=jnp.float32)[:, None] * inv[None, :]
    return jnp.cos(ang), jnp.sin(ang)

def partial_rope(x, cos, sin):
    half = ROT_DIM // 2
    x1, x2, xp = x[..., :half], x[..., half:ROT_DIM], x[..., ROT_DIM:]
    c, s = cos.astype(x.dtype), sin.astype(x.dtype)
    return jnp.concatenate([x1 * c - x2 * s, x1 * s + x2 * c, xp], axis=-1)

def diff_attention(qa, ka, va, lam_params, sub_g, lam_init, cos, sin):
    B, S = qa.shape[:2]
    q = partial_rope(qa.transpose(0, 2, 3, 1, 4), cos, sin) * (DA_HEAD_DIM ** -0.5)
    k = partial_rope(ka.transpose(0, 2, 3, 1, 4), cos, sin)
    v = va.transpose(0, 2, 1, 3)
    lp = lam_params.astype(jnp.float32)
    lam = jnp.exp(jnp.sum(lp[0] * lp[1])) - jnp.exp(jnp.sum(lp[2] * lp[3])) + lam_init
    nb = S // Q_BLOCK
    qb = q.reshape(B, DA_HEADS, 2, nb, Q_BLOCK, DA_HEAD_DIM).transpose(3, 0, 1, 2, 4, 5)
    kpos = jnp.arange(S)

    def block(args):
        qi, i = args
        s = jnp.einsum('bhcqd,bhckd->bhcqk', qi, k).astype(jnp.float32)
        qpos = i * Q_BLOCK + jnp.arange(Q_BLOCK)
        s = jnp.where(kpos[None, :] <= qpos[:, None], s, -jnp.inf)
        pr = jax.nn.softmax(s, axis=-1)
        a = pr[:, :, 0] - lam * pr[:, :, 1]
        return jnp.einsum('bhqk,bhkd->bhqd', a.astype(v.dtype), v)

    o = lax.map(block, (qb, jnp.arange(nb)))
    o = o.transpose(1, 2, 0, 3, 4).reshape(B, DA_HEADS, S, DA_V_DIM)
    o = rms_norm(o, sub_g) * (1.0 - lam_init)
    return o.transpose(0, 2, 1, 3).reshape(B, S, DA_WIDTH)

def hgrn2(hq, hf, hi, hg, lb, out_g):
    B, S, H, dk = hq.shape
    dv = hi.shape[-1]
    f32 = jnp.float32
    q = jax.nn.silu(hq.astype(f32))
    f = lb + (1.0 - lb) * jax.nn.sigmoid(hf.astype(f32))
    kk = 1.0 - f
    logf = jnp.log(f)
    C = HG_CHUNK
    n = S // C

    def chunks(t):
        return t.reshape(B, n, C, H, t.shape[-1]).transpose(1, 0, 3, 2, 4)

    qc, kc, lc, vc = chunks(q), chunks(kk), chunks(logf), chunks(hi.astype(f32))
    b = jnp.cumsum(lc, axis=-2)
    b_last = b[..., C - 1:C, :]
    b_mid = b[..., C // 2 - 1:C // 2, :]
    a = jnp.einsum('nbhtk,nbhsk->nbhts', qc * jnp.exp(b - b_mid), kc * jnp.exp(b_mid - b))
    a = jnp.where(jnp.tril(jnp.ones((C, C), bool)), a, 0.0)
    o_intra = jnp.einsum('nbhts,nbhsv->nbhtv', a, vc)
    q_out = qc * jnp.exp(b)
    k_st = kc * jnp.exp(b_last - b)
    decay = jnp.exp(b_last[..., 0, :])

    def step(state, xs):
        qo, ks, vv, dc = xs
        o_inter = jnp.einsum('bhtk,bhkv->bhtv', qo, state)
        state = dc[..., None] * state + jnp.einsum('bhsk,bhsv->bhkv', ks, vv)
        return state, o_inter

    s0 = jnp.zeros((B, H, dk, dv), f32)
    _, o_inter = lax.scan(step, s0, (q_out, k_st, vc, decay))
    o = (o_intra + o_inter).transpose(1, 0, 3, 2, 4).reshape(B, S, H, dv)
    o = rms_norm(o, out_g) * jax.nn.silu(hg.astype(f32))
    return o.reshape(B, S, H * dv).astype(hi.dtype)

def even_mixer(x, w_in, w_out, lam_params, sub_g, lb, hg_g, lam_init, cos, sin):
    B, S, _ = x.shape
    h = x @ w_in
    sizes = (DA_QK_WIDTH, DA_QK_WIDTH, DA_WIDTH, HG_KWIDTH, HG_KWIDTH, HG_WIDTH, HG_WIDTH)
    cuts = [sum(sizes[:i + 1]) for i in range(len(sizes) - 1)]
    qa, ka, va, hq, hf, hi, hg = jnp.split(h, cuts, axis=-1)
    o_a = diff_attention(qa.reshape(B, S, DA_HEADS, 2, DA_HEAD_DIM),
                         ka.reshape(B, S, DA_HEADS, 2, DA_HEAD_DIM),
                         va.reshape(B, S, DA_HEADS, DA_V_DIM),
                         lam_params, sub_g, lam_init, cos, sin)
    o_b = hgrn2(hq.reshape(B, S, HG_HEADS, HG_KDIM), hf.reshape(B, S, HG_HEADS, HG_KDIM),
                hi.reshape(B, S, HG_HEADS, HG_VDIM), hg.reshape(B, S, HG_HEADS, HG_VDIM),
                lb.reshape(HG_HEADS, HG_KDIM), hg_g)
    return jnp.concatenate([o_a.astype(x.dtype), o_b.astype(x.dtype)], axis=-1) @ w_out

def dilated_branch(q, k, v, dil, span):
    B, H, S, hd = q.shape
    L = S // dil

    def to_res(t):
        return t.reshape(B, H, L, dil, hd).transpose(0, 1, 3, 2, 4)

    blk = span
    nb = -(-L // blk)
    pad = nb * blk - L

    def padl(t, front):
        return jnp.pad(t, ((0, 0), (0, 0), (0, 0), (front, pad), (0, 0)))

    qp = padl(to_res(q), 0).reshape(B, H, dil, nb, blk, hd)
    kp = padl(to_res(k), blk).reshape(B, H, dil, nb + 1, blk, hd)
    vp = padl(to_res(v), blk).reshape(B, H, dil, nb + 1, blk, hd)
    kw = jnp.concatenate([kp[:, :, :, :-1], kp[:, :, :, 1:]], axis=-2)
    vw = jnp.concatenate([vp[:, :, :, :-1], vp[:, :, :, 1:]], axis=-2)
    s = jnp.einsum('bhrnqd,bhrnkd->bhrnqk', qp, kw).astype(jnp.float32)
    a_idx = jnp.arange(blk)[:, None]
    c_idx = jnp.arange(2 * blk)[None, :]
    dist = blk + a_idx - c_idx
    key_idx = (jnp.arange(nb)[:, None, None] - 1) * blk + c_idx[None]
    valid = (dist >= 0)[None] & (dist <= span)[None] & (key_idx >= 0)
    s = jnp.where(valid, s, -jnp.inf)
    m = jnp.max(s, axis=-1, keepdims=True)
    e = jnp.exp(s - m)
    den = jnp.sum(e, axis=-1)
    o = jnp.einsum('bhrnqk,bhrnkd->bhrnqd', e.astype(v.dtype), vw) / den[..., None].astype(v.dtype)
    lse = m[..., 0] + jnp.log(den)
    o = o.reshape(B, H, dil, nb * blk, hd)[:, :, :, :L].transpose(0, 1, 3, 2, 4).reshape(B, H, S, hd)
    lse = lse.reshape(B, H, dil, nb * blk)[..., :L].transpose(0, 1, 3, 2).reshape(B, H, S)
    return o, lse

def odd_mixer(x, w_in, w_out, cos, sin):
    B, S, D = x.shape
    q, k, v = jnp.split(x @ w_in, 3, axis=-1)

    def heads(t):
        return t.reshape(B, S, DL_HEADS, DL_HEAD_DIM).transpose(0, 2, 1, 3)

    q = partial_rope(heads(q), cos, sin) * (DL_HEAD_DIM ** -0.5)
    k = partial_rope(heads(k), cos, sin)
    v = heads(v)
    outs, lses = [], []
    for (w, d) in DL_PAIRS:
        o, lse = dilated_branch(q, k, v, d, w // d)
        outs.append(o)
        lses.append(lse)
    wts = jax.nn.softmax(jnp.stack(lses, axis=0), axis=0)
    o = jnp.einsum('gbhs,gbhsd->bhsd', wts.astype(v.dtype), jnp.stack(outs, axis=0))
    return o.transpose(0, 2, 1, 3).reshape(B, S, D) @ w_out

def second_inputs(seed: int = 0) -> dict:
    key = jax.random.key(seed)
    ks = jax.random.split(key, 20)
    f32 = jnp.float32

    def nrm(k, shape, s):
        return jax.random.normal(k, shape, f32) * s

    def gain(k, shape):
        return 1.0 + 0.02 * jax.random.normal(k, shape, f32)

    even_in = 2 * DA_QK_WIDTH + DA_WIDTH + 2 * HG_KWIDTH + 2 * HG_WIDTH
    return {
        "x": nrm(ks[0], (BATCH, SEQ, D_MODEL), 1.0),
        "p": nrm(ks[1], (DEPTH, BATCH, SEQ, PLE_DIM), 1.0),
        "ev_w_in": nrm(ks[2], (N_EVEN, D_MODEL, even_in), D_MODEL ** -0.5),
        "ev_w_out": nrm(ks[3], (N_EVEN, DA_WIDTH + HG_WIDTH, D_MODEL), BETA * (DA_WIDTH + HG_WIDTH) ** -0.5),
        "da_lambda": nrm(ks[4], (N_EVEN, 4, DA_HEAD_DIM), 0.1),
        "da_subln_g": gain(ks[5], (N_EVEN, DA_V_DIM)),
        "hg_lb_logits": nrm(ks[6], (N_EVEN + 1, HG_KWIDTH), 0.1),
        "hg_norm_g": gain(ks[7], (N_EVEN, HG_VDIM)),
        "od_w_in": nrm(ks[8], (N_ODD, D_MODEL, 3 * D_MODEL), D_MODEL ** -0.5),
        "od_w_out": nrm(ks[9], (N_ODD, D_MODEL, D_MODEL), BETA * D_MODEL ** -0.5),
        "ln1_g": gain(ks[10], (DEPTH, D_MODEL)),
        "ln1_b": nrm(ks[11], (DEPTH, D_MODEL), 0.02),
        "ffn_w1": nrm(ks[12], (DEPTH, D_MODEL, FFN_DIM), D_MODEL ** -0.5),
        "ffn_w2": nrm(ks[13], (DEPTH, FFN_DIM, D_MODEL), BETA * FFN_DIM ** -0.5),
        "ln2_g": gain(ks[14], (DEPTH, D_MODEL)),
        "ln2_b": nrm(ks[15], (DEPTH, D_MODEL), 0.02),
        "ple_w_proj": nrm(ks[16], (DEPTH, PLE_DIM, D_MODEL), PLE_DIM ** -0.5),
        "ple_w_gate": nrm(ks[17], (DEPTH, D_MODEL, D_MODEL), D_MODEL ** -0.5),
        "ple_norm_g": gain(ks[18], (DEPTH, D_MODEL)),
    }

def second_block(x, p, ev_w_in, ev_w_out, da_lambda, da_subln_g, hg_lb_logits, hg_norm_g,
              od_w_in, od_w_out, ln1_g, ln1_b, ffn_w1, ffn_w2, ln2_g, ln2_b,
              ple_w_proj, ple_w_gate, ple_norm_g):
    S = x.shape[1]
    cos, sin = rope_tables(S)
    lb_all = jnp.cumsum(jax.nn.softmax(hg_lb_logits.astype(jnp.float32), axis=0), axis=0)
    for l in range(DEPTH):
        j = l // 2
        if l % 2 == 0:
            lam_init = 0.8 - 0.6 * math.exp(-0.3 * l)
            mix = even_mixer(x, ev_w_in[j], ev_w_out[j], da_lambda[j], da_subln_g[j],
                             lb_all[j], hg_norm_g[j], lam_init, cos, sin)
        else:
            mix = odd_mixer(x, od_w_in[j], od_w_out[j], cos, sin)
        x = layer_norm(ALPHA * x + mix, ln1_g[l], ln1_b[l])
        hdn = jnp.square(jax.nn.relu(x @ ffn_w1[l]))
        x = layer_norm(ALPHA * x + hdn @ ffn_w2[l], ln2_g[l], ln2_b[l])
        e = rms_norm(p[l] @ ple_w_proj[l], ple_norm_g[l])
        x = x + jax.nn.sigmoid(x @ ple_w_gate[l]) * e
    return x


def setup_inputs(seed=0):
    out = dict(first_inputs(seed))
    for name, value in second_inputs(seed + 1).items():
        if name != "x":
            out[name + "_2"] = value
    return out


def reference(
    x, c, ctx, c_ctx, ada_w, ada_b, norm1_g, norm2_g, mlp_w1, mlp_w2, att_w_qkv, att_q_gain,
    att_k_gain, att_sink, att_w_o, rwkv_mu, rwkv_w_rkv, rwkv_w0, rwkv_w1, rwkv_w2, rwkv_a0,
    rwkv_a1, rwkv_a2, rwkv_g1, rwkv_g2, rwkv_k_k, rwkv_k_a, rwkv_r_k, rwkv_gn_g, rwkv_gn_b,
    rwkv_w_o, p_2, ev_w_in_2, ev_w_out_2, da_lambda_2, da_subln_g_2, hg_lb_logits_2,
    hg_norm_g_2, od_w_in_2, od_w_out_2, ln1_g_2, ln1_b_2, ffn_w1_2, ffn_w2_2, ln2_g_2, ln2_b_2,
    ple_w_proj_2, ple_w_gate_2, ple_norm_g_2,
):
    x = first_block(
        x, c, ctx, c_ctx, ada_w, ada_b, norm1_g, norm2_g, mlp_w1, mlp_w2, att_w_qkv, att_q_gain,
        att_k_gain, att_sink, att_w_o, rwkv_mu, rwkv_w_rkv, rwkv_w0, rwkv_w1, rwkv_w2, rwkv_a0,
        rwkv_a1, rwkv_a2, rwkv_g1, rwkv_g2, rwkv_k_k, rwkv_k_a, rwkv_r_k, rwkv_gn_g, rwkv_gn_b,
        rwkv_w_o,
    )
    return second_block(
        x, p_2, ev_w_in_2, ev_w_out_2, da_lambda_2, da_subln_g_2, hg_lb_logits_2, hg_norm_g_2,
        od_w_in_2, od_w_out_2, ln1_g_2, ln1_b_2, ffn_w1_2, ffn_w2_2, ln2_g_2, ln2_b_2,
        ple_w_proj_2, ple_w_gate_2, ple_norm_g_2,
    )


_drawn_inputs = setup_inputs


def setup_inputs(seed=0):
    import zlib

    import numpy as np

    out = dict(_drawn_inputs(seed))
    spreads = {}
    factors = {'ada_b': 2.792,
     'att_q_gain': 8.0,
     'att_k_gain': 8.0,
     'att_sink': 8.0,
     'rwkv_w1': 5.484,
     'rwkv_w2': 5.829,
     'rwkv_gn_g': 3.213,
     'rwkv_gn_b': 46.947,
     'da_lambda_2': 5.601,
     'da_subln_g_2': 64.0,
     'hg_lb_logits_2': 26.859,
     'hg_norm_g_2': 64.0,
     'ple_norm_g_2': 4.297,
     'ln1_g_2': 4.101,
     'ln1_b_2': 4.279,
     'ln2_g_2': 4.182,
     'ln2_b_2': 4.528}
    for name, (base, spread) in spreads.items():
        noise = np.random.default_rng([zlib.crc32(name.encode()), seed]).standard_normal(out[name].shape)
        drawn = base * np.exp(spread * noise) if base else spread * noise
        out[name] = jnp.asarray(drawn.astype(out[name].dtype))
    for name, factor in factors.items():
        out[name] = (out[name] * factor).astype(out[name].dtype)
    return out
```

```python
from contextlib import ExitStack

import numpy as np

import concourse.bass as bass
from concourse import mybir

P = 128
F32 = mybir.dt.float32
ALU = mybir.AluOpType
ACT = mybir.ActivationFunctionType
AX = mybir.AxisListType
T = 512
TC = 256
TT = T + TC
CH = 64
RING = 5
NEG = -1e30
ALPHA = 4 ** 0.25

PAIRS = [(0, 4), (1, 5), (2, 6), (3, 7), (8, 12), (9, 13), (10, 14), (11, 15)]

VCOLS = {}


def _vec_layout():
    at = 0
    for name, n in [("adab0", 48), ("adab1", 48), ("n10", 8), ("n11", 8), ("n20", 8), ("n21", 8),
                    ("qg", 1), ("kg", 1), ("sink", 16), ("mu", 48), ("w0", 16), ("a0", 8), ("kk", 8),
                    ("ka", 8), ("rk", 8), ("gng", 8), ("gnb", 8), ("c", 16),
                    ("ln1g0", 8), ("ln1b0", 8), ("ln2g0", 8), ("ln2b0", 8), ("plg0", 8),
                    ("ln1g1", 8), ("ln1b1", 8), ("ln2g1", 8), ("ln2b1", 8), ("plg1", 8),
                    ("subg", 1), ("hgg", 1), ("lb", 8), ("lam", 4), ("e6", 1), ("e5", 1), ("egn", 1),
                    ("one", 1), ("mhalf", 1)]:
        VCOLS[name] = (at, n)
        at += n
    return at


NVEC = _vec_layout()


class Engine:

    def __init__(self, name, sem):
        self.name, self.sem, self.count, self.items, self.seen = name, sem, 0, [], {}

    def wait(self, toks):
        need = {}
        flat = [toks]
        while flat:
            t = flat.pop()
            if t is None:
                continue
            if isinstance(t, list) or not _is_tok(t):
                flat += list(t)
                continue
            sem, v, key = t
            if v > self.seen.get(key, 0) and v > need.get(key, (None, 0))[1]:
                need[key] = (sem, v)
        for key, (sem, v) in need.items():
            self.seen[key] = v
            self.items.append((None, sem, v))

    def do(self, w, f, s=True):
        self.wait([w])
        if s:
            self.count += 1
            self.items.append((f, self.sem, 1))
            return (self.sem, self.count, self.name)
        self.items.append((f, None, 0))
        return None

    def last(self):
        return (self.sem, self.count, self.name) if self.count else None

    def emit(self, eng):
        for f, sem, v in self.items:
            if f is None:
                eng.wait_ge(sem, v)
            else:
                ins = f(eng)
                if sem is not None:
                    ins.then_inc(sem, v)


def _is_tok(t):
    return isinstance(t, tuple) and len(t) == 3 and isinstance(t[2], str)


def program(nc, ins, out_d, scratch, npanels, order):
    ctx = ExitStack()
    uid = [0]

    def alloc(stack, shape, dt=F32):
        uid[0] += 1
        return stack.enter_context(nc.sbuf_tensor(f"t{uid[0]}", shape, dt))

    def new_sem(name):
        return ctx.enter_context(nc.semaphore(name))

    PE = Engine("pe", new_sem("s_pe"))
    DV = Engine("dv", new_sem("s_dv"))
    AC = Engine("ac", new_sem("s_ac"))
    PO = Engine("po", new_sem("s_po"))
    SP = Engine("sp", None)
    dmas = {}

    def dma(q, name, dst, src, w=()):
        if name not in dmas:
            dmas[name] = [new_sem("d_" + name), 0]
        d = dmas[name]
        q.wait(list(w))
        d[1] += 16
        sem = d[0]
        q.items.append((lambda e: e.dma_start(dst, src), sem, 16))
        return (sem, d[1], "d_" + name)


    def mm(out, lhsT, rhs, start=True, stop=True, w=(), s=False):
        return PE.do(w, lambda e: e.matmul(out, lhsT, rhs, start=start, stop=stop), s)

    def tr(out, in_, ident, w=(), s=False):
        return PE.do(w, lambda e: e.transpose(out, in_, ident), s)

    def tt(out, a, b, op, w=(), E=None):
        if E is PO:
            w = [w, PO.last()]
        return (E or DV).do(w, lambda e: e.tensor_tensor(out, a, b, op))

    def ts(out, a, s1, s2, op0, op1=None, w=(), E=None):
        if op1 is None:
            return (E or DV).do(w, lambda e: e.tensor_scalar(out, a, s1, None, op0))
        return (E or DV).do(w, lambda e: e.tensor_scalar(out, a, s1, s2, op0, op1))

    def stt(out, a, sc, b, op0, op1, w=()):
        return DV.do(w, lambda e: e.scalar_tensor_tensor(out=out, in0=a, scalar=sc, in1=b, op0=op0, op1=op1))

    def act(out, a, f, w=(), **k):
        return AC.do(w, lambda e: e.activation(out, a, f, **k))

    def cp(E, out, a, w=()):
        if E is AC:
            return act(out, a, ACT.Copy, w)
        if E is PO:
            w = [w, PO.last()]
        return E.do(w, lambda e: e.tensor_copy(out, a))

    def recip(out, a, w=()):
        return DV.do(w, lambda e: e.reciprocal(out, a))

    def rmax(out, a, w=()):
        return DV.do(w, lambda e: e.tensor_reduce(out, a, AX.X, ALU.max))

    MUL, ADD, SUB, MAX, MIN = ALU.mult, ALU.add, ALU.subtract, ALU.max, ALU.min

    banks = [ctx.enter_context(nc.psum_tensor(f"ps{i}", [P, 512], F32)) for i in range(8)]
    bfree = [None] * 8
    bturn = [0]

    def bank():
        i = bturn[0] % 8
        bturn[0] += 1
        return i, banks[i], bfree[i]

    def fence():
        toks = [e.last() for e in (PE, DV, AC, PO)]
        for e in (PE, DV, AC, PO, SP):
            e.wait(list(toks))
        return toks

    CST = alloc(ctx, [P, 5, P])
    VEC = alloc(ctx, [P, NVEC])
    X = alloc(ctx, [P, 8, T])
    RW = [alloc(ctx, [P, 2048]) for _ in range(RING)]
    ADA = alloc(ctx, [P, 2, 6, 8, 2])
    MOD = alloc(ctx, [P, 2, 2, 8, 2])
    SC = alloc(ctx, [P, 8, 2])
    SM = alloc(ctx, [P, 64])
    ID, ONES, BONES = CST[:, 0, :], CST[:, 1, :], CST[:, 2, :]
    PERM = [CST[:, 3, :], CST[:, 4, :]]

    def vec(name, i=0, n=1, rows=slice(0, P)):
        a = VCOLS[name][0] + i
        return VEC[rows, a:a + n]

    d_cst = [dma(AC, "c0", CST[:, :, :], ins["cst"].rearrange("p (a b) -> p a b", a=5)),
             dma(AC, "c1", VEC[:, :], ins["vec"])]
    d_x = dma(AC, "x", X[:, :, :], ins["xT"].rearrange("p (k t) -> p k t", k=8))
    for e in (PE, DV, AC, PO):
        e.wait(d_cst)

    wp = ins["w"]
    rfree = [None] * RING
    issued = [0]
    wtok = {}

    def issue():
        n = issued[0]
        if n >= npanels:
            return
        s = n % RING
        wtok[n] = dma(SP, f"w{s}", RW[s][:, :], wp[n], [rfree[s]])
        issued[0] += 1

    for _ in range(RING):
        issue()
    used = [0]

    def panel(key):
        n = used[0]
        used[0] += 1
        order.append(key)
        s = n % RING
        return s, RW[s], wtok.get(n)

    def release(s, tok):
        rfree[s] = tok
        issue()

    def gemm(keys, src, segs, evac, w=(), tick=None):
        for pi, key in enumerate(keys):
            s, W, wt = panel(key)
            tok = None
            for m in range(2):
                for sg in segs:
                    bi, B, fr = bank()
                    for k in range(8):
                        tok = mm(B[:, 0:sg[1]], W[:, k * 256 + m * P:k * 256 + m * P + P], src(k, sg),
                                 k == 0, k == 7, [wt, fr, list(w)] if k == 0 else (), k == 7)
                    bfree[bi] = evac(pi * 2 + m, sg, B[:, 0:sg[1]], tok)
            release(s, tok)
            if tick:
                tick()

    def gemm_tok(keys, src, ntok, evac, w=()):
        for pi, key in enumerate(keys):
            s, W, wt = panel(key)
            tok = None
            for tb in range(ntok):
                bi, B, fr = bank()
                for k in range(8):
                    tok = mm(B[:, 0:256], src(k, tb), W[:, k * 256:k * 256 + 256],
                             k == 0, k == 7, [wt, fr, list(w)] if k == 0 else (), k == 7)
                bfree[bi] = evac(pi, tb, B[:, 0:256], tok)
            release(s, tok)

    MAIN, CTX = (0, T, 0), (T, TC, 1)

    e0 = act(SC[:, :, :], vec("c", 0, 16).rearrange("p (k c) -> p k c", c=2), ACT.Exp, scale=-1.0)
    e1 = ts(SC[:, :, :], SC[:, :, :], 1.0, None, ADD, w=[e0])
    e2 = recip(SC[:, :, :], SC[:, :, :], [e1])
    t_sc = tt(SC[:, :, :], SC[:, :, :], vec("c", 0, 16).rearrange("p (k c) -> p k c", c=2), MUL, [e2])

    def ada(layer, parts):
        for part in parts:
            tok = None
            for pj in range(4):
                s, W, wt = panel(("ada", layer, part * 4 + pj))
                bi, B, fr = bank()
                for m in range(2):
                    for k in range(8):
                        t = mm(B[:, 2 * m:2 * m + 2], W[:, k * 256 + m * P:k * 256 + m * P + P], SC[:, k, :],
                               k == 0, k == 7, [wt, fr, t_sc], m == 1 and k == 7)
                release(s, t)
                a = VCOLS[f"adab{layer}"][0] + part * 8 + pj * 2
                bfree[bi] = tok = tt(ADA[:, layer, part, pj * 2:pj * 2 + 2, :],
                                     B[:, 0:4].rearrange("p (a b) -> p a b", b=2),
                                     VEC[:, a:a + 2].unsqueeze(2).broadcast_to([P, 2, 2]), ADD, [t])
                yield
            if part in (1, 4):
                which = 0 if part == 1 else 1
                g = vec(f"n{which + 1}{layer}", 0, 8).unsqueeze(2).broadcast_to([P, 8, 2])
                tok = ts(MOD[:, layer, which, :, :], ADA[:, layer, part, :, :], 1.0, None, ADD, w=[tok])
                tok = tt(MOD[:, layer, which, :, :], MOD[:, layer, which, :, :], g, MUL, [tok])
                for e in (AC, DV):
                    e.wait([tok])

    def run(g):
        for _ in g:
            pass

    def rms_mod(srcf, H, segs, layer, which, st, w=()):
        outs = []
        AC.wait([DV.last()])
        for sg in segs:
            o, n, c = sg
            R = alloc(st, [P, n])
            bi, B, fr = bank()
            for k in range(8):
                t = act(H[:, k, o:o + n], srcf(k, sg), ACT.Square, list(w))
                t = mm(B[:, 0:n], ONES, H[:, k, o:o + n], k == 0, k == 7, [t, fr], True)
            t1 = act(R[:, :], B[:, 0:n], ACT.Sqrt, [t], scale=1.0 / 1024, bias=vec("e6"))
            bfree[bi] = t1
            t2 = recip(R[:, :], R[:, :], [t1])
            for k in range(8):
                t3 = tt(H[:, k, o:o + n], srcf(k, sg), R[:, :], MUL, [t2])
                t4 = act(H[:, k, o:o + n], H[:, k, o:o + n], ACT.Identity, [t3],
                         scale=MOD[:, layer, which, k, c:c + 1], bias=ADA[:, layer, 3 * which, k, c:c + 1])
            outs.append(t4)
        return outs

    def mlp(srcf, segs, layer, st, keys1, keys2, H, gate, tick=None, alpha=None, w=()):
        n_all = sum(s[1] for s in segs)
        HD = [alloc(st, [P, 8, n_all]) for _ in range(2)]
        R = [alloc(st, [P, T]) for _ in range(2)]
        rfr = [None, None]
        hfr = [None, None]
        xt = {}
        cnt = [0]
        for q in range(4):
            D = HD[q % 2]
            hts = []

            def ev1(m, sg, B, tok):
                i = cnt[0] % 2
                cnt[0] += 1
                t = act(R[i][:, 0:sg[1]], B, ACT.Relu, [tok, rfr[i]])
                t2 = act(D[:, m, sg[0]:sg[0] + sg[1]], R[i][:, 0:sg[1]], ACT.Square, [t, hfr[q % 2]])
                rfr[i] = t2
                hts.append(t2)
                return t

            gemm(keys1[4 * q:4 * q + 4], lambda k, sg: H[:, k, sg[0]:sg[0] + sg[1]], segs, ev1, w, tick)

            def ev2(m, sg, B, tok):
                dst = srcf(m, sg)
                key = (m, sg[2])
                pre = xt.get(key)
                if alpha is not None and q == 0:
                    t = stt(dst, dst, alpha, B, MUL, ADD, [tok, pre])
                elif gate is None:
                    t = tt(dst, B, dst, ADD, [tok, pre])
                else:
                    t = stt(dst, B, gate(m, sg), dst, MUL, ADD, [tok, pre])
                xt[key] = t
                return t

            gemm(keys2[4 * q:4 * q + 4], lambda k, sg: D[:, k, sg[0]:sg[0] + sg[1]], segs, ev2, [hts[-1]], tick)
            hfr[q % 2] = PE.last()

    stS = ExitStack()
    SG = alloc(stS, [P, 2, T])
    stC = ExitStack()
    CR = alloc(stC, [P, 8, TC])
    d_c = dma(AC, "x", CR[:, :, :], ins["ctxT"].rearrange("p (k t) -> p k t", k=8))
    for e in (DV, AC):
        e.wait([d_x, d_c])

    def res(k, sg):
        return X[:, k, :] if sg[2] == 0 else CR[:, k, :]

    run(ada(0, [0, 1]))
    st = ExitStack()
    KT = alloc(st, [P, 2, TT])
    VT = alloc(st, [P, 6, 256])
    QT = alloc(st, [P, 8, TT])
    CS = alloc(st, [P, 2, T])
    WM = alloc(st, [P, 3, P])
    d_cs = [dma(AC, "cs", CS[:, :, :], ins["cs0"].rearrange("p (a t) -> p a t", a=2)),
            dma(AC, "cs", WM[:, :, :], ins["wm"].rearrange("p (a t) -> p a t", a=3))]
    DV.wait(d_cs)
    H = alloc(st, [P, 8, TT])
    st2 = ExitStack()
    hh = rms_mod(res, H, [MAIN, CTX], 0, 0, st2)
    SQ = [alloc(st2, [P, T]) for _ in range(2)]
    QR = [alloc(st2, [P, T]) for _ in range(2)]
    RR = [alloc(st2, [P, T]) for _ in range(2)]
    turn = [0]
    busy = [[None], [None]]

    def qk_evac(dst, gain):
        def f(m, sg, B, tok):
            i = turn[0] % 2
            turn[0] += 1
            o, n, c = sg
            q, sq, rr = QR[i][:, 0:n], SQ[i][:, 0:n], RR[i][:, 0:n]
            t0 = act(q, B, ACT.Copy, [tok] + busy[i])
            t1 = act(sq, q, ACT.Square, [t0])
            bi, S, fr = bank()
            t2 = mm(S[:, 0:n], BONES, sq, True, True, [t1, fr], True)
            t3 = act(rr, S[:, 0:n], ACT.Sqrt, [t2], scale=1.0 / 64, bias=vec("e6"))
            bfree[bi] = t3
            t4 = recip(rr, rr, [t3])
            d = dst[:, m, o:o + n]
            if c:
                t5 = stt(d, q, vec(gain), rr, MUL, MUL, [t4])
                busy[i] = [t5]
                return t0
            t5 = stt(q, q, vec(gain), rr, MUL, MUL, [t4])
            bi, S, fr = bank()
            t6 = mm(S[:, 0:n], PERM[0], q, True, True, [t5, fr], True)
            t7 = tt(d, q, CS[:, 0, :], MUL, [t5])
            t8 = tt(sq, S[:, 0:n], CS[:, 1, :], MUL, [t6])
            bfree[bi] = t8
            t9 = tt(d, d, sq, ADD, [t7, t8])
            busy[i] = [t9, t6]
            return t0
        return f

    hsrc = lambda k, sg: H[:, k, sg[0]:sg[0] + sg[1]]
    gemm([("q", j) for j in range(4)], hsrc, [MAIN, CTX], qk_evac(QT, "qg"), hh)
    gemm([("k", 0)], hsrc, [MAIN, CTX], qk_evac(KT, "kg"), hh)
    gemm_tok([("v", 0)], lambda k, tb: H[:, k, tb * P:tb * P + P], 6,
             lambda pi, tb, B, tok: cp(AC, VT[:, tb, :], B, [tok]), hh)
    fence()
    st2.close()
    O = H
    S4 = [alloc(st, [P, 4, 640]) for _ in range(2)]
    PT = [alloc(st, [P, 5, 512]) for _ in range(2)]
    sfree = [None, None]
    pfree = [None, None]
    ada_rest = ada(0, [2, 3, 4, 5])
    un = [0]
    NSM = alloc(st, [P, 2, 4, 8])

    def att_unit(g, q0, blocks, masks):
        u = un[0] % 2
        un[0] += 1
        S, PTu, nb, half, sm = S4[u], PT[u], len(blocks), g % 2, NSM[:, u, :, :]
        rows = slice(64 * half, 64 * half + 64)
        runs = []
        for i, b in enumerate(blocks):
            if runs and runs[-1][1] + runs[-1][2] == b and b != 4:
                runs[-1][2] += 1
            else:
                runs.append([i, b, 1])
        ev = []
        for i in range(4):
            tile = 4 * (g // 2) + i
            for (i0, b0, cnt) in runs:
                bi, B, fr = bank()
                t = mm(B[:, 0:cnt * P], QT[rows, tile, q0:q0 + P], KT[rows, g // 2, b0 * P:(b0 + cnt) * P],
                       True, True, [fr], True)
                if b0 >= 4:
                    r = act(S[:, i, i0 * P:(i0 + cnt) * P], B[:, 0:cnt * P], ACT.Copy, [t, sfree[u]], scale=0.125)
                else:
                    r = stt(S[:, i, i0 * P:(i0 + cnt) * P], B[:, 0:cnt * P], 0.125,
                            WM[:, masks:masks + cnt, :].rearrange("p a b -> p (a b)"), MUL, ADD, [t, sfree[u]])
                bfree[bi] = r
                ev.append(r)
        mx, ng, dn, es = sm[:, :, 0], sm[:, :, 1], sm[:, :, 2], sm[:, :, 3]
        t = rmax(mx, S[:, :, 0:nb * P], ev)
        sk = VCOLS["sink"][0] + 4 * g
        t = tt(ng, mx, VEC[:, sk:sk + 4], MAX, [t])
        t = ts(ng, ng, -1.0, None, MUL, w=[t])
        ee = []
        for i in range(4):
            ee.append(act(S[:, i, 0:nb * P], S[:, i, 0:nb * P], ACT.Exp, [t], bias=ng[:, i:i + 1],
                          accum_out=dn[:, i:i + 1]))
        t = tt(es, ng, VEC[:, sk:sk + 4], ADD, [t])
        t = act(es, es, ACT.Exp, [t])
        t = tt(dn, dn, es, ADD, [t, ee])
        t = recip(dn, dn, [t])
        pn = [ts(S[:, i, 0:nb * P], S[:, i, 0:nb * P], dn[:, i:i + 1], None, MUL, w=[t]) for i in range(4)]

        def back():
            pts = []
            for b in range(nb):
                bi, B, fr = bank()
                for i in range(4):
                    t = tr(B[:, i * P:i * P + P], S[:, i, b * P:b * P + P], ID, [fr, pn], i == 3)
                E = (AC, DV)[b % 2]
                r = cp(E, PTu[:, b, :], B[:, :], [t, pfree[u]])
                bfree[bi] = r
                pts.append(r)
            sfree[u] = PE.last()
            bi, B, fr = bank()
            for b in range(nb):
                t = mm(B[rows, :], VT[:, blocks[b], 64 * g:64 * g + 64], PTu[:, b, :], b == 0, b == nb - 1,
                       [fr, pts[b]], b == nb - 1)
            pfree[u] = t
            bfree[bi] = cp(DV, O[rows, 4 * (g // 2):4 * (g // 2) + 4, q0:q0 + P],
                           B[rows, :].rearrange("p (a b) -> p a b", a=4), [t])
        return back

    pend = None
    for qb in range(6):
        for g in range(4):
            if qb < 4:
                blk = [b for b in (qb - 1, qb, qb + 1) if 0 <= b < 4]
                nxt = att_unit(g, qb * P, blk + [4, 5], 1 if qb == 0 else 0)
            else:
                nxt = att_unit(g, qb * P, [4, 5], 0)
            if pend:
                pend()
            pend = nxt
            next(ada_rest, None)
    pend()
    run(ada_rest)

    def resid(layer, part):
        def f(m, sg, B, tok):
            d = res(m, sg)
            return stt(d, B, ADA[:, layer, part, m, sg[2]:sg[2] + 1], d, MUL, ADD, [tok])
        return f

    gemm([("wo", j) for j in range(4)], lambda k, sg: O[:, k, sg[0]:sg[0] + sg[1]], [MAIN, CTX],
         resid(0, 2), [DV.last()])
    fence()
    st.close()

    st = ExitStack()
    ada1 = ada(1, range(6))
    H = alloc(st, [P, 8, TT])
    hh = rms_mod(res, H, [MAIN, CTX], 0, 1, st)
    mlp(res, [MAIN, CTX], 0, st, [("m1", 0, j) for j in range(16)],
        [("m2", 0, q * 4 + j) for q in range(4) for j in range(4)], H,
        lambda m, sg: ADA[:, 0, 5, m, sg[2]:sg[2] + 1], lambda: next(ada1, None), None, hh)
    run(ada1)
    fence()
    st.close()

    FE = scratch["fe"]
    BON = scratch["bon"]
    YS = scratch["ys"]

    def fe_store(name, idx, tile_ap, m, seg, w):
        o, n, c = seg
        c0, cn = o // CH, n // CH
        dst = FE[c0:c0 + cn, :, idx, m, :].rearrange("c p t -> p c t")
        return dma(SP, "fe" + name, dst, tile_ap.rearrange("p (c t) -> p c t", t=CH), w)

    st = ExitStack()
    H = alloc(st, [P, 8, TT])
    XX = alloc(st, [P, 8, TT])
    XM = alloc(st, [P, 8, TT])
    AT = alloc(st, [P, 8, TT])
    BS = alloc(st, [P, 8, T])
    TM = [alloc(st, [P, T]) for _ in range(4)]
    rs = alloc(st, [P, T])
    outs = []
    AC.wait([DV.last()])
    for sg in (MAIN, CTX):
        o, n, c = sg
        R = rs[:, 0:n]
        bi, B, fr = bank()
        for k in range(8):
            t = act(H[:, k, o:o + n], res(k, sg), ACT.Square)
            t = mm(B[:, 0:n], ONES, H[:, k, o:o + n], k == 0, k == 7, [t, fr], True)
        t1 = act(R, B[:, 0:n], ACT.Sqrt, [t, outs], scale=1.0 / 1024, bias=vec("e6"))
        bfree[bi] = t1
        t2 = recip(R, R, [t1])
        for k in range(8):
            t3 = tt(H[:, k, o:o + n], res(k, sg), R, MUL, [t2])
            t4 = act(H[:, k, o:o + n], H[:, k, o:o + n], ACT.Identity, [t3],
                     scale=MOD[:, 1, 0, k, c:c + 1], bias=ADA[:, 1, 0, k, c:c + 1])
        outs += [t3, t4]
    for sg in (MAIN, CTX):
        o, n, c = sg
        e = o + n
        t = tt(XX[:, :, o + 1:e - 1], H[:, :, o:e - 2], H[:, :, o + 2:e], ADD, [outs])
        a = cp(DV, XX[:, :, o:o + 1], H[:, :, o + 1:o + 2])
        b = cp(DV, XX[:, :, e - 1:e], H[:, :, e - 2:e - 1])
        t = stt(XX[:, :, o:e], XX[:, :, o:e], 0.5, H[:, :, o:e], MUL, SUB, [t, a, b])
    t_xx = t
    xmfree = [None]

    def mix(m, segs):
        toks = []
        for k in range(8):
            a, e = segs[0][0], segs[-1][0] + segs[-1][1]
            toks.append(stt(XM[:, k, a:e], XX[:, k, a:e], vec("mu", m * 8 + k), H[:, k, a:e], MUL, ADD,
                            [t_xx, xmfree[0]]))
        return toks[-1]

    xsrc = lambda k, sg: XM[:, k, sg[0]:sg[0] + sg[1]]
    BOTH = [MAIN, CTX]
    LR = [alloc(st, [P, TT]) for _ in range(2)]
    sA, WA, wtA = panel("loraA")
    tx = mix(1, BOTH)
    for sg in BOTH:
        o, n, c = sg
        bi, B, fr = bank()
        for k in range(8):
            t = mm(B[:, 0:n], WA[:, k * 256:k * 256 + P], xsrc(k, sg), k == 0, k == 7, [wtA, fr, tx], k == 7)
        t = act(LR[0][:, o:o + n], B[:, 0:n], ACT.Tanh, [t])
        bfree[bi] = t
    tw = t
    xmfree[0] = PE.last()
    tx = mix(4, BOTH)
    for sg in BOTH:
        o, n, c = sg
        bi, B, fr = bank()
        for k in range(8):
            t = mm(B[0:64, 0:n], WA[:, k * 256 + P:k * 256 + P + 64], xsrc(k, sg), k == 0, k == 7, [wtA, fr, tx],
                   k == 7)
        ta = cp(AC, LR[1][0:64, o:o + n], B[0:64, 0:n], [t])
        bfree[bi] = ta
    xmfree[0] = PE.last()
    release(sA, PE.last())
    sB, WB, wtB = panel("loraB")
    RES = TM
    tfree = [None] * 4
    SCN = alloc(st, [P, TT])
    DV.wait([dma(AC, "cs", SCN[:, :], ins["scn"])])

    def sigmoid(dst, B, w, bias, nb):
        t = act(dst, B, ACT.Exp, w, scale=-1.0, bias=nb)
        t2 = ts(dst, dst, 1.0, None, ADD, w=[t])
        return t, recip(dst, dst, [t2])

    NB = alloc(st, [P, 24])
    a = VCOLS["w0"][0]
    tnb = ts(NB[:, 0:24], VEC[:, a:a + 24], -1.0, None, MUL)
    for m in range(8):
        for sg in BOTH:
            o, n, c = sg
            bi, B, fr = bank()
            t = mm(B[:, 0:n], WB[0:64, 1024 + m * P:1024 + m * P + P], LR[1][0:64, o:o + n], True, True,
                   [wtB, fr, ta], True)
            t, ts_ = sigmoid(AT[:, m, o:o + n], B[:, 0:n], [t, tnb], None, NB[:, 16 + m:17 + m])
            bfree[bi] = t
    tq = 0
    for d in range(2):
        rows = slice(64 * d, 64 * d + 64)
        for m in range(8):
            for sg in BOTH:
                o, n, c = sg
                i = tq % 2
                tq += 1
                L, C = TM[2 * i][:, 0:n], TM[2 * i + 1][:, 0:n]
                bi, B, fr = bank()
                t = mm(B[:, 0:n], WB[rows, m * P:m * P + P], LR[0][rows, o:o + n], True, True, [wtB, fr, tw], True)
                t, t2 = sigmoid(L, B[:, 0:n], [t, tfree[i]], None, NB[:, 8 * d + m:8 * d + m + 1])
                bfree[bi] = t
                t3 = ts(L, L, -float(np.exp(-0.5)), None, MUL, w=[t2])
                sc, Lc, Cc = SCN[:, 0:n], L, C
                t4 = DV.do([t3, tfree[2 + i]], lambda e, sc=sc, Lc=Lc, Cc=Cc: e.tensor_tensor_scan(
                    Cc, sc, Lc, 0.0, MUL, ADD))
                tfree[i] = [fe_store(f"t{2 * i}", 1 if d == 0 else 8, L, m, sg, [t3]), t4]
                tfree[2 + i] = fe_store(f"t{2 * i + 1}", 0 if d == 0 else 7, C, m, sg, [t4])
    release(sB, PE.last())
    t_fe_f = tfree
    sG, WG, wtG = panel("g1")
    tx = mix(5, [MAIN])
    for d in range(2):
        bi, B, fr = bank()
        for k in range(8):
            t = mm(B[:, :], WG[:, k * 256 + d * P:k * 256 + d * P + P], xsrc(k, MAIN), k == 0, k == 7,
                   [wtG, fr, tx], k == 7)
        t = act(SG[:, d, :], B[:, :], ACT.Exp, [t], scale=-1.0)
        bfree[bi] = t
        t = ts(SG[:, d, :], SG[:, d, :], 1.0, None, ADD, w=[t])
        recip(SG[:, d, :], SG[:, d, :], [t])
    xmfree[0] = PE.last()
    release(sG, PE.last())
    tx = mix(0, [MAIN])

    rts = []

    def ev_r(m, sg, B, tok):
        t = cp(AC, BS[:, m, :], B, [tok])
        rts.append(t)
        rts.append(fe_store("r", 2, BS[:, m, :], m, sg, [t]))
        return t
    gemm([("r", j) for j in range(4)], xsrc, [MAIN], ev_r, [tx])
    xmfree[0] = PE.last()
    tx = mix(2, BOTH)
    fence()
    K1, KK, B1, NR = TM[0], TM[1], TM[2], TM[3]
    lastst = [list(tfree)]

    def ev_k(m, sg, B, tok):
        o, n, c = sg
        k, kk, b, nr = K1[:, 0:n], KK[:, 0:n], B1[:, 0:n], NR[:, 0:n]
        t0 = act(k, B, ACT.Copy, [tok, lastst[0]])
        t1 = ts(kk, k, vec("kk", m), None, MUL, w=[t0, lastst[0]])
        t2 = act(nr, kk, ACT.Square, [t1])
        bi, S, fr = bank()
        t3 = mm(S[:, 0:n], BONES, nr, True, True, [t2, fr], True)
        t4 = act(nr, S[:, 0:n], ACT.Sqrt, [t3])
        bfree[bi] = t4
        t5 = ts(nr, nr, 1e-12, None, MAX, w=[t4])
        t6 = recip(nr, nr, [t5])
        t7 = tt(kk, kk, nr, MUL, [t6])
        t8 = tt(b, kk, AT[:, m, o:o + n], MUL, [t7, lastst[0]])
        t9 = ts(nr, AT[:, m, o:o + n], 1.0, vec("ka", m), SUB, MUL, w=[t7])
        t10 = stt(k, nr, 1.0, k, ADD, MUL, [t9])
        a1 = fe_store("t0", 3, k, m, sg, [t10])
        a2 = fe_store("t1", 5, kk, m, sg, [t7])
        a3 = fe_store("t2", 6, b, m, sg, [t8])
        lastst[0] = [a1, a2, a3, t10]
        if c == 0:
            t11 = tt(BS[:, m, :], BS[:, m, :], k, MUL, [t10, rts])
            t12 = ts(BS[:, m, :], BS[:, m, :], vec("rk", m), None, MUL, w=[t11])
            bi, S, fr = bank()
            t13 = mm(S[:, 0:n], BONES, BS[:, m, :], True, True, [t12, fr], True)
            t14 = cp(AC, BS[:, m, :], S[:, 0:n], [t13])
            bfree[bi] = t14
            lastst[0] = [a1, a2, a3, t12, t14]
        return t0
    gemm([("kr", j) for j in range(4)], xsrc, BOTH, ev_k, [tx])
    xmfree[0] = PE.last()
    tx = mix(3, BOTH)
    vfree = [[lastst[0]], [lastst[0]]]
    vc = [0]

    def ev_v(m, sg, B, tok):
        o, n, c = sg
        i = vc[0] % 2
        vc[0] += 1
        v = TM[i][:, 0:n]
        t0 = act(v, B, ACT.Copy, [tok, vfree[i]])
        a1 = fe_store(f"t{i}", 4, v, m, sg, [t0])
        vfree[i] = [a1]
        if c == 0:
            t1 = tt(BS[:, m, :], BS[:, m, :], v, MUL, [t0])
            vfree[i] = [a1, t1]
            vfree.append(dma(SP, "bon", BON[:, m, :], BS[:, m, :], [t1]))
        return t0
    gemm([("vr", j) for j in range(4)], xsrc, BOTH, ev_v, [tx])
    fe_done = [vfree[0][0], vfree[1][0], vfree[-1], lastst[0]]
    for e in (PE, DV, AC, PO, SP):
        e.wait(fe_done)
    fence()
    st.close()
    stC.close()

    st = ExitStack()
    MG = alloc(st, [P, 2, P])
    ML = alloc(st, [P, 2, 6, CH])
    E64 = alloc(st, [P, CH])
    tmk = [dma(AC, "cs", MG[:, :, :], ins["mg"].rearrange("p (a t) -> p a t", a=2)),
           dma(AC, "cs", ML[:, :, :, :], ins["ml"].rearrange("p (a b t) -> p a b t", a=2, b=6)),
           dma(AC, "cs", E64[:, :], ins["e64"])]
    DV.wait(tmk)
    PO.wait(tmk)
    NA = 7
    LD = [alloc(st, [P, NA, 8, CH]) for _ in range(2)]
    AR = [alloc(st, [P, 8, 2, CH]) for _ in range(2)]
    BK = [alloc(st, [P, 8, 3, CH]) for _ in range(2)]
    GG = [alloc(st, [P, 16, P]) for _ in range(2)]
    ON = [[alloc(st, [P, 8, CH]) for _ in range(2)] for _ in range(2)]
    XA = [alloc(st, [P, 8, CH]) for _ in range(2)]
    XB = [alloc(st, [P, 8, CH]) for _ in range(2)]
    PP = [alloc(st, [P, 8, CH]) for _ in range(2)]
    UV = [alloc(st, [P, 16, CH]) for _ in range(2)]
    BT = [alloc(st, [P, 16, CH]) for _ in range(2)]
    EE = [alloc(st, [P, 8, CH]) for _ in range(2)]
    SS = [alloc(st, [P, 8, CH]) for _ in range(2)]
    YY = [alloc(st, [P, 8, CH]) for _ in range(2)]
    GM = [alloc(st, [P, 3, 8]) for _ in range(2)]
    for d in range(2):
        DV.do((), lambda e, d=d: e.memset(SS[d][:, :, :], 0.0))
        DV.do((), lambda e, d=d: e.memset(AR[d][:, :, :, :], 0.0))
    tms = DV.last()
    for e in (PE, DV, AC, PO, SP):
        e.wait([tms])

    seqs = [[8, 9, 10, 11] + list(range(8)), [11, 10, 9, 8] + list(range(7, -1, -1))]
    ldf = [[None], [None]]
    yfree = [None, None]
    prev = [dict(), dict()]
    ys_tok = []

    def load(d, i):
        c = seqs[d][i]
        L = LD[d]
        if c >= 8:
            if d == 0:
                a = dma(SP, f"l{d}", L[:, 0:2, :, :], FE[c, :, 0:2, :, :], ldf[d])
                return dma(SP, f"l{d}", L[:, 3:7, :, :], FE[c, :, 3:7, :, :])
            return dma(SP, f"l{d}", L[:, 1:7, :, :], FE[c, :, 3:9, :, :], ldf[d])
        a0 = 0 if d == 0 else 2
        return dma(SP, f"l{d}", L[:, :, :, :], FE[c, :, a0:a0 + 7, :, :], ldf[d])

    ldt = [load(0, 0), load(1, 0)]
    

    def unit(d, i):
        c = seqs[d][i]
        main = c < 8
        L = LD[d]
        if d == 0:
            pf, lf, r, k, v, kk, b = [L[:, j, :, :] for j in range(7)]
        else:
            r, k, v, kk, b, pf, lf = [L[:, j, :, :] for j in range(7)]
        lt = ldt[d]
        pv = prev[d]
        ar, bk, G, E = AR[d], BK[d], GG[d], EE[d]
        last = CH - 1
        mid = CH // 2 - 1
        sl0, sl1 = ar[:, :, 0, :], ar[:, :, 1, :]
        if d == 0:
            t = tt(lf, pf, lf, SUB, [lt])
            gi, ge = pf, lf
        else:
            gl = GM[d][:, 2, :]
            t = cp(DV, gl, pf[:, :, last], [lt, pv.get("gm")])
            t = tt(pf, gl.unsqueeze(2).broadcast_to([P, 8, CH]), pf, SUB, [t])
            t = tt(lf, pf, lf, ADD, [t])
            gi, ge = lf, pf
        m_ix = mid if d == 0 else CH - 1 - mid
        l_ix = last if d == 0 else 0
        gm = GM[d]
        newf = gm[:, 0, :]
        tm = cp(DV, newf, gi[:, :, m_ix], [t, pv.get("gm")])
        mb = newf.unsqueeze(2).broadcast_to([P, 8, CH])
        ta = tt(E[:, :, :], gi, mb, SUB, [tm, pv.get("bk")])
        tb = tt(sl0, ge, mb, SUB, [tm, pv.get("g_mm"), pv.get("z_mm")])
        ea = act(sl0, sl0, ACT.Exp, [tb])
        if main:
            eb = act(sl1, E[:, :, :], ACT.Exp, [ta, pv.get("y_mm")])
        ec = act(E[:, :, :], E[:, :, :], ACT.Exp, [ta], scale=-1.0)
        fac = gm[:, 1, :]
        tf = tt(fac, gi[:, :, l_ix], newf, SUB, [tm, pv.get("s_upd")])
        t1 = stt(sl0, sl0, -1.0, kk, MUL, MUL, [ea])
        t2 = tt(sl1, sl1, r, MUL, [eb]) if main else None
        t3 = tt(bk[:, :, 0, :], E[:, :, :], b, MUL, [ec])
        t4 = tt(bk[:, :, 1, :], E[:, :, :], k, MUL, [ec])
        t5 = tt(bk[:, :, 2, :], E[:, :, :], b, MUL, [ec], E=PO)
        yield
        feats = [t1, t2, t3, t4, t5]
        pv["bk"] = [t3, t4, t5]
        vts = []
        for hf in range(2):
            bi, B, fr = bank()
            for j in range(4):
                h = 8 * hf + 2 * j
                pr = h // 2
                t = tr(B[0:64, j * 128:j * 128 + 128], v[:, pr, :], ID, [fr, lt], j == 3)
            vts.append((bi, B, t))
        ev_v = []
        for hf, (bi, B, t) in enumerate(vts):
            src = B[0:64, :].rearrange("p (j a c) -> p j a c", j=4, a=2)
            dsto = UV[d][0:64, 8 * hf:8 * hf + 8, :].rearrange("p (j a) c -> p j a c", a=2)
            dste = UV[d][64:128, 8 * hf:8 * hf + 8, :].rearrange("p (j a) c -> p j a c", a=2)
            x1 = cp(AC, dsto[:, :, 1, :], src[:, :, 1, :], [t, pv.get("uv")])
            x2 = cp(AC, dste[:, :, 0, :], src[:, :, 0, :], [t, pv.get("uv")])
            bfree[bi] = [x1, x2]
            ev_v += [x1, x2]
        n2 = P if main else CH
        gts = []
        for q in range(4):
            bi, B, fr = bank()
            h0 = 8 * (q // 2) + q % 2
            for j in range(4):
                h = h0 + 2 * j
                rows = slice(64 * (h % 2), 64 * (h % 2) + 64)
                lhs = bk[rows, h // 2, (h % 2):(h % 2) + 2, :].rearrange("p a t -> p (a t)")
                t = mm(B[:, j * P:j * P + n2], lhs, ar[rows, h // 2, 0:(2 if main else 1), :].rearrange(
                    "p a t -> p (a t)"), True, True, [fr, feats], j == 3)
            gts.append(tt(G[:, h0:h0 + 7:2, 0:n2], B[:, :].rearrange("p (j n) -> p j n", j=4)[:, :, 0:n2],
                          MG[:, d:d + 1, 0:n2].broadcast_to([P, 4, n2]), MUL, [t, pv.get("gfree")]))
            bfree[bi] = gts[-1]
        pv["g_mm"] = PE.last()
        bts = []
        for q in range(2):
            bi, B, fr = bank()
            for j in range(8):
                h = 2 * j + q
                rows = slice(64 * (h % 2), 64 * (h % 2) + 64)
                lhs = bk[rows, h // 2, (h % 2):(h % 2) + 2, :].rearrange("p a t -> p (a t)")
                t = tr(B[:, j * CH:j * CH + CH], lhs, ID[rows, 64 * (h % 2):64 * (h % 2) + 64], [fr], j == 7)
            x = cp(AC, BT[d][:, q:16:2, :], B[:, :].rearrange("p (a t) -> p a t", t=CH), [t, pv.get("s_mm")])
            bfree[bi] = x
            bts.append(x)
        pv["bk"] = [pv["bk"], PE.last()]
        ldf[d] = [DV.last(), PE.last(), PO.last(), AC.last()]
        if i + 1 < 12:
            ldt[d] = load(d, i + 1)
        yield
        def gview(half):
            rows = slice(64 * half, 64 * half + 64)
            return G[rows, :, 0:CH].rearrange("p (j a) t -> p j a t", a=2)[:, :, half, :]

        def omask(lev, w, out):
            ts_ = []
            for half in range(2):
                rows = slice(64 * half, 64 * half + 64)
                ts_.append(tt(out[rows, :, :], gview(half), ML[rows, d, lev:lev + 1, :].broadcast_to([64, 8, CH]),
                              MUL, w, E=PO))
            return ts_
        o0 = omask(0, [gts, pv.get("inv")], ON[d][0])
        o1 = omask(1, [gts, pv.get("inv")], ON[d][1])
        Xt, Xn, Pm = XA[d], XB[d], PP[d]
        eb8 = E64[:, :].unsqueeze(1).broadcast_to([P, 8, CH])
        tx = tt(Xt[:, :, :], ON[d][0][:, :, :], eb8, ADD, [o0, pv.get("u_mm")])
        bi, B, fr = bank()
        for h in range(16):
            rows = slice(64 * (h % 2), 64 * (h % 2) + 64)
            t = mm(B[rows, (h // 2) * CH:(h // 2) * CH + CH], Xt[rows, h // 2, :], E64[rows, :], True, True,
                   [fr, tx, tmk], h == 15)
        tn = cp(AC, Xn[:, :, :], B[:, :].rearrange("p (a t) -> p a t", t=CH), [t, pv.get("inv")])
        bfree[bi] = tn
        pmt = pv.get("inv")
        for lev in range(1, 6):
            O = ON[d][lev % 2]
            if lev < 5:
                on = omask(lev + 1, [t if lev == 1 else pmt, DV.last()], ON[d][(lev + 1) % 2])
            yield
            ot = o1 if lev == 1 else onp
            bi, B, fr = bank()
            for h in range(16):
                rows = slice(64 * (h % 2), 64 * (h % 2) + 64)
                t = mm(B[rows, (h // 2) * CH:(h // 2) * CH + CH], O[rows, h // 2, :], Xn[rows, h // 2, :],
                       True, True, [fr, ot, tn], h == 15)
            tp = cp(AC, Pm[:, :, :], B[:, :].rearrange("p (a t) -> p a t", t=CH), [t, pmt])
            bfree[bi] = tp
            yield
            bi, B, fr = bank()
            for h in range(16):
                rows = slice(64 * (h % 2), 64 * (h % 2) + 64)
                t = mm(B[rows, (h // 2) * CH:(h // 2) * CH + CH], Pm[rows, h // 2, :], Xt[rows, h // 2, :],
                       True, True, [fr, tp, tx], h == 15)
            if lev < 5:
                bj, B2, fr2 = bank()
                for h in range(16):
                    rows = slice(64 * (h % 2), 64 * (h % 2) + 64)
                    t2_ = mm(B2[rows, (h // 2) * CH:(h // 2) * CH + CH], Xt[rows, h // 2, :], Pm[rows, h // 2, :],
                             True, True, [fr2], h == 15)
                tn = tt(Xn[:, :, :], Xn[:, :, :], B2[:, :].rearrange("p (a t) -> p a t", t=CH), ADD, [t2_])
                bfree[bj] = tn
            tx = tt(Xt[:, :, :], Xt[:, :, :], B[:, :].rearrange("p (a t) -> p a t", t=CH), ADD, [t, PE.last()])
            bfree[bi] = tx
            pmt = PE.last()
            if lev < 5:
                onp = on
        pv["inv"] = PE.last()
        yield
        S = SS[d]
        te = act(pv["fx"][:, 0, :], newf, ACT.Exp, [tm, pv.get("s_upd")])
        tS = tt(S[:, :, :], S[:, :, :], pv["fx"][:, 0, :].unsqueeze(2).broadcast_to([P, 8, CH]), MUL,
                [te, pv.get("s_upd")])
        uv = UV[d]
        zb = []
        for which in range(2):
            bi, B, fr = bank()
            for h in range(16):
                par = h % 2
                rows = slice(64 * par, 64 * par + 64)
                oth = slice(64 * (1 - par), 64 * (1 - par) + 64)
                col = (h // 2) * CH
                if which == 0:
                    t = mm(B[rows, col:col + CH], G[oth, h, 0:CH], uv[oth, h, :], True, True, [fr, ev_v, gts], h == 15)
                else:
                    t = mm(B[rows, col:col + CH], ar[rows, h // 2, 0, :], S[rows, h // 2, :], True, True, [fr, tS],
                           h == 15)
            zb.append((bi, B, t))
        yield
        z = Pm
        fl = lambda B: B[:, :].rearrange("p (a t) -> p a t", t=CH)
        z0 = cp(AC, z[:, :, :], fl(zb[0][1]), [zb[0][2], pmt])
        bfree[zb[0][0]] = z0
        zt = tt(z[:, :, :], z[:, :, :], fl(zb[1][1]), ADD, [z0, zb[1][2]])
        bfree[zb[1][0]] = zt
        bi, B, fr = bank()
        for h in range(16):
            rows = slice(64 * (h % 2), 64 * (h % 2) + 64)
            t = mm(B[rows, (h // 2) * CH:(h // 2) * CH + CH], Xt[rows, h // 2, :], z[rows, h // 2, :], True, True,
                   [fr, zt, tx], h == 15)
        pv["u_mm"] = PE.last()
        pv["inv"] = PE.last()
        yield
        ut = []
        for par in range(2):
            rows = slice(64 * par, 64 * par + 64)
            ut.append(cp((AC, DV)[par], uv[rows, par:16:2, :], fl(B)[rows, :, :], [t, zt]))
        bfree[bi] = ut
        if main:
            bi, B, fr = bank()
            for h in range(16):
                par = h % 2
                rows = slice(64 * par, 64 * par + 64)
                col = (h // 2) * CH
                mm(B[rows, col:col + CH], S[rows, h // 2, :], ar[rows, h // 2, 1, :], True, False, [fr])
                t = mm(B[rows, col:col + CH], uv[:, h, :], G[:, h, CH:P], False, True, [ut], h == 15)
            ty = cp(AC, YY[d][:, :, :], B[:, :].rearrange("p (a t) -> p a t", t=CH), [t, yfree[d]])
            bfree[bi] = ty
            yfree[d] = dma(SP, f"y{d}", YS[d, c].rearrange("p (a t) -> p a t", t=CH), YY[d][:, :, :], [ty])
            pv["y_mm"] = PE.last()
        bi, B, fr = bank()
        for h in range(16):
            par = h % 2
            rows = slice(64 * par, 64 * par + 64)
            t = mm(B[rows, (h // 2) * CH:(h // 2) * CH + CH], BT[d][:, h, :], uv[:, h, :], True, True,
                   [fr, bts, ut], h == 15)
        pv["s_mm"] = t
        pv["uv"] = t
        pv["gfree"] = [PE.last(), PO.last()]
        pv["z_mm"] = t
        tex = act(pv["fx"][:, 1, :], fac, ACT.Exp, [tf, pv.get("s_upd")])
        t = tt(S[:, :, :], S[:, :, :], B[:, :].rearrange("p (a t) -> p a t", t=CH), ADD, [t])
        bfree[bi] = t
        t = tt(S[:, :, :], S[:, :, :], pv["fx"][:, 1, :].unsqueeze(2).broadcast_to([P, 8, CH]), MUL, [t, tex])
        pv["s_upd"] = [t, tex, te]
        pv["gm"] = [t, tex, te, DV.last()]

    for d in range(2):
        prev[d]["fx"] = alloc(st, [P, 2, 8])

    for i in range(12):
        gens = [unit(0, i), unit(1, i)]
        while gens:
            for g in list(gens):
                try:
                    next(g)
                except StopIteration:
                    gens.remove(g)
    for e in (PE, DV, AC, PO, SP):
        e.wait(list(yfree))
    fence()
    st.close()

    st = ExitStack()
    YA = [alloc(st, [P, 8, 8, CH]) for _ in range(2)]
    BO = alloc(st, [P, 8, T])
    OO = alloc(st, [P, 8, T])
    tl = [dma(SP, "rd", YA[d][:, :, :, :], YS[d].rearrange("c p (a t) -> p c a t", t=CH)) for d in range(2)]
    tl.append(dma(SP, "rd", BO[:, :, :], BON))
    TR = [[alloc(st, [P, T]) for _ in range(3)] for _ in range(2)]
    trf = [[None], [None]]
    sG, WG, wtG = panel("g2")
    cnt = 0
    for m in range(8):
        for d in range(2):
            i = cnt % 2
            cnt += 1
            y = YA[d][:, :, m, :]
            a, b, c_ = TR[i]
            v3 = lambda z: z[:, :].rearrange("p (c t) -> p c t", t=CH)
            t0 = cp(PO, v3(a), y, [tl, trf[i]])
            bi, B, fr = bank()
            t = mm(B[:, :], BONES, a[:, :], True, True, [t0, fr], True)
            t1 = stt(a[:, :], B[:, :], -1.0 / 64, a[:, :], MUL, ADD, [t])
            bfree[bi] = t1
            t2 = act(b[:, :], a[:, :], ACT.Square, [t1, trf[i]])
            bi, B, fr = bank()
            t = mm(B[:, :], BONES, b[:, :], True, True, [t2, fr], True)
            t3 = act(b[:, :], B[:, :], ACT.Sqrt, [t], scale=1.0 / 64, bias=vec("egn"))
            bfree[bi] = t3
            t4 = recip(b[:, :], b[:, :], [t3])
            t5 = tt(a[:, :], a[:, :], b[:, :], MUL, [t4])
            t6 = act(a[:, :], a[:, :], ACT.Identity, [t5], scale=vec("gng", m), bias=vec("gnb", m))
            t7 = tt(a[:, :], a[:, :], BO[:, m, :], ADD, [t6])
            bi, B, fr = bank()
            t = mm(B[:, :], WG[:, d * 1024 + m * P:d * 1024 + m * P + P], SG[:, d, :], True, True, [wtG, fr], True)
            if d == 0:
                t8 = tt(OO[:, m, :], a[:, :], B[:, :], MUL, [t, t7])
                bfree[bi] = t8
            else:
                t9 = tt(c_[:, :], a[:, :], B[:, :], MUL, [t, t7])
                bfree[bi] = t9
                t8 = tt(OO[:, m, :], OO[:, m, :], c_[:, :], ADD, [t9])
            trf[i] = [t8]
    release(sG, PE.last())
    gemm([("wor", j) for j in range(4)], lambda k, sg: OO[:, k, :], [MAIN], resid(1, 2), [t8])
    fence()
    st.close()
    stS.close()

    st = ExitStack()
    H = alloc(st, [P, 8, T])
    hh = rms_mod(res, H, [MAIN], 1, 1, st)
    mlp(res, [MAIN], 1, st, [("m1", 1, j) for j in range(16)],
        [("m2", 1, q * 4 + j) for q in range(4) for j in range(4)], H,
        lambda m, sg: ADA[:, 1, 5, m, 0:1], None, None, hh)
    fence()
    st.close()

    def layer_norm(g, b):
        st = ExitStack()
        Q = alloc(st, [P, 8, T])
        R = alloc(st, [P, T])
        M = alloc(st, [P, T])
        PE.wait([DV.last()])
        bi, B, fr = bank()
        for k in range(8):
            t = mm(B[:, :], ONES, X[:, k, :], k == 0, k == 7, [fr], k == 7)
        t = act(M[:, :], B[:, :], ACT.Copy, [t], scale=1.0 / 1024)
        bfree[bi] = t
        bi, B, fr = bank()
        for k in range(8):
            t1 = tt(X[:, k, :], X[:, k, :], M[:, :], SUB, [t])
            t2 = act(Q[:, k, :], X[:, k, :], ACT.Square, [t1])
            t3 = mm(B[:, :], ONES, Q[:, k, :], k == 0, k == 7, [fr, t2], k == 7)
        t4 = act(R[:, :], B[:, :], ACT.Sqrt, [t3], scale=1.0 / 1024, bias=vec("e5"))
        bfree[bi] = t4
        t5 = recip(R[:, :], R[:, :], [t4])
        for k in range(8):
            t6 = tt(X[:, k, :], X[:, k, :], R[:, :], MUL, [t5])
            t7 = act(X[:, k, :], X[:, k, :], ACT.Identity, [t6], scale=vec(g, k), bias=vec(b, k))
        fence()
        st.close()

    xmain = lambda k, sg: X[:, k, :]

    def ffn_ple(l):
        layer_norm(f"ln1g{l}", f"ln1b{l}")
        st = ExitStack()
        XC = alloc(st, [P, 8, T])
        for k in range(8):
            t = cp((PO, AC)[k % 2], XC[:, k, :], X[:, k, :])
        fence()
        mlp(lambda k, sg: X[:, k, :], [MAIN], l, st, [("f1", l, j) for j in range(16)],
            [("f2", l, q * 4 + j) for q in range(4) for j in range(4)], XC, None, None, ALPHA)
        fence()
        st.close()
        layer_norm(f"ln2g{l}", f"ln2b{l}")
        st = ExitStack()
        PTt = alloc(st, [P, 2, T])
        tp = dma(AC, "cs", PTt[:, :, :], ins[f"p{l}"].rearrange("p (k t) -> p k t", k=2))
        EM = alloc(st, [P, 8, T])
        SQ = [alloc(st, [P, T]) for _ in range(2)]
        R = alloc(st, [P, T])
        s, W, wt = panel(("pp", l))
        for m in range(8):
            bi, B, fr = bank()
            for k in range(2):
                t = mm(B[:, :], W[:, k * 1024 + m * P:k * 1024 + m * P + P], PTt[:, k, :], k == 0, k == 1,
                       [wt, fr, tp], k == 1)
            t1 = cp(AC, EM[:, m, :], B[:, :], [t])
            bfree[bi] = t1
        release(s, t)
        bi, B, fr = bank()
        sf = [None, None]
        for m in range(8):
            t2 = act(SQ[m % 2][:, :], EM[:, m, :], ACT.Square, [t1, sf[m % 2]])
            t3 = mm(B[:, :], ONES, SQ[m % 2][:, :], m == 0, m == 7, [fr, t2], True)
            sf[m % 2] = t3
        t4 = act(R[:, :], B[:, :], ACT.Sqrt, [t3], scale=1.0 / 1024, bias=vec("e5"))
        bfree[bi] = t4
        t5 = recip(R[:, :], R[:, :], [t4])
        for m in range(8):
            t6 = stt(EM[:, m, :], EM[:, m, :], vec(f"plg{l}", m), R[:, :], MUL, MUL, [t5])
        Gt = [alloc(st, [P, T]) for _ in range(2)]
        XN = alloc(st, [P, 8, T])
        gf = [None, None]

        def ev(m, sg, B, tok):
            g = Gt[m % 2][:, :]
            t = act(g, B, ACT.Exp, [tok, gf[m % 2]], scale=-1.0)
            t1 = ts(g, g, 1.0, None, ADD, w=[t])
            t1 = recip(g, g, [t1])
            t1 = tt(g, g, EM[:, m, :], MUL, [t1, t6])
            gf[m % 2] = tt(XN[:, m, :], g, X[:, m, :], ADD, [t1])
            return t
        gemm([("pg", l, j) for j in range(4)], xmain, [MAIN], ev)
        fence()
        for k in range(8):
            t = cp((PO, AC)[k % 2], X[:, k, :], XN[:, k, :])
        fence()
        st.close()

    st = ExitStack()
    CS = alloc(st, [P, 2, T])
    tcs = dma(AC, "cs", CS[:, :, :], ins["cs1"].rearrange("p (a t) -> p a t", a=2))
    MK = alloc(st, [P, 4, P])
    CZ = alloc(st, [P, 3, P])
    tcs = [tcs, dma(AC, "cs", MK[:, :, :], ins["ck"].rearrange("p (a t) -> p a t", a=4)),
           dma(AC, "cs", CZ[:, :, :], ins["cz"].rearrange("p (a t) -> p a t", a=3))]
    for e in (DV, PO):
        e.wait(tcs)
    Q4 = alloc(st, [P, 4, T])
    K4 = alloc(st, [P, 4, T])
    VA = alloc(st, [P, 4, 512])
    OM = alloc(st, [P, 8, T])
    TQ = [alloc(st, [P, T]) for _ in range(4)]

    def rope_evac(dst, m0, TQ):
        fr2 = [[None], [None]]
        n = [0]

        def f(m, sg, B, tok):
            i = n[0] % 2
            n[0] += 1
            a, b = TQ[2 * i][:, :], TQ[2 * i + 1][:, :]
            t0 = act(a, B, ACT.Copy, [tok] + fr2[i])
            bi, S, fr = bank()
            t1 = mm(S[:, :], PERM[1], a, True, True, [t0, fr], True)
            t2 = tt(b, S[:, :], CS[:, 1, :], MUL, [t1] + fr2[i])
            bfree[bi] = t2
            t3 = tt(dst[:, m, :], a, CS[:, 0, :], MUL, [t0])
            t4 = tt(dst[:, m, :], dst[:, m, :], b, ADD, [t3, t2])
            fr2[i] = [t4, t1]
            return t0
        return f

    gemm([("qa", j) for j in range(2)], xmain, [MAIN], rope_evac(Q4, 0, TQ))
    fence()
    gemm([("ka", j) for j in range(2)], xmain, [MAIN], rope_evac(K4, 0, TQ))
    gemm_tok([("va", j) for j in range(2)], lambda k, tb: X[:, k, tb * P:tb * P + P], 4,
             lambda pi, tb, B, tok: cp(AC, VA[:, tb, pi * 256:pi * 256 + 256], B, [tok]))
    t = tt(SM[0:64, 0:1], vec("lam", 0, 1, slice(0, 64)), vec("lam", 1, 1, slice(0, 64)), MUL)
    t = [t, tt(SM[0:64, 1:2], vec("lam", 2, 1, slice(0, 64)), vec("lam", 3, 1, slice(0, 64)), MUL)]
    bi, B, fr = bank()
    t = mm(B[:, 0:2], ONES[0:64, :], SM[0:64, 0:2], True, True, [t, fr], True)
    t = act(SM[:, 2:4], B[:, 0:2], ACT.Exp, [t])
    bfree[bi] = t
    t = tt(SM[:, 4:5], SM[:, 3:4], SM[:, 2:3], SUB, [t])
    t_lam = ts(SM[:, 4:5], SM[:, 4:5], -(0.8 - 0.6), None, ADD, w=[t])
    fence()
    S2 = [alloc(st, [P, 2, T]) for _ in range(2)]
    P2 = [alloc(st, [P, 4, P]) for _ in range(2)]
    NS = alloc(st, [P, 2, 2, 4])
    s2f, p2f = [None, None], [None, None]
    un2 = 0

    def diff_unit(h, qb, u):
        nk = (qb + 1) * P
        S, Pt, sm = S2[u], P2[u], NS[:, u, :, :]
        ev = []
        for c in range(2):
            rows = slice(64 * c, 64 * c + 64)
            bi, B, fr = bank()
            t = mm(B[:, 0:nk], Q4[rows, h, qb * P:qb * P + P], K4[rows, h, 0:nk], True, True, [fr], True)
            r = stt(S[:, c, 0:nk], B[:, 0:nk], 0.125, MK[:, 3 - qb:4, :].rearrange("p a b -> p (a b)"), MUL, ADD,
                    [t, s2f[u]])
            bfree[bi] = r
            ev.append(r)
        mx, ng, dn = sm[:, :, 0], sm[:, :, 1], sm[:, :, 2]
        t = rmax(mx, S[:, :, 0:nk], ev)
        t = ts(ng, mx, -1.0, None, MUL, w=[t])
        ee = [act(S[:, c, 0:nk], S[:, c, 0:nk], ACT.Exp, [t], bias=ng[:, c:c + 1], accum_out=dn[:, c:c + 1])
              for c in range(2)]
        t = recip(dn, dn, ee)
        t = tt(dn[:, 1:2], dn[:, 1:2], SM[:, 4:5], MUL, [t])
        a = ts(S[:, 0, 0:nk], S[:, 0, 0:nk], dn[:, 0:1], None, MUL, w=[t])
        pn = stt(S[:, 0, 0:nk], S[:, 1, 0:nk], dn[:, 1:2], S[:, 0, 0:nk], MUL, ADD, [a])

        def back():
            bi, B, fr = bank()
            for b in range(qb + 1):
                t = tr(B[:, b * P:b * P + P], S[:, 0, b * P:b * P + P], ID, [fr, pn], b == qb)
            s2f[u] = t
            r = cp(AC, Pt[:, 0:qb + 1, :], B[:, 0:nk].rearrange("p (a b) -> p a b", b=P), [t, p2f[u]])
            bfree[bi] = r
            bi, B, fr = bank()
            for b in range(qb + 1):
                t = mm(B[:, 0:P], VA[:, b, h * P:h * P + P], Pt[:, b, :], b == 0, b == qb, [fr, r], b == qb)
            p2f[u] = t
            bfree[bi] = cp(DV, OM[:, h, qb * P:qb * P + P], B[:, 0:P], [t])
        return back

    pend = None
    for qb in range(4):
        for h in range(4):
            nxt = diff_unit(h, qb, un2 % 2)
            un2 += 1
            if pend:
                pend()
            pend = nxt
    pend()

    def rms_head(ap, gain, sq, rr, w, scale):
        t = act(sq, ap, ACT.Square, w)
        bi, B, fr = bank()
        t = mm(B[:, :], ONES, sq, True, True, [t, fr], True)
        t = act(rr, B[:, :], ACT.Sqrt, [t], scale=1.0 / 128, bias=vec("e5"))
        bfree[bi] = t
        t = recip(rr, rr, [t])
        t = stt(ap, ap, vec(gain), rr, MUL, MUL, [t])
        if scale != 1.0:
            t = ts(ap, ap, scale, None, MUL, w=[t])
        return t

    fence()
    for h in range(4):
        rms_head(OM[:, h, :], "subg", TQ[0][:, :], TQ[1][:, :], [DV.last(), PE.last()], 1.0 - (0.8 - 0.6))
    fence()
    LF = alloc(st, [P, 4, T])
    SCN = alloc(st, [P, T])
    DV.wait([dma(AC, "cs", SCN[:, :], ins["scn"][:, 0:T])])
    LB = alloc(st, [P, 2, 4])
    lb2 = vec("lb", 0, 8).rearrange("p (a b) -> p a b", a=2)
    L3 = alloc(st, [P, 3, 4])
    t = tt(L3[:, 0, :], lb2[:, 0, :], lb2[:, 1, :], MAX)
    ta_ = tt(L3[:, 1, :], lb2[:, 0, :], L3[:, 0, :], SUB, [t])
    tb_ = tt(L3[:, 2, :], lb2[:, 1, :], L3[:, 0, :], SUB, [t])
    t = act(L3[:, 1:3, :], L3[:, 1:3, :], ACT.Exp, [ta_, tb_])
    t = tt(L3[:, 0, :], L3[:, 1, :], L3[:, 2, :], ADD, [t])
    t = recip(L3[:, 0, :], L3[:, 0, :], [t])
    t = tt(LB[:, 0, :], L3[:, 1, :], L3[:, 0, :], MUL, [t])
    t_lb = ts(LB[:, 1, :], LB[:, 0, :], -1.0, 1.0, MUL, ADD, w=[t])
    fr4 = [[None]] * 4

    def ev_silu(dst, T0):
        fr = [[None], [None]]

        def f(m, sg, B, tok):
            i = m % 2
            a, b = T0[2 * i][:, :], T0[2 * i + 1][:, :]
            t0 = act(a, B, ACT.Copy, [tok] + fr[i])
            t1 = act(b, a, ACT.Exp, [t0], scale=-1.0)
            t2 = ts(b, b, 1.0, None, ADD, w=[t1])
            t3 = recip(b, b, [t2])
            fr[i] = [tt(dst[:, m, :], a, b, MUL, [t3])]
            return t0
        return f

    def ev_f(m, sg, B, tok):
        t0 = act(K4[:, m, :], B, ACT.Exp, [tok], scale=-1.0)
        t1 = ts(K4[:, m, :], K4[:, m, :], 1.0, None, ADD, w=[t0])
        t2 = recip(K4[:, m, :], K4[:, m, :], [t1])
        t3 = ts(LF[:, m, :], K4[:, m, :], LB[:, 1, m:m + 1], LB[:, 0, m:m + 1], MUL, ADD, w=[t2, t_lb])
        t4 = ts(K4[:, m, :], LF[:, m, :], -1.0, 1.0, MUL, ADD, w=[t3])
        t5 = act(LF[:, m, :], LF[:, m, :], ACT.Ln, [t4])
        return t0
    gemm([("hq", j) for j in range(2)], xmain, [MAIN], ev_silu(Q4, TQ))
    gemm([("hf", j) for j in range(2)], xmain, [MAIN], ev_f)
    gemm_tok([("hi", j) for j in range(2)], lambda k, tb: X[:, k, tb * P:tb * P + P], 4,
             lambda pi, tb, B, tok: cp(AC, VA[:, tb, pi * 256:pi * 256 + 256], B, [tok]))
    fence()
    HG = alloc(st, [P, 4, T])
    gemm([("hg", j) for j in range(2)], xmain, [MAIN], ev_silu(HG, TQ))
    CB = alloc(st, [P, 4, T])
    QP = alloc(st, [P, T])
    KP = alloc(st, [P, T])
    QO = alloc(st, [P, T])
    KS = alloc(st, [P, T])
    KST = alloc(st, [P, 4, P])
    AA = [alloc(st, [P, CH]) for _ in range(2)]
    DC = alloc(st, [P, 8])
    SH = alloc(st, [P, P])
    MU = alloc(st, [P, CH], mybir.dt.uint32)
    tmu = ts(MU[:, :], CZ[:, 1, 0:CH], 1.0, None, MUL)
    fence()
    for h in range(4):
        c3 = lambda z: z.rearrange("p (c t) -> p c t", t=CH)
        b_, l_ = CB[:, h, :], LF[:, h, :]
        t0 = DV.do((), lambda e, b_=b_, l_=l_: e.tensor_tensor_scan(b_, SCN[:, :], l_, 0.0, MUL, ADD))
        bc = c3(b_)
        mid = bc[:, :, CH // 2 - 1:CH // 2].broadcast_to([P, 8, CH])
        las = bc[:, :, CH - 1:CH].broadcast_to([P, 8, CH])
        q_, k_ = Q4[:, h, :], K4[:, h, :]
        t1 = tt(c3(QP[:, :]), bc, mid, SUB, [t0])
        t2 = act(KP[:, :], QP[:, :], ACT.Exp, [t1], scale=-1.0)
        t3 = act(QP[:, :], QP[:, :], ACT.Exp, [t1])
        t4 = act(QO[:, :], b_, ACT.Exp, [t0])
        t5 = tt(c3(KS[:, :]), las, bc, SUB, [t0])
        t6 = act(KS[:, :], KS[:, :], ACT.Exp, [t5])
        t7 = act(DC[:, :], bc[:, :, CH - 1], ACT.Exp, [t0])
        u = [tt(QP[:, :], QP[:, :], q_, MUL, [t3, t2]), tt(KP[:, :], KP[:, :], k_, MUL, [t2]),
             tt(QO[:, :], QO[:, :], q_, MUL, [t4]), tt(KS[:, :], KS[:, :], k_, MUL, [t6])]
        bi, B, fr = bank()
        for tb in range(4):
            t = tr(B[:, tb * P:tb * P + P], KS[:, tb * P:tb * P + P], ID, [fr, u], tb == 3)
        tk = cp(AC, KST[:, :, :], B[:, :].rearrange("p (a b) -> p a b", b=P), [t])
        bfree[bi] = tk
        tS = DV.do((), lambda e: e.memset(SH[:, :], 0.0))
        for i in range(2):
            tz = DV.do([PE.last()], lambda e, i=i: e.memset(AA[i][:, :], 0.0))
        aaf = [None, None]
        atok = {}

        def intra(c):
            rows = slice(64 * (c % 2), 64 * (c % 2) + 64)
            A = AA[(c // 2) % 2]
            bi, B, fr = bank()
            cc = slice(c * CH, c * CH + CH)
            r0, c0, hf = rows.start, c * CH, CH // 2
            mm(B[r0:r0 + hf, 0:CH], KP[:, c0:c0 + hf], QP[:, cc], True, True, [fr, u])
            t = mm(B[r0 + hf:r0 + CH, hf:CH], KP[:, c0 + hf:c0 + CH], QP[:, c0 + hf:c0 + CH], True, True, (), True)
            w = [t, aaf[(c // 2) % 2], tmu, tz]
            q4 = []
            for r, co in ((r0, 0), (r0 + hf, hf)):
                am, bm, mm_ = A[r:r + hf, co:CH], B[r:r + hf, co:CH], MU[r:r + hf, co:CH]
                q4.append(DV.do(w, lambda e, am=am, bm=bm, mm_=mm_: e.copy_predicated(am, mm_, bm)))
            atok[c] = q4
            bfree[bi] = atok[c]
        intra(0)
        intra(1)
        for c in range(8):
            rows = slice(64 * (c % 2), 64 * (c % 2) + 64)
            A = AA[(c // 2) % 2]
            cc = slice(c * CH, c * CH + CH)
            bi, B, fr = bank()
            v_ = VA[rows, c // 2, h * P:h * P + P]
            mm(B[:, 0:CH], v_, A[rows, :], True, False, [fr, atok[c]])
            t = mm(B[:, 0:CH], SH[:, :], QO[:, cc], False, True, [tS], True)
            aaf[(c // 2) % 2] = t
            bfree[bi] = cp(AC, OM[:, 4 + h, cc], B[:, 0:CH], [t])
            if c < 7:
                bj, B2, fr2 = bank()
                t2 = mm(B2[:, 0:P], KST[rows, c // 2, :], v_, True, True, [fr2, tk], True)
                tS = stt(SH[:, :], SH[:, :], DC[:, c:c + 1], B2[:, 0:P], MUL, ADD, [t2, tS, t7])
                bfree[bj] = tS
            if c % 2 == 1 and c < 7:
                intra(c + 1)
                intra(c + 2)
        fence()
        t = rms_head(OM[:, 4 + h, :], "hgg", QP[:, :], KP[:, :], (), 1.0)
        tt(OM[:, 4 + h, :], OM[:, 4 + h, :], HG[:, h, :], MUL, [t])
        fence()

    def ev_mix(m, sg, B, tok):
        return stt(X[:, m, :], X[:, m, :], ALPHA, B, MUL, ADD, [tok])
    gemm([("evo", j) for j in range(4)], lambda k, sg: OM[:, k, :], [MAIN], ev_mix)
    fence()
    st.close()
    ffn_ple(0)

    st = ExitStack()
    CS = alloc(st, [P, 2, T])
    tcs = [dma(AC, "cs", CS[:, :, :], ins["cs1"].rearrange("p (a t) -> p a t", a=2))]
    MK = alloc(st, [P, 4, P])
    tcs.append(dma(AC, "cs", MK[:, :, :], ins["mk"].rearrange("p (a t) -> p a t", a=4)))
    DV.wait(tcs)
    Q8 = alloc(st, [P, 8, T])
    K8 = alloc(st, [P, 8, T])
    V8 = alloc(st, [P, 4, 1024])
    OM = alloc(st, [P, 8, T])
    st2 = ExitStack()
    TQ = [alloc(st2, [P, T]) for _ in range(4)]
    gemm([("oq", j) for j in range(4)], xmain, [MAIN], rope_evac(Q8, 0, TQ))
    fence()
    gemm([("ok", j) for j in range(4)], xmain, [MAIN], rope_evac(K8, 0, TQ))
    gemm_tok([("ov", j) for j in range(4)], lambda k, tb: X[:, k, tb * P:tb * P + P], 4,
             lambda pi, tb, B, tok: cp(AC, V8[:, tb, pi * 256:pi * 256 + 256], B, [tok]))
    fence()
    st2.close()
    S4 = [alloc(st, [P, 4, T]) for _ in range(2)]
    P4 = [alloc(st, [P, 4, 512]) for _ in range(2)]
    NS = alloc(st, [P, 2, 4, 4])
    s4f, p4f = [None, None], [None, None]

    def dil_unit(g, qb, u):
        nk = (qb + 1) * P
        S, Pt, sm = S4[u], P4[u], NS[:, u, :, :]
        mk = MK[:, 3 - qb:4, :].rearrange("p a b -> p (a b)")
        ev = []
        for i in range(4):
            h = 4 * g + i
            rows = slice(64 * (h % 2), 64 * (h % 2) + 64)
            bi, B, fr = bank()
            t = mm(B[:, 0:nk], Q8[rows, h // 2, qb * P:qb * P + P], K8[rows, h // 2, 0:nk], True, True, [fr], True)
            r = stt(S[:, i, 0:nk], B[:, 0:nk], 0.125, mk, MUL, ADD, [t, s4f[u]])
            bfree[bi] = r
            ev.append(r)
        mx, ng, dn = sm[:, :, 0], sm[:, :, 1], sm[:, :, 2]
        t = rmax(mx, S[:, :, 0:nk], ev)
        t = ts(ng, mx, -1.0, None, MUL, w=[t])
        ee = [act(S[:, c, 0:nk], S[:, c, 0:nk], ACT.Exp, [t], bias=ng[:, c:c + 1], accum_out=dn[:, c:c + 1])
              for c in range(4)]
        t = recip(dn, dn, ee)
        pn = [ts(S[:, i, 0:nk], S[:, i, 0:nk], dn[:, i:i + 1], None, MUL, w=[t]) for i in range(4)]

        def back():
            pts = []
            for b in range(qb + 1):
                bi, B, fr = bank()
                for i in range(4):
                    t = tr(B[:, i * P:i * P + P], S[:, i, b * P:b * P + P], ID, [fr, pn], i == 3)
                r = cp(AC, Pt[:, b, :], B[:, :], [t, p4f[u]])
                bfree[bi] = r
                pts.append(r)
            s4f[u] = PE.last()
            bi, B, fr = bank()
            for i in range(4):
                h = 4 * g + i
                rows = slice(64 * (h % 2), 64 * (h % 2) + 64)
                col = (i // 2) * P
                for b in range(qb + 1):
                    t = mm(B[rows, col:col + P], V8[:, b, h * 64:h * 64 + 64], Pt[:, b, i * P:i * P + P], b == 0,
                           b == qb, [fr, pts], i == 3 and b == qb)
            p4f[u] = t
            bfree[bi] = cp(AC, OM[:, 2 * g:2 * g + 2, qb * P:qb * P + P],
                           B[:, 0:256].rearrange("p (a b) -> p a b", b=P), [t])
        return back

    pend = None
    n = 0
    for qb in range(4):
        for g in range(4):
            nxt = dil_unit(g, qb, n % 2)
            n += 1
            if pend:
                pend()
            pend = nxt
    pend()
    gemm([("odo", j) for j in range(4)], lambda k, sg: OM[:, k, :], [MAIN], ev_mix, [AC.last()])
    fence()
    st.close()
    ffn_ple(1)

    t = dma(SP, "out", out_d, X[:, :, :].rearrange("p k t -> p (k t)"))
    SP.wait([t])

    block = ctx.enter_context(nc.Block())

    @block.tensor
    def _(e):
        PE.emit(e)

    @block.vector
    def _(e):
        DV.emit(e)

    @block.scalar
    def _(e):
        AC.emit(e)

    @block.gpsimd
    def _(e):
        PO.emit(e)

    @block.sync
    def _(e):
        SP.emit(e)

    ctx.close()


def constants():
    f = np.float32
    c = {}
    i = np.arange(P)
    cst = np.zeros((P, 5, P), f)
    cst[:, 0] = np.eye(P)
    cst[:, 1] = 1
    cst[:, 2] = (i[:, None] // 64 == i[None, :] // 64)
    for m in range(P):
        r = m % 32
        if r < 16:
            cst[m + 16, 3, m] = -1
        else:
            cst[m - 16, 3, m] = 1
        r = m % 64
        if r < 8:
            cst[m + 8, 4, m] = -1
        elif r < 16:
            cst[m - 8, 4, m] = 1
    c["cst"] = cst.reshape(P, -1)
    t = np.arange(T)
    fr = f(10000.0) ** (-np.arange(16, dtype=f) / f(16))
    pos = np.where((i % 64 < 32)[:, None], (t // 64)[None, :], (t % 64)[None, :]).astype(f)
    ang = (pos * fr[i % 16][:, None]).astype(f)
    c["cs0"] = np.concatenate([np.cos(ang), np.sin(ang)], 1).astype(f)
    inv = f(500000.0) ** (-np.arange(0, 16, 2, dtype=f) / f(16))
    ang = (t[None, :].astype(f) * inv[i % 8][:, None]).astype(f)
    rot = (i % 64 < 16)[:, None]
    c["cs1"] = np.concatenate([np.where(rot, np.cos(ang), 1), np.where(rot, np.sin(ang), 0)], 1).astype(f)
    q, k = i[:, None], i[None, :]
    z = np.zeros((P, P))
    c["wm"] = np.concatenate([np.where(k >= q, 0, NEG), z, np.where(k <= q, 0, NEG)], 1).astype(f)

    def mult(off):
        d = q - k + off
        ok = d >= 0
        n = (ok & (d <= 128)).astype(int) + (ok & (d % 4 == 0)) + (ok & (d % 16 == 0))
        return np.where(n > 0, np.log(np.maximum(n, 1)), NEG)
    c["mk"] = np.concatenate([mult(384), mult(256), mult(128), mult(0)], 1).astype(f)
    c["ck"] = np.concatenate([z, z, z, np.where(k <= q, 0, NEG)], 1).astype(f)
    s64, t64 = (i % 64)[:, None], np.arange(64)[None, :]
    c["cz"] = np.concatenate([np.where(k <= q, 0, NEG), np.tile(s64 <= t64, (1, 2)).astype(f), z], 1).astype(f)
    c["scn"] = np.tile((np.arange(TT) % CH != 0).astype(f), (P, 1))
    c["mg"] = np.concatenate([s64 < t64, s64 <= t64, s64 > t64, s64 >= t64], 1).astype(f)
    ml = []
    for d in range(2):
        for lev in range(6):
            n = 1 << lev
            a, b = (s64, t64) if d == 0 else (t64, s64)
            ml.append((a // (2 * n) == b // (2 * n)) & (a // n % 2 == 0) & (b // n % 2 == 1))
    c["ml"] = np.concatenate(ml, 1).astype(f)
    c["e64"] = (s64 == t64).astype(f)
    return {k_: np.ascontiguousarray(v, dtype=f) for k_, v in c.items()}


def _cols(v):
    return np.ascontiguousarray(np.asarray(v).reshape(-1, P).T)


def _fm(a):
    a = np.asarray(a)
    return np.ascontiguousarray(a.T.reshape(a.shape[1] // P, P, a.shape[0]).transpose(1, 0, 2).reshape(P, -1))


def _panel(W):
    K, N = W.shape
    return W.reshape(K // P, P, N).transpose(1, 0, 2).reshape(P, -1)


def lay_out(inp):
    f = np.float32
    g = {k: np.asarray(v) for k, v in inp.items()}
    vec = np.zeros((P, NVEC), f)

    def put(name, a):
        s, n = VCOLS[name]
        vec[:a.shape[0], s:s + n] = a
    for l in range(2):
        put(f"adab{l}", _cols(g["ada_b"][l]))
        put(f"n1{l}", _cols(g["norm1_g"][l]))
        put(f"n2{l}", _cols(g["norm2_g"][l]))
        put(f"ln1g{l}", _cols(g["ln1_g_2"][l]))
        put(f"ln1b{l}", _cols(g["ln1_b_2"][l]))
        put(f"ln2g{l}", _cols(g["ln2_g_2"][l]))
        put(f"ln2b{l}", _cols(g["ln2_b_2"][l]))
        put(f"plg{l}", _cols(g["ple_norm_g_2"][l]))
    put("qg", np.tile(g["att_q_gain"][0], 2)[:, None])
    put("kg", np.tile(g["att_k_gain"][0], 2)[:, None])
    put("sink", np.tile(g["att_sink"][0][None, :], (P, 1)))
    put("mu", _cols(g["rwkv_mu"][0]))
    put("w0", _cols(g["rwkv_w0"][0]))
    put("a0", _cols(g["rwkv_a0"][0]))
    put("kk", _cols(g["rwkv_k_k"][0]))
    put("ka", _cols(g["rwkv_k_a"][0]))
    put("rk", _cols(g["rwkv_r_k"][0]))
    put("gng", _cols(g["rwkv_gn_g"][0]))
    put("gnb", _cols(g["rwkv_gn_b"][0]))
    put("c", np.stack([_cols(g["c"][0]), _cols(g["c_ctx"])], 2).reshape(P, 16))
    put("subg", g["da_subln_g_2"][0][:, None])
    put("hgg", g["hg_norm_g_2"][0][:, None])
    put("lb", _cols(g["hg_lb_logits_2"]))
    put("lam", g["da_lambda_2"][0].T)
    for name, v in (("e6", 1e-6), ("e5", 1e-5), ("egn", 64e-5), ("one", 1.0), ("mhalf", -0.5)):
        put(name, np.full((P, 1), v, f))
    qcols = np.concatenate([np.arange(64) + 64 * h for pr in PAIRS for h in pr])
    wqkv = g["att_w_qkv"][0]
    evi, odi = g["ev_w_in_2"][0], g["od_w_in_2"][0]

    def cut(W, j):
        return _panel(W[:, 256 * j:256 * j + 256])

    def one(key):
        if key == "loraA":
            return _panel(np.concatenate([g["rwkv_w1"][0, 0], g["rwkv_w1"][0, 1], g["rwkv_a1"][0],
                                          np.zeros((1024, 64), f)], 1))
        if key == "loraB":
            a = np.zeros((P, 2048), f)
            a[0:64, 0:1024] = g["rwkv_w2"][0, 0]
            a[64:128, 0:1024] = g["rwkv_w2"][0, 1]
            a[0:64, 1024:2048] = g["rwkv_a2"][0]
            return a
        if key == "g1":
            return _panel(np.concatenate([g["rwkv_g1"][0, 0], g["rwkv_g1"][0, 1]], 1))
        if key == "g2":
            return np.concatenate([g["rwkv_g2"][0, 0], g["rwkv_g2"][0, 1]], 1)
        k, j = key[0], key[-1]
        if k == "ada":
            return cut(g["ada_w"][key[1]], j)
        if k == "q":
            return cut(wqkv[:, qcols], j)
        if k == "k":
            return cut(wqkv[:, 1024:], 0)
        if k == "v":
            return cut(wqkv[:, 1280:], 0)
        if k == "wo":
            return cut(g["att_w_o"][0][qcols], j)
        if k in ("m1", "f1"):
            return cut(g["mlp_w1" if k == "m1" else "ffn_w1_2"][key[1]], j)
        if k in ("m2", "f2"):
            w = g["mlp_w2" if k == "m2" else "ffn_w2_2"][key[1]]
            return cut(w[1024 * (j // 4):1024 * (j // 4) + 1024], j % 4)
        if k in ("r", "kr", "vr"):
            return cut(g["rwkv_w_rkv"][0, ("r", "kr", "vr").index(k)], j)
        if k == "wor":
            return cut(g["rwkv_w_o"][0], j)
        if k in ("qa", "ka", "va", "hq", "hf", "hi", "hg"):
            return cut(evi[:, 512 * ("qa", "ka", "va", "hq", "hf", "hi", "hg").index(k):], j)
        if k == "evo":
            return cut(g["ev_w_out_2"][0], j)
        if k in ("oq", "ok", "ov"):
            return cut(odi[:, 1024 * ("oq", "ok", "ov").index(k):], j)
        if k == "odo":
            return cut(g["od_w_out_2"][0], j)
        if k == "pp":
            return _panel(g["ple_w_proj_2"][key[1]])
        if k == "pg":
            return cut(g["ple_w_gate_2"][key[1]], j)
        raise ValueError(key)

    arrays = dict(constants())
    arrays["vec"] = vec
    arrays["xT"] = _fm(g["x"][0])
    arrays["ctxT"] = _fm(g["ctx"][0])
    arrays["p0"] = _fm(g["p_2"][0, 0])
    arrays["p1"] = _fm(g["p_2"][1, 0])
    return arrays, one


NPANELS = 250


def kernel(**inputs):
    import concourse.bacc as _bacc
    from concourse.bass_utils import run_bass_kernel_spmd as _run

    arrays, one = lay_out(inputs)
    nc = _bacc.Bacc("TRN2", target_bir_lowering=False, num_devices=1)
    dt = mybir.dt.float32
    ins = {}
    for name, a in arrays.items():
        ins[name] = nc.dram_tensor("in_" + name, a.shape, dt, kind="ExternalInput").ap()
    ins["w"] = nc.dram_tensor("in_w", (NPANELS, P, 2048), dt, kind="ExternalInput").ap()
    scratch = {
        "fe": nc.dram_tensor("s_fe", (12, P, 9, 8, CH), dt, kind="Internal").ap(),
        "bon": nc.dram_tensor("s_bon", (P, 8, T), dt, kind="Internal").ap(),
        "ys": nc.dram_tensor("s_ys", (2, 8, P, 8 * CH), dt, kind="Internal").ap(),
    }
    out = nc.dram_tensor("out_0", (P, 8 * T), dt, kind="ExternalOutput").ap()
    order = []
    program(nc, ins, out, scratch, NPANELS, order)
    assert len(order) == NPANELS, len(order)
    arrays["w"] = np.stack([one(k) for k in order])
    r = _run(nc, [{("in_" + k): v for k, v in arrays.items()}], core_ids=[0])
    got = r.results[0]["out_0"]
    return np.ascontiguousarray(got.reshape(P, 8, T).transpose(2, 1, 0).reshape(1, T, 1024))
```

```python
from contextlib import ExitStack

import numpy as np

import concourse.bass as bass
from concourse import mybir

P = 128
F32 = mybir.dt.float32
F32R = mybir.dt.float32r
ALU = mybir.AluOpType
ACT = mybir.ActivationFunctionType
AX = mybir.AxisListType
T = 512
TC = 256
TT = T + TC
CH = 64
RING = 4
NEG = -1e30
ALPHA = 4 ** 0.25

PAIRS = [(0, 4), (1, 5), (2, 6), (3, 7), (8, 12), (9, 13), (10, 14), (11, 15)]

VCOLS = {}


def _vec_layout():
    at = 0
    for name, n in [("adab0", 48), ("adab1", 48), ("n10", 8), ("n11", 8), ("n20", 8), ("n21", 8),
                    ("qg", 1), ("kg", 1), ("sink", 16), ("mu", 48), ("w0", 16), ("a0", 8), ("kk", 8),
                    ("ka", 8), ("rk", 8), ("gng", 8), ("gnb", 8), ("c", 16),
                    ("ln1g0", 8), ("ln1b0", 8), ("ln2g0", 8), ("ln2b0", 8), ("plg0", 8),
                    ("ln1g1", 8), ("ln1b1", 8), ("ln2g1", 8), ("ln2b1", 8), ("plg1", 8),
                    ("subg", 1), ("hgg", 1), ("lb", 8), ("lam", 4), ("e6", 1), ("e5", 1), ("egn", 1),
                    ("l10", 1)]:
        VCOLS[name] = (at, n)
        at += n
    return at


NVEC = _vec_layout()


class Engine:

    def __init__(self, name, sem):
        self.name, self.sem, self.count, self.items, self.seen = name, sem, 0, [], {}

    def wait(self, toks):
        need = {}
        flat = [toks]
        while flat:
            t = flat.pop()
            if t is None:
                continue
            if isinstance(t, list) or not _is_tok(t):
                flat += list(t)
                continue
            sem, v, key = t
            if v > self.seen.get(key, 0) and v > need.get(key, (None, 0))[1]:
                need[key] = (sem, v)
        for key, (sem, v) in need.items():
            self.seen[key] = v
            self.items.append((None, sem, v))

    def do(self, w, f, s=True):
        self.wait([w])
        if s:
            self.count += 1
            self.items.append((f, self.sem, 1))
            return (self.sem, self.count, self.name)
        self.items.append((f, None, 0))
        return None

    def last(self):
        return (self.sem, self.count, self.name) if self.count else None

    def emit(self, eng):
        for f, sem, v in self.items:
            if f is None:
                eng.wait_ge(sem, v)
            else:
                ins = f(eng)
                if sem is not None:
                    ins.then_inc(sem, v)


def _is_tok(t):
    return isinstance(t, tuple) and len(t) == 3 and isinstance(t[2], str)


def program(nc, ins, out_d, scratch, npanels, order):
    ctx = ExitStack()
    uid = [0]

    def alloc(stack, shape, dt=F32):
        uid[0] += 1
        return stack.enter_context(nc.sbuf_tensor(f"t{uid[0]}", shape, dt))

    def new_sem(name):
        return ctx.enter_context(nc.semaphore(name))

    PE = Engine("pe", new_sem("s_pe"))
    DV = Engine("dv", new_sem("s_dv"))
    AC = Engine("ac", new_sem("s_ac"))
    PO = Engine("po", new_sem("s_po"))
    SP = Engine("sp", None)
    dmas = {}

    def dma(q, name, dst, src, w=()):
        if name not in dmas:
            dmas[name] = [new_sem("d_" + name), 0]
        d = dmas[name]
        q.wait(list(w))
        d[1] += 16
        sem = d[0]
        q.items.append((lambda e: e.dma_start(dst, src), sem, 16))
        return (sem, d[1], "d_" + name)


    def mm(out, lhsT, rhs, start=True, stop=True, w=(), s=False):
        return PE.do(w, lambda e: e.matmul(out, lhsT, rhs, start=start, stop=stop), s)

    def tr(out, in_, ident, w=(), s=False):
        return PE.do(w, lambda e: e.transpose(out, in_, ident), s)

    def tt(out, a, b, op, w=(), E=None):
        if E is PO:
            w = [w, PO.last()]
        return (E or DV).do(w, lambda e: e.tensor_tensor(out, a, b, op))

    def ts(out, a, s1, s2, op0, op1=None, w=(), E=None):
        if op1 is None:
            return (E or DV).do(w, lambda e: e.tensor_scalar(out, a, s1, None, op0))
        return (E or DV).do(w, lambda e: e.tensor_scalar(out, a, s1, s2, op0, op1))

    def stt(out, a, sc, b, op0, op1, w=()):
        return DV.do(w, lambda e: e.scalar_tensor_tensor(out=out, in0=a, scalar=sc, in1=b, op0=op0, op1=op1))

    def act(out, a, f, w=(), **k):
        return AC.do(w, lambda e: e.activation(out, a, f, **k))

    def cp(E, out, a, w=()):
        if E is AC:
            return act(out, a, ACT.Copy, w)
        if E is PO:
            w = [w, PO.last()]
        return E.do(w, lambda e: e.tensor_copy(out, a))

    def recip(out, a, w=()):
        return DV.do(w, lambda e: e.reciprocal(out, a))

    def rmax(out, a, w=()):
        return DV.do(w, lambda e: e.tensor_reduce(out, a, AX.X, ALU.max))

    MUL, ADD, SUB, MAX, MIN = ALU.mult, ALU.add, ALU.subtract, ALU.max, ALU.min

    banks = [ctx.enter_context(nc.psum_tensor(f"ps{i}", [P, 512], F32)) for i in range(8)]
    bfree = [None] * 8
    bturn = [0]

    def bank():
        i = bturn[0] % 8
        bturn[0] += 1
        return i, banks[i], bfree[i]


    def fence():
        toks = [e.last() for e in (PE, DV, AC, PO)]
        for e in (PE, DV, AC, PO, SP):
            e.wait(list(toks))
        return toks

    CST = alloc(ctx, [P, 5, P])
    VEC = alloc(ctx, [P, NVEC])
    X = alloc(ctx, [P, 8, T])
    RW = [alloc(ctx, [P, 2048]) for _ in range(RING)]
    ADA = alloc(ctx, [P, 2, 6, 8, 2])
    MOD = alloc(ctx, [P, 2, 2, 8, 2])
    SC = alloc(ctx, [P, 8, 2])
    SM = alloc(ctx, [P, 64])
    ID, ONES, BONES = CST[:, 0, :], CST[:, 1, :], CST[:, 2, :]
    PERM = [CST[:, 3, :], CST[:, 4, :]]

    def vec(name, i=0, n=1, rows=slice(0, P)):
        a = VCOLS[name][0] + i
        return VEC[rows, a:a + n]

    d_cst = [dma(AC, "c0", CST[:, :, :], ins["cst"].rearrange("p (a b) -> p a b", a=5)),
             dma(AC, "c1", VEC[:, :], ins["vec"])]
    d_x = dma(AC, "x", X[:, :, :], ins["xT"].rearrange("p (k t) -> p k t", k=8))
    for e in (PE, DV, AC, PO):
        e.wait(d_cst)

    wp = ins["w"]
    rfree = {}
    issued = [0]
    wtok = {}

    def issue():
        while issued[0] < npanels and (issued[0] < RING or issued[0] - RING in rfree):
            n = issued[0]
            wtok[n] = dma(SP, f"w{n % RING}", RW[n % RING][:, :], wp[n], [rfree.get(n - RING)])
            issued[0] += 1

    issue()
    used = [0]

    def panel(key):
        n = used[0]
        used[0] += 1
        order.append(key)
        return n, RW[n % RING], wtok.get(n)

    def release(n, tok):
        rfree[n] = tok
        issue()

    WS = {"bufs": None, "free": None, "turn": 0}
    plan = []
    ready = []
    open_panel = {}

    def splits_begin(st, n=3):
        WS["bufs"] = [(alloc(st, [P, 8, P], F32R), alloc(st, [P, 8, P], F32R)) for _ in range(n)]
        WS["free"] = [None] * n
        WS["turn"] = 0

    def will_use(keys, kc=8):
        nm = 16 // kc
        for key in keys:
            for m in range(nm):
                plan.append((key, kc, m, nm))
        ahead()

    def ahead():
        while plan and len(ready) < len(WS["bufs"]) - 1:
            key, kc, m, nm = plan.pop(0)
            if m == 0:
                open_panel["n"], open_panel["W"], open_panel["t"] = panel(key)
            W = open_panel["W"][:, :].rearrange("p (k n) -> p k n", k=kc)[:, :, m * P:m * P + P]
            i = WS["turn"] % len(WS["bufs"])
            WS["turn"] += 1
            hi, lo = WS["bufs"][i]
            a = act(hi[:, 0:kc, :], W, ACT.Copy, [open_panel["t"], WS["free"][i]])
            b = tt(lo[:, 0:kc, :], W, hi[:, 0:kc, :].bitcast(F32), SUB, [a])
            if m == nm - 1:
                release(open_panel["n"], b)
            ready.append((i, hi, lo, b))

    def unit_of(kc):
        ahead()
        return ready.pop(0)

    def unit_done(i, tok):
        WS["free"][i] = tok
        ahead()

    def mm3(out, whi, wlo, xhi, xlo, start, stop, w=(), s=False):
        mm(out, whi, xhi, start, False, w)
        mm(out, wlo, xhi, False, False)
        return mm(out, whi, xlo, False, stop, (), s)

    def gemm3(nunits, kc, src, segs, evac, w=(), tick=None):
        for m in range(nunits):
            i, hi, lo, wt = unit_of(kc)
            tok = None
            for sg in segs:
                bi, B, fr = bank()
                for k in range(kc):
                    xh, xl = src(k, sg)
                    tok = mm3(B[:, 0:sg[1]], hi[:, k, :], lo[:, k, :], xh, xl, k == 0, k == kc - 1,
                              [wt, fr, list(w)] if k == 0 else (), k == kc - 1)
                bfree[bi] = evac(m, sg, B[:, 0:sg[1]], tok)
            unit_done(i, tok)
            if tick and m % 2:
                tick()

    def gemm3_tok(nunits, src, segs, dst, st, w=()):
        VT_ = [alloc(st, [P, T]) for _ in range(2)]
        vf = [None, None]
        n_ = [0]
        later = []

        def turn(v, m, sg, t0, i):
            bi, B, fr = bank()
            cnt = sg[1] // P
            for b in range(cnt):
                t = tr(B[:, b * P:b * P + P], v[:, b * P:b * P + P], ID, [fr, t0], b == cnt - 1)
            vf[i] = t
            bfree[bi] = cp(DV, dst[:, sg[0] // P:sg[0] // P + cnt, m * P:m * P + P],
                           B[:, 0:sg[1]].rearrange("p (a b) -> p a b", b=P), [t])

        def ev(m, sg, B, tok):
            i = n_[0] % 2
            n_[0] += 1
            t = cp(AC, VT_[i][:, 0:sg[1]], B, [tok, vf[i]])
            if later:
                turn(*later.pop())
            later.append((VT_[i], m, sg, t, i))
            return t
        gemm3(nunits, 8, src, segs, ev, w)
        turn(*later.pop())

    def gemm(keys, src, segs, evac, w=(), tick=None):
        for pi, key in enumerate(keys):
            s, W, wt = panel(key)
            tok = None
            for m in range(2):
                for sg in segs:
                    bi, B, fr = bank()
                    for k in range(8):
                        tok = mm(B[:, 0:sg[1]], W[:, k * 256 + m * P:k * 256 + m * P + P], src(k, sg),
                                 k == 0, k == 7, [wt, fr, list(w)] if k == 0 else (), k == 7)
                    bfree[bi] = evac(pi * 2 + m, sg, B[:, 0:sg[1]], tok)
            release(s, tok)
            if tick:
                tick()

    def split(hi, lo, a, w=()):
        t = act(hi, a, ACT.Copy, w)
        return tt(lo, a, hi.bitcast(F32), SUB, [t])

    def rstd(out, B, scale, eps, w):
        t = act(out, B, ACT.Ln, w, scale=scale, bias=vec(eps))
        return t, act(out, out, ACT.Exp, [t], scale=-0.5)

    MAIN, CTX = (0, T, 0), (T, TC, 1)

    e0 = act(SC[:, :, :], vec("c", 0, 16).rearrange("p (k c) -> p k c", c=2), ACT.Exp, scale=-1.0)
    e1 = ts(SC[:, :, :], SC[:, :, :], 1.0, None, ADD, w=[e0])
    e2 = recip(SC[:, :, :], SC[:, :, :], [e1])
    t_sc = tt(SC[:, :, :], SC[:, :, :], vec("c", 0, 16).rearrange("p (k c) -> p k c", c=2), MUL, [e2])

    def ada(layer, parts):
        for part in parts:
            tok = None
            for pj in range(4):
                s, W, wt = panel(("ada", layer, part * 4 + pj))
                bi, B, fr = bank()
                for m in range(2):
                    for k in range(8):
                        t = mm(B[:, 2 * m:2 * m + 2], W[:, k * 256 + m * P:k * 256 + m * P + P], SC[:, k, :],
                               k == 0, k == 7, [wt, fr, t_sc], m == 1 and k == 7)
                release(s, t)
                a = VCOLS[f"adab{layer}"][0] + part * 8 + pj * 2
                bfree[bi] = tok = tt(ADA[:, layer, part, pj * 2:pj * 2 + 2, :],
                                     B[:, 0:4].rearrange("p (a b) -> p a b", b=2),
                                     VEC[:, a:a + 2].unsqueeze(2).broadcast_to([P, 2, 2]), ADD, [t])
                yield
            if part in (1, 4):
                which = 0 if part == 1 else 1
                g = vec(f"n{which + 1}{layer}", 0, 8).unsqueeze(2).broadcast_to([P, 8, 2])
                tok = ts(MOD[:, layer, which, :, :], ADA[:, layer, part, :, :], 1.0, None, ADD, w=[tok])
                tok = tt(MOD[:, layer, which, :, :], MOD[:, layer, which, :, :], g, MUL, [tok])
                for e in (AC, DV):
                    e.wait([tok])

    def run(g):
        for _ in g:
            pass

    def rms_mod(srcf, HH, HL, segs, layer, which, st, w=()):
        outs = []
        AC.wait([DV.last()])
        Q = [alloc(st, [P, T]) for _ in range(4)]
        qf = [None] * 4
        R = alloc(st, [P, T])
        n_ = 0
        for sg in segs:
            o, n, c = sg
            bi, B, fr = bank()
            for k in range(8):
                i = n_ % 4
                n_ += 1
                t = act(Q[i][:, 0:n], srcf(k, sg), ACT.Square, [list(w), qf[i]])
                qf[i] = t = mm(B[:, 0:n], ONES, Q[i][:, 0:n], k == 0, k == 7, [t, fr], True)
            t1, t2 = rstd(R[:, 0:n], B[:, 0:n], 1.0 / 1024, "e6", [t, outs])
            bfree[bi] = t1
            for k in range(8):
                i = n_ % 4
                n_ += 1
                t3 = tt(Q[i][:, 0:n], srcf(k, sg), R[:, 0:n], MUL, [t2, qf[i]])
                t4 = act(Q[i][:, 0:n], Q[i][:, 0:n], ACT.Identity, [t3],
                         scale=MOD[:, layer, which, k, c:c + 1], bias=ADA[:, layer, 3 * which, k, c:c + 1])
                qf[i] = split(HH[:, k, o:o + n], HL[:, k, o:o + n], Q[i][:, 0:n], [t4])
            outs = [t3, qf[i]]
        return outs

    def mlp_keys(a, b, layer):
        k1 = lambda q: ([(a, layer, 2 * q + j) for j in range(2)], 8)
        k2 = lambda q: ([(b, layer, 2 * q + j) for j in range(2)], 4)
        seq = [k1(0)]
        for q in range(8):
            if q < 7:
                seq.append(k1(q + 1))
            seq.append(k2(q))
        return seq

    def mlp(srcf, segs, st, seq, HH, HL, gate, tick=None, alpha=None, w=()):
        n_all = sum(s[1] for s in segs)
        HD = [(alloc(st, [P, 4, n_all], F32R), alloc(st, [P, 4, n_all], F32R)) for _ in range(2)]
        R = [alloc(st, [P, T]) for _ in range(2)]
        rfr = [None, None]
        hfr = [None, None]
        xt = {}
        cnt = [0]
        hts = {}
        for keys, kc in seq:
            for key in keys:
                will_use([key], kc)

        def first(q):
            DH, DL = HD[q % 2]
            hts[q] = []

            def ev1(m, sg, B, tok):
                i = cnt[0] % 2
                cnt[0] += 1
                r = R[i][:, 0:sg[1]]
                t = act(r, B, ACT.Relu, [tok, rfr[i]])
                t2 = tt(r, r, r, MUL, [t])
                rfr[i] = split(DH[:, m, sg[0]:sg[0] + sg[1]], DL[:, m, sg[0]:sg[0] + sg[1]], r, [t2, hfr[q % 2]])
                hts[q].append(rfr[i])
                return t
            gemm3(4, 8, lambda k, sg: (HH[:, k, sg[0]:sg[0] + sg[1]], HL[:, k, sg[0]:sg[0] + sg[1]]), segs, ev1, w,
                  tick)

        def second(q):
            DH, DL = HD[q % 2]

            def ev2(m, sg, B, tok):
                dst = srcf(m, sg)
                key = (m, sg[2])
                pre = xt.get(key)
                if alpha is not None and q == 0:
                    t = stt(dst, dst, alpha, B, MUL, ADD, [tok, pre])
                elif gate is None:
                    t = tt(dst, B, dst, ADD, [tok, pre])
                else:
                    t = stt(dst, B, gate(m, sg), dst, MUL, ADD, [tok, pre])
                xt[key] = t
                return t
            gemm3(8, 4, lambda k, sg: (DH[:, k, sg[0]:sg[0] + sg[1]], DL[:, k, sg[0]:sg[0] + sg[1]]), segs, ev2,
                  [hts[q]], tick)
            hfr[q % 2] = PE.last()

        first(0)
        for q in range(8):
            if q < 7:
                first(q + 1)
            second(q)

    stS = ExitStack()
    SG = alloc(stS, [P, 2, T])
    stC = ExitStack()
    CR = alloc(stC, [P, 8, TC])
    d_c = dma(AC, "x", CR[:, :, :], ins["ctxT"].rearrange("p (k t) -> p k t", k=8))
    for e in (DV, AC):
        e.wait([d_x, d_c])

    def res(k, sg):
        return X[:, k, :] if sg[2] == 0 else CR[:, k, :]

    run(ada(0, [0, 1]))
    st = ExitStack()
    KT = alloc(st, [P, 2, TT])
    VT = alloc(st, [P, 6, 256])
    QT = alloc(st, [P, 8, TT])
    CS = alloc(st, [P, 2, T])
    WM = alloc(st, [P, 3, P])
    d_cs = [dma(AC, "cs", CS[:, :, :], ins["cs0"].rearrange("p (a t) -> p a t", a=2)),
            dma(AC, "cs", WM[:, :, :], ins["wm"].rearrange("p (a t) -> p a t", a=3))]
    DV.wait(d_cs)
    st2 = ExitStack()
    splits_begin(st2)
    will_use([("q", j) for j in range(4)] + [("k", 0), ("v", 0)])
    HH, HL = alloc(st2, [P, 8, TT], F32R), alloc(st2, [P, 8, TT], F32R)
    st3 = ExitStack()
    hh = rms_mod(res, HH, HL, [MAIN, CTX], 0, 0, st3)
    fence()
    st3.close()
    SQ = [alloc(st2, [P, T]) for _ in range(2)]
    QR = [alloc(st2, [P, T]) for _ in range(2)]
    RR = [alloc(st2, [P, T]) for _ in range(2)]
    turn = [0]
    busy = [[None], [None]]

    def qk_evac(dst, gain):
        def f(m, sg, B, tok):
            i = turn[0] % 2
            turn[0] += 1
            o, n, c = sg
            q, sq, rr = QR[i][:, 0:n], SQ[i][:, 0:n], RR[i][:, 0:n]
            t0 = act(q, B, ACT.Copy, [tok] + busy[i])
            t1 = act(sq, q, ACT.Square, [t0])
            bi, S, fr = bank()
            t2 = mm(S[:, 0:n], BONES, sq, True, True, [t1, fr], True)
            t3, t4 = rstd(rr, S[:, 0:n], 1.0 / 64, "e6", [t2])
            bfree[bi] = t3
            d = dst[:, m, o:o + n]
            if c:
                t5 = stt(d, q, vec(gain), rr, MUL, MUL, [t4])
                busy[i] = [t5]
                return t0
            t5 = stt(q, q, vec(gain), rr, MUL, MUL, [t4])
            bi, S, fr = bank()
            t6 = mm(S[:, 0:n], PERM[0], q, True, True, [t5, fr], True)
            t7 = tt(d, q, CS[:, 0, :], MUL, [t5])
            t8 = tt(sq, S[:, 0:n], CS[:, 1, :], MUL, [t6])
            bfree[bi] = t8
            t9 = tt(d, d, sq, ADD, [t7, t8])
            busy[i] = [t9, t6]
            return t0
        return f

    hsrc = lambda k, sg: (HH[:, k, sg[0]:sg[0] + sg[1]], HL[:, k, sg[0]:sg[0] + sg[1]])
    gemm3(8, 8, hsrc, [MAIN, CTX], qk_evac(QT, "qg"), hh)
    gemm3(2, 8, hsrc, [MAIN, CTX], qk_evac(KT, "kg"), hh)
    gemm3_tok(2, hsrc, [MAIN, CTX], VT, st2, hh)
    fence()
    st2.close()
    O = alloc(st, [P, 8, TT])
    stA = ExitStack()
    S4 = [alloc(stA, [P, 4, 640]) for _ in range(3)]
    PT = [alloc(stA, [P, 5, 512]) for _ in range(2)]
    sfree = [None] * 3
    pfree = [None, None]
    ada_rest = ada(0, [2, 3, 4, 5])
    un = [0]
    NSM = alloc(stA, [P, 3, 4, 8])

    def att_unit(g, q0, blocks, masks):
        u, v = un[0] % 3, un[0] % 2
        un[0] += 1
        S, PTu, nb, half, sm = S4[u], PT[v], len(blocks), g % 2, NSM[:, u, :, :]
        rows = slice(64 * half, 64 * half + 64)
        runs = []
        for i, b in enumerate(blocks):
            if runs and runs[-1][1] + runs[-1][2] == b and b != 4:
                runs[-1][2] += 1
            else:
                runs.append([i, b, 1])
        ev = []
        for i in range(4):
            tile = 4 * (g // 2) + i
            for (i0, b0, cnt) in runs:
                bi, B, fr = bank()
                t = mm(B[:, 0:cnt * P], QT[rows, tile, q0:q0 + P], KT[rows, g // 2, b0 * P:(b0 + cnt) * P],
                       True, True, [fr], True)
                if b0 >= 4:
                    r = act(S[:, i, i0 * P:(i0 + cnt) * P], B[:, 0:cnt * P], ACT.Copy, [t, sfree[u]], scale=0.125)
                else:
                    r = stt(S[:, i, i0 * P:(i0 + cnt) * P], B[:, 0:cnt * P], 0.125,
                            WM[:, masks:masks + cnt, :].rearrange("p a b -> p (a b)"), MUL, ADD, [t, sfree[u]])
                bfree[bi] = r
                ev.append(r)
        mx, ng, dn, es = sm[:, :, 0], sm[:, :, 1], sm[:, :, 2], sm[:, :, 3]
        t = rmax(mx, S[:, :, 0:nb * P], ev)
        sk = VCOLS["sink"][0] + 4 * g
        t = tt(ng, mx, VEC[:, sk:sk + 4], MAX, [t])
        t = ts(ng, ng, -1.0, None, MUL, w=[t])
        ee = []
        for i in range(4):
            ee.append(act(S[:, i, 0:nb * P], S[:, i, 0:nb * P], ACT.Exp, [t], bias=ng[:, i:i + 1],
                          accum_out=dn[:, i:i + 1]))
        t = tt(es, ng, VEC[:, sk:sk + 4], ADD, [t])
        t = act(es, es, ACT.Exp, [t])
        t = tt(dn, dn, es, ADD, [t, ee])
        t = recip(dn, dn, [t])
        pn = [ts(S[:, i, 0:nb * P], S[:, i, 0:nb * P], dn[:, i:i + 1], None, MUL, w=[t]) for i in range(4)]

        def back():
            pts = []
            for b in range(nb):
                bi, B, fr = bank()
                for i in range(4):
                    t = tr(B[:, i * P:i * P + P], S[:, i, b * P:b * P + P], ID, [fr, pn], i == 3)
                E = (AC, DV)[b % 2]
                r = cp(E, PTu[:, b, :], B[:, :], [t, pfree[v]])
                bfree[bi] = r
                pts.append(r)
            sfree[u] = PE.last()
            bi, B, fr = bank()
            for b in range(nb):
                t = mm(B[rows, :], VT[:, blocks[b], 64 * g:64 * g + 64], PTu[:, b, :], b == 0, b == nb - 1,
                       [fr, pts[b]], b == nb - 1)
            pfree[v] = t
            bfree[bi] = cp(DV, O[rows, 4 * (g // 2):4 * (g // 2) + 4, q0:q0 + P],
                           B[rows, :].rearrange("p (a b) -> p a b", a=4), [t])
        return back

    pend = []
    for qb in range(6):
        for g in range(4):
            if qb < 4:
                blk = [b for b in (qb - 1, qb, qb + 1) if 0 <= b < 4]
                nxt = att_unit(g, qb * P, blk + [4, 5], 1 if qb == 0 else 0)
            else:
                nxt = att_unit(g, qb * P, [4, 5], 0)
            next(ada_rest, None)
            pend.append(nxt)
            if len(pend) > 2:
                pend.pop(0)()
    for f in pend:
        f()
    run(ada_rest)
    fence()
    stA.close()
    splits_begin(st)
    will_use([("wo", j) for j in range(4)])
    OH, OL = alloc(st, [P, 8, TT], F32R), alloc(st, [P, 8, TT], F32R)
    for k in range(8):
        t_o = split(OH[:, k, :], OL[:, k, :], O[:, k, :])

    def resid(layer, part):
        def f(m, sg, B, tok):
            d = res(m, sg)
            return stt(d, B, ADA[:, layer, part, m, sg[2]:sg[2] + 1], d, MUL, ADD, [tok])
        return f

    gemm3(8, 8, lambda k, sg: (OH[:, k, sg[0]:sg[0] + sg[1]], OL[:, k, sg[0]:sg[0] + sg[1]]), [MAIN, CTX],
          resid(0, 2), [t_o])
    fence()
    st.close()

    st = ExitStack()
    ada1 = ada(1, range(6))
    splits_begin(st)
    HH, HL = alloc(st, [P, 8, TT], F32R), alloc(st, [P, 8, TT], F32R)
    st3 = ExitStack()
    hh = rms_mod(res, HH, HL, [MAIN, CTX], 0, 1, st3)
    fence()
    st3.close()
    mlp(res, [MAIN, CTX], st, mlp_keys("m1", "m2", 0), HH, HL,
        lambda m, sg: ADA[:, 0, 5, m, sg[2]:sg[2] + 1], lambda: next(ada1, None), None, hh)
    run(ada1)
    fence()
    st.close()

    FE = scratch["fe"]
    BON = scratch["bon"]
    YS = scratch["ys"]

    def fe_store(name, idx, tile_ap, m, seg, w):
        o, n, c = seg
        c0, cn = o // CH, n // CH
        dst = FE[c0:c0 + cn, :, idx, m, :].rearrange("c p t -> p c t")
        return dma(SP, "fe" + name, dst, tile_ap.rearrange("p (c t) -> p c t", t=CH), w)

    st = ExitStack()
    H = alloc(st, [P, 8, TT])
    XX = alloc(st, [P, 8, TT])
    XM = alloc(st, [P, 8, TT])
    AT = alloc(st, [P, 8, TT])
    BS = alloc(st, [P, 8, T])
    TM = [alloc(st, [P, T]) for _ in range(4)]
    rs = alloc(st, [P, T])
    outs = []
    AC.wait([DV.last()])
    for sg in (MAIN, CTX):
        o, n, c = sg
        R = rs[:, 0:n]
        bi, B, fr = bank()
        for k in range(8):
            t = act(H[:, k, o:o + n], res(k, sg), ACT.Square)
            t = mm(B[:, 0:n], ONES, H[:, k, o:o + n], k == 0, k == 7, [t, fr], True)
        t1, t2 = rstd(R, B[:, 0:n], 1.0 / 1024, "e6", [t, outs])
        bfree[bi] = t1
        for k in range(8):
            t3 = tt(H[:, k, o:o + n], res(k, sg), R, MUL, [t2])
            t4 = act(H[:, k, o:o + n], H[:, k, o:o + n], ACT.Identity, [t3],
                     scale=MOD[:, 1, 0, k, c:c + 1], bias=ADA[:, 1, 0, k, c:c + 1])
        outs += [t3, t4]
    for sg in (MAIN, CTX):
        o, n, c = sg
        e = o + n
        t = tt(XX[:, :, o + 1:e - 1], H[:, :, o:e - 2], H[:, :, o + 2:e], ADD, [outs])
        a = cp(DV, XX[:, :, o:o + 1], H[:, :, o + 1:o + 2])
        b = cp(DV, XX[:, :, e - 1:e], H[:, :, e - 2:e - 1])
        t = stt(XX[:, :, o:e], XX[:, :, o:e], 0.5, H[:, :, o:e], MUL, SUB, [t, a, b])
    t_xx = t
    xmfree = [None]

    def mix(m, segs):
        toks = []
        for k in range(8):
            a, e = segs[0][0], segs[-1][0] + segs[-1][1]
            toks.append(stt(XM[:, k, a:e], XX[:, k, a:e], vec("mu", m * 8 + k), H[:, k, a:e], MUL, ADD,
                            [t_xx, xmfree[0]]))
        return toks[-1]

    xsrc = lambda k, sg: XM[:, k, sg[0]:sg[0] + sg[1]]
    BOTH = [MAIN, CTX]
    LR = [alloc(st, [P, TT]) for _ in range(2)]
    sA, WA, wtA = panel("loraA")
    tx = mix(1, BOTH)
    for sg in BOTH:
        o, n, c = sg
        bi, B, fr = bank()
        for k in range(8):
            t = mm(B[:, 0:n], WA[:, k * 256:k * 256 + P], xsrc(k, sg), k == 0, k == 7, [wtA, fr, tx], k == 7)
        t = act(LR[0][:, o:o + n], B[:, 0:n], ACT.Tanh, [t])
        bfree[bi] = t
    tw = t
    xmfree[0] = PE.last()
    tx = mix(4, BOTH)
    for sg in BOTH:
        o, n, c = sg
        bi, B, fr = bank()
        for k in range(8):
            t = mm(B[0:64, 0:n], WA[:, k * 256 + P:k * 256 + P + 64], xsrc(k, sg), k == 0, k == 7, [wtA, fr, tx],
                   k == 7)
        ta = cp(AC, LR[1][0:64, o:o + n], B[0:64, 0:n], [t])
        bfree[bi] = ta
    xmfree[0] = PE.last()
    release(sA, PE.last())
    sB, WB, wtB = panel("loraB")
    RES = TM
    tfree = [None] * 4
    SCN = alloc(st, [P, TT])
    DV.wait([dma(AC, "cs", SCN[:, :], ins["scn"])])

    def sigmoid(dst, B, w, bias, nb):
        t = act(dst, B, ACT.Sigmoid, w, bias=nb)
        return t, t

    NB = alloc(st, [P, 24])
    a = VCOLS["w0"][0]
    tnb = cp(DV, NB[:, 0:24], VEC[:, a:a + 24])
    for m in range(8):
        for sg in BOTH:
            o, n, c = sg
            bi, B, fr = bank()
            t = mm(B[:, 0:n], WB[0:64, 1024 + m * P:1024 + m * P + P], LR[1][0:64, o:o + n], True, True,
                   [wtB, fr, ta], True)
            t, ts_ = sigmoid(AT[:, m, o:o + n], B[:, 0:n], [t, tnb], None, NB[:, 16 + m:17 + m])
            bfree[bi] = t
    tq = 0
    for d in range(2):
        rows = slice(64 * d, 64 * d + 64)
        for m in range(8):
            for sg in BOTH:
                o, n, c = sg
                i = tq % 2
                tq += 1
                L, C = TM[2 * i][:, 0:n], TM[2 * i + 1][:, 0:n]
                bi, B, fr = bank()
                t = mm(B[:, 0:n], WB[rows, m * P:m * P + P], LR[0][rows, o:o + n], True, True, [wtB, fr, tw], True)
                t, t2 = sigmoid(L, B[:, 0:n], [t, tfree[i]], None, NB[:, 8 * d + m:8 * d + m + 1])
                bfree[bi] = t
                t3 = ts(L, L, -float(np.exp(-0.5)), None, MUL, w=[t2])
                sc, Lc, Cc = SCN[:, 0:n], L, C
                t4 = DV.do([t3, tfree[2 + i]], lambda e, sc=sc, Lc=Lc, Cc=Cc: e.tensor_tensor_scan(
                    Cc, sc, Lc, 0.0, MUL, ADD))
                tfree[i] = [fe_store(f"t{2 * i}", 1 if d == 0 else 8, L, m, sg, [t3]), t4]
                tfree[2 + i] = fe_store(f"t{2 * i + 1}", 0 if d == 0 else 7, C, m, sg, [t4])
    release(sB, PE.last())
    t_fe_f = tfree
    sG, WG, wtG = panel("g1")
    tx = mix(5, [MAIN])
    for d in range(2):
        bi, B, fr = bank()
        for k in range(8):
            t = mm(B[:, :], WG[:, k * 256 + d * P:k * 256 + d * P + P], xsrc(k, MAIN), k == 0, k == 7,
                   [wtG, fr, tx], k == 7)
        bfree[bi] = act(SG[:, d, :], B[:, :], ACT.Sigmoid, [t])
    xmfree[0] = PE.last()
    release(sG, PE.last())
    tx = mix(0, [MAIN])

    rts = []

    def ev_r(m, sg, B, tok):
        t = cp(AC, BS[:, m, :], B, [tok])
        rts.append(t)
        rts.append(fe_store("r", 2, BS[:, m, :], m, sg, [t]))
        return t
    gemm([("r", j) for j in range(4)], xsrc, [MAIN], ev_r, [tx])
    xmfree[0] = PE.last()
    tx = mix(2, BOTH)
    fence()
    K1, KK, B1, NR = TM[0], TM[1], TM[2], TM[3]
    lastst = [list(tfree)]

    def ev_k(m, sg, B, tok):
        o, n, c = sg
        k, kk, b, nr = K1[:, 0:n], KK[:, 0:n], B1[:, 0:n], NR[:, 0:n]
        t0 = act(k, B, ACT.Copy, [tok, lastst[0]])
        t1 = ts(kk, k, vec("kk", m), None, MUL, w=[t0, lastst[0]])
        t2 = act(nr, kk, ACT.Square, [t1])
        bi, S, fr = bank()
        t3 = mm(S[:, 0:n], BONES, nr, True, True, [t2, fr], True)
        t4 = ts(nr, S[:, 0:n], 1e-24, 2.0 ** 20, MAX, MUL, w=[t3])
        bfree[bi] = t4
        t5 = act(nr, nr, ACT.Ln, [t4])
        t6 = act(nr, nr, ACT.Exp, [t5], scale=-0.5, bias=vec("l10"))
        t7 = tt(kk, kk, nr, MUL, [t6])
        t8 = tt(b, kk, AT[:, m, o:o + n], MUL, [t7, lastst[0]])
        t9 = ts(nr, AT[:, m, o:o + n], 1.0, vec("ka", m), SUB, MUL, w=[t7])
        t10 = stt(k, nr, 1.0, k, ADD, MUL, [t9])
        a1 = fe_store("t0", 3, k, m, sg, [t10])
        a2 = fe_store("t1", 5, kk, m, sg, [t7])
        a3 = fe_store("t2", 6, b, m, sg, [t8])
        lastst[0] = [a1, a2, a3, t10]
        if c == 0:
            t11 = tt(BS[:, m, :], BS[:, m, :], k, MUL, [t10, rts])
            t12 = ts(BS[:, m, :], BS[:, m, :], vec("rk", m), None, MUL, w=[t11])
            bi, S, fr = bank()
            t13 = mm(S[:, 0:n], BONES, BS[:, m, :], True, True, [t12, fr], True)
            t14 = cp(AC, BS[:, m, :], S[:, 0:n], [t13])
            bfree[bi] = t14
            lastst[0] = [a1, a2, a3, t12, t14]
        return t0
    gemm([("kr", j) for j in range(4)], xsrc, BOTH, ev_k, [tx])
    xmfree[0] = PE.last()
    tx = mix(3, BOTH)
    vfree = [[lastst[0]], [lastst[0]]]
    vc = [0]

    def ev_v(m, sg, B, tok):
        o, n, c = sg
        i = vc[0] % 2
        vc[0] += 1
        v = TM[i][:, 0:n]
        t0 = act(v, B, ACT.Copy, [tok, vfree[i]])
        a1 = fe_store(f"t{i}", 4, v, m, sg, [t0])
        vfree[i] = [a1]
        if c == 0:
            t1 = tt(BS[:, m, :], BS[:, m, :], v, MUL, [t0])
            vfree[i] = [a1, t1]
            vfree.append(dma(SP, "bon", BON[:, m, :], BS[:, m, :], [t1]))
        return t0
    gemm([("vr", j) for j in range(4)], xsrc, BOTH, ev_v, [tx])
    fe_done = [vfree[0][0], vfree[1][0], vfree[-1], lastst[0]]
    for e in (PE, DV, AC, PO, SP):
        e.wait(fe_done)
    fence()
    st.close()
    stC.close()

    st = ExitStack()
    MG = alloc(st, [P, 2, P])
    ML = alloc(st, [P, 2, 6, CH])
    E64 = alloc(st, [P, CH])
    tmk = [dma(AC, "cs", MG[:, :, :], ins["mg"].rearrange("p (a t) -> p a t", a=2)),
           dma(AC, "cs", ML[:, :, :, :], ins["ml"].rearrange("p (a b t) -> p a b t", a=2, b=6)),
           dma(AC, "cs", E64[:, :], ins["e64"])]
    DV.wait(tmk)
    PO.wait(tmk)
    NA = 7
    LD = [alloc(st, [P, NA, 8, CH]) for _ in range(2)]
    AR = [[alloc(st, [P, 8, 2, CH]) for _ in range(2)] for _ in range(2)]
    BK = [alloc(st, [P, 8, 3, CH]) for _ in range(2)]
    GG = [alloc(st, [P, 16, P]) for _ in range(2)]
    OB = [[alloc(st, [P, 8, P]) for _ in range(2)] for _ in range(2)]
    XD = [alloc(st, [P, 8, P]) for _ in range(2)]
    AU = [alloc(st, [P, 8, CH]) for _ in range(2)]
    XA = [alloc(st, [P, 8, CH]) for _ in range(2)]
    PP = [alloc(st, [P, 8, CH]) for _ in range(2)]
    UV = [alloc(st, [P, 16, CH]) for _ in range(2)]
    BT = [alloc(st, [P, 16, CH]) for _ in range(2)]
    EE = [alloc(st, [P, 8, CH]) for _ in range(2)]
    SS = [alloc(st, [P, 8, CH]) for _ in range(2)]
    YY = [alloc(st, [P, 8, CH]) for _ in range(2)]
    GM = [[alloc(st, [P, 3, 8]) for _ in range(2)] for _ in range(2)]
    for d in range(2):
        DV.do((), lambda e, d=d: e.memset(SS[d][:, :, :], 0.0))
        for j in range(2):
            DV.do((), lambda e, d=d, j=j: e.memset(AR[d][j][:, :, :, :], 0.0))
            DV.do((), lambda e, d=d, j=j: e.memset(OB[d][j][:, :, :], 0.0))
        DV.do((), lambda e, d=d: e.memset(XD[d][:, :, :], 0.0))
    tms = DV.last()
    for e in (PE, DV, AC, PO, SP):
        e.wait([tms])

    seqs = [[8, 9, 10, 11] + list(range(8)), [11, 10, 9, 8] + list(range(7, -1, -1))]
    ldf = [[None], [None]]
    yfree = [None, None]
    prev = [dict(), dict()]
    ys_tok = []

    def load(d, i):
        c = seqs[d][i]
        L = LD[d]
        if c >= 8:
            if d == 0:
                a = dma(SP, f"l{d}", L[:, 0:2, :, :], FE[c, :, 0:2, :, :], ldf[d])
                return dma(SP, f"l{d}", L[:, 3:7, :, :], FE[c, :, 3:7, :, :])
            return dma(SP, f"l{d}", L[:, 1:7, :, :], FE[c, :, 3:9, :, :], ldf[d])
        a0 = 0 if d == 0 else 2
        return dma(SP, f"l{d}", L[:, :, :, :], FE[c, :, a0:a0 + 7, :, :], ldf[d])

    ldt = [load(0, 0), load(1, 0)]
    

    def half(par):
        return slice(64 * par, 64 * par + 64)

    fl = lambda B: B[:, :].rearrange("p (a t) -> p a t", t=CH)

    def tilde(d, i):
        c = seqs[d][i]
        main = c < 8
        L, lt, pv = LD[d], ldt[d], prev[d]
        if d == 0:
            pf, lf, r, k, v, kk, b = [L[:, j, :, :] for j in range(7)]
        else:
            r, k, v, kk, b, pf, lf = [L[:, j, :, :] for j in range(7)]
        ar, bk, E, gm = AR[d][i % 2], BK[d], EE[d], GM[d][i % 2]
        last, mid = CH - 1, CH // 2 - 1
        if d == 0:
            t = tt(lf, pf, lf, SUB, [lt])
            gi, ge = pf, lf
        else:
            gl = gm[:, 2, :]
            t = cp(DV, gl, pf[:, :, last], [lt, pv.get(("gm", i % 2))])
            t = tt(pf, gl.unsqueeze(2).broadcast_to([P, 8, CH]), pf, SUB, [t])
            t = tt(lf, pf, lf, ADD, [t])
            gi, ge = lf, pf
        m_ix = mid if d == 0 else CH - 1 - mid
        l_ix = last if d == 0 else 0
        newf = gm[:, 0, :]
        tm = cp(DV, newf, gi[:, :, m_ix], [t, pv.get(("gm", i % 2))])
        mb = newf.unsqueeze(2).broadcast_to([P, 8, CH])
        sl0, sl1 = ar[:, :, 0, :], ar[:, :, 1, :]
        arf = pv.get(("ar", i % 2))
        tb = tt(sl0, ge, mb, SUB, [tm, arf])
        ta = tt(E[:, :, :], gi, mb, SUB, [tm, pv.get("bk")])
        tf = tt(gm[:, 1, :], gi[:, :, l_ix], newf, SUB, [tm])
        ea = act(sl0, sl0, ACT.Exp, [tb])
        if main:
            eb = act(sl1, E[:, :, :], ACT.Exp, [ta, arf])
        ec = act(E[:, :, :], E[:, :, :], ACT.Exp, [ta], scale=-1.0)
        t1 = stt(sl0, sl0, -1.0, kk, MUL, MUL, [ea])
        t3 = tt(bk[:, :, 0, :], E[:, :, :], b, MUL, [ec, pv.get("bk")])
        t4 = tt(bk[:, :, 1, :], E[:, :, :], k, MUL, [ec])
        t2 = tt(sl1, sl1, r, MUL, [eb]) if main else None
        t5 = cp(PO, bk[:, :, 2, :], bk[:, :, 0, :], [t3])
        pv["feats"] = [t1, t2, t3, t4, t5]
        pv["tm"], pv["tf"] = tm, tf

    def unit(d, i):
        c = seqs[d][i]
        main = c < 8
        L, lt, pv = LD[d], ldt[d], prev[d]
        v = L[:, 4, :, :] if d == 0 else L[:, 2, :, :]
        ar, bk, G, gm = AR[d][i % 2], BK[d], GG[d], GM[d][i % 2]
        Xt, Xd, Pm, A = XA[d], XD[d], PP[d], AU[d]
        feats, tm, tf = pv["feats"], pv["tm"], pv["tf"]
        bi, B, fr = bank()
        for h in range(16):
            rows = half(h % 2)
            t = mm(B[rows, (h // 2) * CH:(h // 2) * CH + CH], ar[rows, h // 2, 0, :], bk[rows, h // 2, 0, :],
                   True, True, [fr, feats], h == 15)
        a_t = tt(A[:, :, :], fl(B), MG[:, 1 - d:2 - d, 0:CH].broadcast_to([P, 8, CH]), MUL, [t, pv.get("inv")])
        bfree[bi] = a_t
        n2 = P if main else CH
        gts = []
        for q in range(4):
            bi, B, fr = bank()
            h0 = 8 * (q // 2) + q % 2
            for j in range(4):
                h = h0 + 2 * j
                rows = half(h % 2)
                lhs = bk[rows, h // 2, (h % 2):(h % 2) + 2, :].rearrange("p a t -> p (a t)")
                t = mm(B[:, j * P:j * P + n2], lhs, ar[rows, h // 2, 0:(2 if main else 1), :].rearrange(
                    "p a t -> p (a t)"), True, True, [fr, feats], j == 3)
            gts.append(tt(G[:, h0:h0 + 7:2, 0:n2], B[:, :].rearrange("p (j n) -> p j n", j=4)[:, :, 0:n2],
                          MG[:, d:d + 1, 0:n2].broadcast_to([P, 4, n2]), MUL, [t, pv.get("gfree")]))
            bfree[bi] = gts[-1]
        xs = []
        for par in range(2):
            rows = half(par)
            gv = G[rows, par:16:2, 0:CH]
            x1 = tt(Xt[rows, :, :], gv, ML[rows, d, 0:1, :].broadcast_to([64, 8, CH]), MUL, [gts, pv.get("inv")], E=PO)
            xs.append(x1)
        tx = tt(Xt[:, :, :], Xt[:, :, :], E64[:, :].unsqueeze(1).broadcast_to([P, 8, CH]), ADD, [xs])

        def omask(lev):
            O, key = OB[d][lev % 2], ("o", lev % 2)
            return [tt(O[half(par), :, 64 * par:64 * par + 64], A[half(par), :, :],
                       ML[half(par), 1 - d, lev:lev + 1, :].broadcast_to([64, 8, CH]), MUL, [a_t, pv.get(key)], E=PO)
                    for par in range(2)]
        ot = omask(1)
        yield
        ev_v = []
        for hf in range(2):
            bi, B, fr = bank()
            for j in range(4):
                t = tr(B[0:64, j * 128:j * 128 + 128], v[:, 4 * hf + j, :], ID, [fr, lt], j == 3)
            src = B[0:64, :].rearrange("p (j a c) -> p j a c", j=4, a=2)
            dsto = UV[d][0:64, 8 * hf + 1:8 * hf + 8:2, :]
            dste = UV[d][64:128, 8 * hf:8 * hf + 8:2, :]
            x1 = cp(AC, dsto, src[:, :, 1, :], [t, pv.get("uv")])
            x2 = cp(AC, dste, src[:, :, 0, :], [t, pv.get("uv")])
            bfree[bi] = [x1, x2]
            ev_v += [x1, x2]
        bts = []
        for q in range(2):
            bi, B, fr = bank()
            for j in range(8):
                h = 2 * j + q
                rows = half(h % 2)
                lhs = bk[rows, h // 2, (h % 2):(h % 2) + 2, :].rearrange("p a t -> p (a t)")
                t = tr(B[:, j * CH:j * CH + CH], lhs, ID[rows, 64 * (h % 2):64 * (h % 2) + 64], [fr], j == 7)
            x = cp(AC, BT[d][:, q:16:2, :], B[:, :].rearrange("p (a t) -> p a t", t=CH), [t, pv.get("s_mm")])
            bfree[bi] = x
            bts.append(x)
        pv["bk"] = PE.last()
        ldf[d] = [DV.last(), PE.last(), PO.last(), AC.last()]
        if i + 1 < 12:
            ldt[d] = load(d, i + 1)
        yield
        for lev in range(1, 6):
            if lev < 5:
                on = omask(lev + 1)
            xd = []
            for q in range(2):
                bi, B, fr = bank()
                for p in range(4):
                    t = tr(B[0:64, p * P:p * P + P], Xt[:, 4 * q + p, :], ID, [fr, tx], p == 3)
                src = B[0:64, :].rearrange("p (j a c) -> p j a c", j=4, a=2)
                for par in range(2):
                    xd.append(cp(AC, Xd[half(par), 4 * q:4 * q + 4, 64 * par:64 * par + 64], src[:, :, par, :],
                                 [t, pv.get("xd")]))
                bfree[bi] = xd[-2:]
            bi, B, fr = bank()
            O = OB[d][lev % 2]
            for p in range(8):
                t = mm(B[:, p * CH:p * CH + CH], O[:, p, :], Xt[:, p, :], True, True, [fr, ot], p == 7)
            pv[("o", lev % 2)] = t
            tp = cp(DV if lev % 2 else AC, Pm[:, :, :], fl(B), [t, pv.get("pm")])
            bfree[bi] = tp
            yield
            bi, B, fr = bank()
            for p in range(8):
                t = mm(B[:, p * CH:p * CH + CH], Xd[:, p, :], Pm[:, p, :], True, True, [fr, tp, xd], p == 7)
            pv["pm"] = pv["xd"] = t
            if lev < 5:
                tx = tt(Xt[:, :, :], Xt[:, :, :], fl(B), ADD, [t])
                ot = on
            else:
                tx = [tt(Xd[half(par), :, 64 * par:64 * par + 64], Xt[half(par), :, :], fl(B)[half(par), :, :], ADD,
                         [t]) for par in range(2)]
                pv["inv"] = tx
            bfree[bi] = tx
            yield
        pv["inv"] = [tx, PE.last(), PO.last()]
        S, uv, fx = SS[d], UV[d], pv["fx"]
        te = act(fx[:, 0, :], gm[:, 0, :], ACT.Exp, [tm, pv.get("s_upd")])
        tex = act(fx[:, 1, :], gm[:, 1, :], ACT.Exp, [tf, pv.get("s_upd")])
        tS = tt(S[:, :, :], S[:, :, :], fx[:, 0, :].unsqueeze(2).broadcast_to([P, 8, CH]), MUL, [te, pv.get("s_upd")])
        zb = []
        for which in range(2):
            bi, B, fr = bank()
            for h in range(16):
                par = h % 2
                rows = half(par)
                oth = half(1 - par)
                col = (h // 2) * CH
                if which == 0:
                    t = mm(B[rows, col:col + CH], G[oth, h, 0:CH], uv[oth, h, :], True, True, [fr, ev_v, gts], h == 15)
                else:
                    t = mm(B[rows, col:col + CH], ar[rows, h // 2, 0, :], S[rows, h // 2, :], True, True, [fr, tS],
                           h == 15)
            zb.append((bi, B, t))
        z = Pm
        z0 = cp(AC, z[:, :, :], fl(zb[0][1]), [zb[0][2], pv["pm"]])
        bfree[zb[0][0]] = z0
        zt = tt(z[:, :, :], z[:, :, :], fl(zb[1][1]), ADD, [z0, zb[1][2]])
        bfree[zb[1][0]] = zt
        if i + 1 < 12:
            tilde(d, i + 1)
        yield
        bi, B, fr = bank()
        for p in range(8):
            t = mm(B[:, p * CH:p * CH + CH], Xd[:, p, :], z[:, p, :], True, True, [fr, zt, tx], p == 7)
        pv["pm"] = pv["xd"] = t
        ut = []
        for par in range(2):
            ut.append(cp((AC, DV)[par], uv[half(par), par:16:2, :], fl(B)[half(par), :, :], [t]))
        bfree[bi] = ut
        yield
        bi, B, fr = bank()
        for h in range(16):
            t = mm(B[half(h % 2), (h // 2) * CH:(h // 2) * CH + CH], BT[d][:, h, :], uv[:, h, :], True, True,
                   [fr, bts, ut], h == 15)
        pv["s_mm"] = pv["uv"] = t
        pv["gfree"] = [t, PO.last()]
        bs, BS_ = bi, B
        if main:
            bi, B, fr = bank()
            for h in range(16):
                rows = half(h % 2)
                col = (h // 2) * CH
                mm(B[rows, col:col + CH], S[rows, h // 2, :], ar[rows, h // 2, 1, :], True, False, [fr])
                t = mm(B[rows, col:col + CH], uv[:, h, :], G[:, h, CH:P], False, True, (), h == 15)
            ty = cp(AC, YY[d][:, :, :], fl(B), [t, yfree[d]])
            bfree[bi] = ty
            yfree[d] = dma(SP, f"y{d}", YS[d, c].rearrange("p (a t) -> p a t", t=CH), YY[d][:, :, :], [ty])
            pv["uv"] = t
            pv["gfree"] = [t, PO.last()]
        pv[("ar", i % 2)] = PE.last()
        t = tt(S[:, :, :], S[:, :, :], fl(BS_), ADD, [t])
        bfree[bs] = t
        t = tt(S[:, :, :], S[:, :, :], fx[:, 1, :].unsqueeze(2).broadcast_to([P, 8, CH]), MUL, [t, tex])
        pv["s_upd"] = [t, tex, te]
        pv[("gm", i % 2)] = [tex, te, t]
        yield

    for d in range(2):
        prev[d]["fx"] = alloc(st, [P, 2, 8])
        tilde(d, 0)
    for i in range(12):
        gens = [unit(0, i), unit(1, i)]
        while gens:
            for g in list(gens):
                try:
                    next(g)
                except StopIteration:
                    gens.remove(g)
    for e in (PE, DV, AC, PO, SP):
        e.wait(list(yfree))
    fence()
    st.close()

    st = ExitStack()
    YA = [alloc(st, [P, 8, 8, CH]) for _ in range(2)]
    BO = alloc(st, [P, 8, T])
    OO = alloc(st, [P, 8, T])
    splits_begin(st)
    OH, OL = alloc(st, [P, 8, T], F32R), alloc(st, [P, 8, T], F32R)
    tl = [dma(SP, "rd", YA[d][:, :, :, :], YS[d].rearrange("c p (a t) -> p c a t", t=CH)) for d in range(2)]
    tl.append(dma(SP, "rd", BO[:, :, :], BON))
    TR = [[alloc(st, [P, T]) for _ in range(3)] for _ in range(2)]
    trf = [[None], [None]]
    sG, WG, wtG = panel("g2")
    cnt = 0
    for m in range(8):
        for d in range(2):
            i = cnt % 2
            cnt += 1
            y = YA[d][:, :, m, :]
            a, b, c_ = TR[i]
            v3 = lambda z: z[:, :].rearrange("p (c t) -> p c t", t=CH)
            t0 = cp(PO, v3(a), y, [tl, trf[i]])
            bi, B, fr = bank()
            t = mm(B[:, :], BONES, a[:, :], True, True, [t0, fr], True)
            t1 = stt(a[:, :], B[:, :], -1.0 / 64, a[:, :], MUL, ADD, [t])
            bfree[bi] = t1
            t2 = act(b[:, :], a[:, :], ACT.Square, [t1, trf[i]])
            bi, B, fr = bank()
            t = mm(B[:, :], BONES, b[:, :], True, True, [t2, fr], True)
            t3, t4 = rstd(b[:, :], B[:, :], 1.0 / 64, "egn", [t])
            bfree[bi] = t3
            t5 = tt(a[:, :], a[:, :], b[:, :], MUL, [t4])
            t6 = act(a[:, :], a[:, :], ACT.Identity, [t5], scale=vec("gng", m), bias=vec("gnb", m))
            t7 = tt(a[:, :], a[:, :], BO[:, m, :], ADD, [t6])
            bi, B, fr = bank()
            t = mm(B[:, :], WG[:, d * 1024 + m * P:d * 1024 + m * P + P], SG[:, d, :], True, True, [wtG, fr], True)
            if d == 0:
                t8 = tt(OO[:, m, :], a[:, :], B[:, :], MUL, [t, t7])
                bfree[bi] = t8
            else:
                t9 = tt(c_[:, :], a[:, :], B[:, :], MUL, [t, t7])
                bfree[bi] = t9
                t8 = tt(OO[:, m, :], OO[:, m, :], c_[:, :], ADD, [t9])
                t_o = split(OH[:, m, :], OL[:, m, :], OO[:, m, :], [t8])
            trf[i] = [t8]
    release(sG, PE.last())
    will_use([("wor", j) for j in range(4)])
    gemm3(8, 8, lambda k, sg: (OH[:, k, :], OL[:, k, :]), [MAIN], resid(1, 2), [t_o])
    fence()
    st.close()
    stS.close()

    st = ExitStack()
    splits_begin(st)
    HH, HL = alloc(st, [P, 8, T], F32R), alloc(st, [P, 8, T], F32R)
    hh = rms_mod(res, HH, HL, [MAIN], 1, 1, st)
    mlp(res, [MAIN], st, mlp_keys("m1", "m2", 1), HH, HL,
        lambda m, sg: ADA[:, 1, 5, m, 0:1], None, None, hh)
    fence()
    st.close()

    def layer_norm(g, b, XH, XL):
        st = ExitStack()
        Q = [alloc(st, [P, T]) for _ in range(3)]
        R = alloc(st, [P, T])
        M = alloc(st, [P, T])
        PE.wait([DV.last()])
        bi, B, fr = bank()
        for k in range(8):
            t = mm(B[:, :], ONES, X[:, k, :], k == 0, k == 7, [fr], k == 7)
        t = act(M[:, :], B[:, :], ACT.Copy, [t], scale=1.0 / 1024)
        bfree[bi] = t
        bi, B, fr = bank()
        qf = [None] * 3
        for k in range(8):
            t1 = tt(X[:, k, :], X[:, k, :], M[:, :], SUB, [t])
            t2 = act(Q[k % 3][:, :], X[:, k, :], ACT.Square, [t1, qf[k % 3]])
            t3 = qf[k % 3] = mm(B[:, :], ONES, Q[k % 3][:, :], k == 0, k == 7, [fr, t2], True)
        t4, t5 = rstd(R[:, :], B[:, :], 1.0 / 1024, "e5", [t3])
        bfree[bi] = t4
        for k in range(8):
            t6 = tt(X[:, k, :], X[:, k, :], R[:, :], MUL, [t5])
            t7 = act(X[:, k, :], X[:, k, :], ACT.Identity, [t6], scale=vec(g, k), bias=vec(b, k))
            t8 = split(XH[:, k, :], XL[:, k, :], X[:, k, :], [t7])
        fence()
        st.close()
        return t8

    def ffn_ple(l):
        st = ExitStack()
        splits_begin(st)
        XH, XL = alloc(st, [P, 8, T], F32R), alloc(st, [P, 8, T], F32R)
        xh = lambda k, sg: (XH[:, k, :], XL[:, k, :])
        layer_norm(f"ln1g{l}", f"ln1b{l}", XH, XL)
        st2 = ExitStack()
        mlp(lambda k, sg: X[:, k, :], [MAIN], st2, mlp_keys("f1", "f2", l), XH, XL, None, None, ALPHA)
        fence()
        st2.close()
        PTt = alloc(st, [P, 2, T])
        tp = dma(AC, "cs", PTt[:, :, :], ins[f"p{l}"].rearrange("p (k t) -> p k t", k=2))
        EM = alloc(st, [P, 8, T])
        SQ = [alloc(st, [P, T]) for _ in range(2)]
        R = alloc(st, [P, T])
        s, W, wt = panel(("pp", l))
        for m in range(8):
            bi, B, fr = bank()
            for k in range(2):
                t = mm(B[:, :], W[:, k * 1024 + m * P:k * 1024 + m * P + P], PTt[:, k, :], k == 0, k == 1,
                       [wt, fr, tp], k == 1)
            t1 = cp(AC, EM[:, m, :], B[:, :], [t])
            bfree[bi] = t1
        release(s, t)
        bi, B, fr = bank()
        sf = [None, None]
        for m in range(8):
            t2 = act(SQ[m % 2][:, :], EM[:, m, :], ACT.Square, [t1, sf[m % 2]])
            t3 = mm(B[:, :], ONES, SQ[m % 2][:, :], m == 0, m == 7, [fr, t2], True)
            sf[m % 2] = t3
        t4, t5 = rstd(R[:, :], B[:, :], 1.0 / 1024, "e5", [t3])
        bfree[bi] = t4
        for m in range(8):
            t6 = stt(EM[:, m, :], EM[:, m, :], vec(f"plg{l}", m), R[:, :], MUL, MUL, [t5])
        layer_norm(f"ln2g{l}", f"ln2b{l}", XH, XL)
        will_use([("pg", l, j) for j in range(4)])
        Gt = [alloc(st, [P, T]) for _ in range(2)]
        gf = [None, None]

        def ev(m, sg, B, tok):
            g = Gt[m % 2][:, :]
            t = act(g, B, ACT.Sigmoid, [tok, gf[m % 2]])
            t1 = tt(g, g, EM[:, m, :], MUL, [t, t6])
            gf[m % 2] = tt(X[:, m, :], g, X[:, m, :], ADD, [t1])
            return t
        gemm3(8, 8, xh, [MAIN], ev)
        fence()
        st.close()

    st = ExitStack()
    splits_begin(st)
    will_use([(a, j) for a in ("qa", "ka", "va", "hq", "hf", "hi", "hg", "evo") for j in range(4 if a == "evo" else 2)])
    XH, XL = alloc(st, [P, 8, T], F32R), alloc(st, [P, 8, T], F32R)
    xh = lambda k, sg: (XH[:, k, :], XL[:, k, :])
    xht = lambda k, tb: (XH[:, k, tb * P:tb * P + P], XL[:, k, tb * P:tb * P + P])
    for k in range(8):
        t_x = split(XH[:, k, :], XL[:, k, :], X[:, k, :])
    CS = alloc(st, [P, 2, T])
    tcs = dma(AC, "cs", CS[:, :, :], ins["cs1"].rearrange("p (a t) -> p a t", a=2))
    MK = alloc(st, [P, 4, P])
    CZ = alloc(st, [P, 3, P])
    tcs = [tcs, dma(AC, "cs", MK[:, :, :], ins["ck"].rearrange("p (a t) -> p a t", a=4)),
           dma(AC, "cs", CZ[:, :, :], ins["cz"].rearrange("p (a t) -> p a t", a=3))]
    for e in (DV, PO):
        e.wait(tcs)
    Q4 = alloc(st, [P, 4, T])
    K4 = alloc(st, [P, 4, T])
    VA = alloc(st, [P, 4, 512])
    OM = alloc(st, [P, 8, T])
    TQ = [alloc(st, [P, T]) for _ in range(4)]

    def rope_evac(dst, m0, TQ):
        fr2 = [[None], [None]]
        n = [0]

        def f(m, sg, B, tok):
            i = n[0] % 2
            n[0] += 1
            a, b = TQ[2 * i][:, :], TQ[2 * i + 1][:, :]
            t0 = act(a, B, ACT.Copy, [tok] + fr2[i])
            bi, S, fr = bank()
            t1 = mm(S[:, :], PERM[1], a, True, True, [t0, fr], True)
            t2 = tt(b, S[:, :], CS[:, 1, :], MUL, [t1] + fr2[i])
            bfree[bi] = t2
            t3 = tt(dst[:, m, :], a, CS[:, 0, :], MUL, [t0])
            t4 = tt(dst[:, m, :], dst[:, m, :], b, ADD, [t3, t2])
            fr2[i] = [t4, t1]
            return t0
        return f

    gemm3(4, 8, xh, [MAIN], rope_evac(Q4, 0, TQ), [t_x])
    fence()
    gemm3(4, 8, xh, [MAIN], rope_evac(K4, 0, TQ))
    st_v = ExitStack()
    gemm3_tok(4, xh, [MAIN], VA, st_v)
    fence()
    st_v.close()
    t = tt(SM[0:64, 0:1], vec("lam", 0, 1, slice(0, 64)), vec("lam", 1, 1, slice(0, 64)), MUL)
    t = [t, tt(SM[0:64, 1:2], vec("lam", 2, 1, slice(0, 64)), vec("lam", 3, 1, slice(0, 64)), MUL)]
    bi, B, fr = bank()
    t = mm(B[:, 0:2], ONES[0:64, :], SM[0:64, 0:2], True, True, [t, fr], True)
    t = act(SM[:, 2:4], B[:, 0:2], ACT.Exp, [t])
    bfree[bi] = t
    t = tt(SM[:, 4:5], SM[:, 3:4], SM[:, 2:3], SUB, [t])
    t_lam = ts(SM[:, 4:5], SM[:, 4:5], -(0.8 - 0.6), None, ADD, w=[t])
    fence()
    stD = ExitStack()
    S2 = [alloc(stD, [P, 2, T]) for _ in range(2)]
    P2 = [alloc(stD, [P, 4, P]) for _ in range(2)]
    NS = alloc(stD, [P, 2, 2, 4])
    s2f, p2f = [None, None], [None, None]
    un2 = 0

    def diff_unit(h, qb, u):
        nk = (qb + 1) * P
        S, Pt, sm = S2[u], P2[u], NS[:, u, :, :]
        ev = []
        for c in range(2):
            rows = slice(64 * c, 64 * c + 64)
            bi, B, fr = bank()
            t = mm(B[:, 0:nk], Q4[rows, h, qb * P:qb * P + P], K4[rows, h, 0:nk], True, True, [fr], True)
            r = stt(S[:, c, 0:nk], B[:, 0:nk], 0.125, MK[:, 3 - qb:4, :].rearrange("p a b -> p (a b)"), MUL, ADD,
                    [t, s2f[u]])
            bfree[bi] = r
            ev.append(r)
        mx, ng, dn = sm[:, :, 0], sm[:, :, 1], sm[:, :, 2]
        t = rmax(mx, S[:, :, 0:nk], ev)
        t = ts(ng, mx, -1.0, None, MUL, w=[t])
        ee = [act(S[:, c, 0:nk], S[:, c, 0:nk], ACT.Exp, [t], bias=ng[:, c:c + 1], accum_out=dn[:, c:c + 1])
              for c in range(2)]
        t = recip(dn, dn, ee)
        t = tt(dn[:, 1:2], dn[:, 1:2], SM[:, 4:5], MUL, [t])
        a = ts(S[:, 0, 0:nk], S[:, 0, 0:nk], dn[:, 0:1], None, MUL, w=[t])
        pn = stt(S[:, 0, 0:nk], S[:, 1, 0:nk], dn[:, 1:2], S[:, 0, 0:nk], MUL, ADD, [a])

        def back():
            bi, B, fr = bank()
            for b in range(qb + 1):
                t = tr(B[:, b * P:b * P + P], S[:, 0, b * P:b * P + P], ID, [fr, pn], b == qb)
            s2f[u] = t
            r = cp(AC, Pt[:, 0:qb + 1, :], B[:, 0:nk].rearrange("p (a b) -> p a b", b=P), [t, p2f[u]])
            bfree[bi] = r
            bi, B, fr = bank()
            for b in range(qb + 1):
                t = mm(B[:, 0:P], VA[:, b, h * P:h * P + P], Pt[:, b, :], b == 0, b == qb, [fr, r], b == qb)
            p2f[u] = t
            bfree[bi] = cp(DV, OM[:, h, qb * P:qb * P + P], B[:, 0:P], [t])
        return back

    pend = None
    for qb in range(4):
        for h in range(4):
            nxt = diff_unit(h, qb, un2 % 2)
            un2 += 1
            if pend:
                pend()
            pend = nxt
    pend()

    def rms_head(ap, gain, sq, rr, w, scale):
        t = act(sq, ap, ACT.Square, w)
        bi, B, fr = bank()
        t = mm(B[:, :], ONES, sq, True, True, [t, fr], True)
        bfree[bi], t = rstd(rr, B[:, :], 1.0 / 128, "e5", [t])
        t = stt(ap, ap, vec(gain), rr, MUL, MUL, [t])
        if scale != 1.0:
            t = ts(ap, ap, scale, None, MUL, w=[t])
        return t

    fence()
    for h in range(4):
        rms_head(OM[:, h, :], "subg", TQ[0][:, :], TQ[1][:, :], [DV.last(), PE.last()], 1.0 - (0.8 - 0.6))
    fence()
    stD.close()
    LF = alloc(st, [P, 4, T])
    SCN = alloc(st, [P, T])
    DV.wait([dma(AC, "cs", SCN[:, :], ins["scn"][:, 0:T])])
    LB = alloc(st, [P, 2, 4])
    lb2 = vec("lb", 0, 8).rearrange("p (a b) -> p a b", a=2)
    L3 = alloc(st, [P, 3, 4])
    t = tt(L3[:, 0, :], lb2[:, 0, :], lb2[:, 1, :], MAX)
    ta_ = tt(L3[:, 1, :], lb2[:, 0, :], L3[:, 0, :], SUB, [t])
    tb_ = tt(L3[:, 2, :], lb2[:, 1, :], L3[:, 0, :], SUB, [t])
    t = act(L3[:, 1:3, :], L3[:, 1:3, :], ACT.Exp, [ta_, tb_])
    t = tt(L3[:, 0, :], L3[:, 1, :], L3[:, 2, :], ADD, [t])
    t = recip(L3[:, 0, :], L3[:, 0, :], [t])
    t = tt(LB[:, 0, :], L3[:, 1, :], L3[:, 0, :], MUL, [t])
    t_lb = ts(LB[:, 1, :], LB[:, 0, :], -1.0, 1.0, MUL, ADD, w=[t])
    fr4 = [[None]] * 4

    def ev_silu(dst, T0):
        fr = [[None], [None]]

        def f(m, sg, B, tok):
            i = m % 2
            a = T0[2 * i][:, :]
            t0 = act(a, B, ACT.Sigmoid, [tok] + fr[i])
            t1 = tt(dst[:, m, :], B, a, MUL, [t0])
            fr[i] = [t1]
            return t1
        return f

    def ev_f(m, sg, B, tok):
        t2 = t0 = act(K4[:, m, :], B, ACT.Sigmoid, [tok])
        t3 = ts(LF[:, m, :], K4[:, m, :], LB[:, 1, m:m + 1], LB[:, 0, m:m + 1], MUL, ADD, w=[t2, t_lb])
        t4 = ts(K4[:, m, :], LF[:, m, :], -1.0, 1.0, MUL, ADD, w=[t3])
        lf_toks.append((m, t4))
        return t0
    lf_toks = []
    gemm3(4, 8, xh, [MAIN], ev_silu(Q4, TQ))
    gemm3(4, 8, xh, [MAIN], ev_f)
    for m, t4 in lf_toks:
        act(LF[:, m, :], LF[:, m, :], ACT.Ln, [t4])
    st_v = ExitStack()
    gemm3_tok(4, xh, [MAIN], VA, st_v)
    fence()
    st_v.close()
    fence()
    HG = alloc(st, [P, 4, T])
    gemm3(4, 8, xh, [MAIN], ev_silu(HG, TQ))
    CB = alloc(st, [P, 4, T])
    QP = alloc(st, [P, T])
    KP = alloc(st, [P, T])
    QO = alloc(st, [P, T])
    KS = alloc(st, [P, T])
    KST = alloc(st, [P, 4, P])
    AA = [alloc(st, [P, CH]) for _ in range(2)]
    DC = alloc(st, [P, 8])
    SH = alloc(st, [P, P])
    MU = alloc(st, [P, CH], mybir.dt.uint32)
    tmu = ts(MU[:, :], CZ[:, 1, 0:CH], 1.0, None, MUL)
    fence()
    for h in range(4):
        c3 = lambda z: z.rearrange("p (c t) -> p c t", t=CH)
        b_, l_ = CB[:, h, :], LF[:, h, :]
        t0 = DV.do((), lambda e, b_=b_, l_=l_: e.tensor_tensor_scan(b_, SCN[:, :], l_, 0.0, MUL, ADD))
        bc = c3(b_)
        mid = bc[:, :, CH // 2 - 1:CH // 2].broadcast_to([P, 8, CH])
        las = bc[:, :, CH - 1:CH].broadcast_to([P, 8, CH])
        q_, k_ = Q4[:, h, :], K4[:, h, :]
        t1 = tt(c3(QP[:, :]), bc, mid, SUB, [t0])
        t2 = act(KP[:, :], QP[:, :], ACT.Exp, [t1], scale=-1.0)
        t3 = act(QP[:, :], QP[:, :], ACT.Exp, [t1])
        t4 = act(QO[:, :], b_, ACT.Exp, [t0])
        t5 = tt(c3(KS[:, :]), las, bc, SUB, [t0])
        t6 = act(KS[:, :], KS[:, :], ACT.Exp, [t5])
        t7 = act(DC[:, :], bc[:, :, CH - 1], ACT.Exp, [t0])
        u = [tt(QP[:, :], QP[:, :], q_, MUL, [t3, t2]), tt(KP[:, :], KP[:, :], k_, MUL, [t2]),
             tt(QO[:, :], QO[:, :], q_, MUL, [t4]), tt(KS[:, :], KS[:, :], k_, MUL, [t6])]
        bi, B, fr = bank()
        for tb in range(4):
            t = tr(B[:, tb * P:tb * P + P], KS[:, tb * P:tb * P + P], ID, [fr, u], tb == 3)
        tk = cp(AC, KST[:, :, :], B[:, :].rearrange("p (a b) -> p a b", b=P), [t])
        bfree[bi] = tk
        tS = DV.do((), lambda e: e.memset(SH[:, :], 0.0))
        for i in range(2):
            tz = DV.do([PE.last()], lambda e, i=i: e.memset(AA[i][:, :], 0.0))
        aaf = [None, None]
        atok = {}

        def intra(c):
            rows = slice(64 * (c % 2), 64 * (c % 2) + 64)
            A = AA[(c // 2) % 2]
            bi, B, fr = bank()
            cc = slice(c * CH, c * CH + CH)
            r0, c0, hf = rows.start, c * CH, CH // 2
            mm(B[r0:r0 + hf, 0:CH], KP[:, c0:c0 + hf], QP[:, cc], True, True, [fr, u])
            t = mm(B[r0 + hf:r0 + CH, hf:CH], KP[:, c0 + hf:c0 + CH], QP[:, c0 + hf:c0 + CH], True, True, (), True)
            w = [t, aaf[(c // 2) % 2], tmu, tz]
            q4 = []
            for r, co in ((r0, 0), (r0 + hf, hf)):
                am, bm, mm_ = A[r:r + hf, co:CH], B[r:r + hf, co:CH], MU[r:r + hf, co:CH]
                q4.append(DV.do(w, lambda e, am=am, bm=bm, mm_=mm_: e.copy_predicated(am, mm_, bm)))
            atok[c] = q4
            bfree[bi] = atok[c]
        intra(0)
        intra(1)
        for c in range(8):
            rows = slice(64 * (c % 2), 64 * (c % 2) + 64)
            A = AA[(c // 2) % 2]
            cc = slice(c * CH, c * CH + CH)
            bi, B, fr = bank()
            v_ = VA[rows, c // 2, h * P:h * P + P]
            mm(B[:, 0:CH], v_, A[rows, :], True, False, [fr, atok[c]])
            t = mm(B[:, 0:CH], SH[:, :], QO[:, cc], False, True, [tS], True)
            aaf[(c // 2) % 2] = t
            bfree[bi] = cp(AC, OM[:, 4 + h, cc], B[:, 0:CH], [t])
            if c < 7:
                bj, B2, fr2 = bank()
                t2 = mm(B2[:, 0:P], KST[rows, c // 2, :], v_, True, True, [fr2, tk], True)
                tS = stt(SH[:, :], SH[:, :], DC[:, c:c + 1], B2[:, 0:P], MUL, ADD, [t2, tS, t7])
                bfree[bj] = tS
            if c % 2 == 1 and c < 7:
                intra(c + 1)
                intra(c + 2)
        fence()
        t = rms_head(OM[:, 4 + h, :], "hgg", QP[:, :], KP[:, :], (), 1.0)
        tt(OM[:, 4 + h, :], OM[:, 4 + h, :], HG[:, h, :], MUL, [t])
        fence()

    def ev_mix(m, sg, B, tok):
        return stt(X[:, m, :], X[:, m, :], ALPHA, B, MUL, ADD, [tok])
    for k in range(8):
        t_o = split(XH[:, k, :], XL[:, k, :], OM[:, k, :])
    gemm3(8, 8, xh, [MAIN], ev_mix, [t_o])
    fence()
    st.close()
    ffn_ple(0)

    st = ExitStack()
    CS = alloc(st, [P, 2, T])
    tcs = [dma(AC, "cs", CS[:, :, :], ins["cs1"].rearrange("p (a t) -> p a t", a=2))]
    MK = alloc(st, [P, 4, P])
    tcs.append(dma(AC, "cs", MK[:, :, :], ins["mk"].rearrange("p (a t) -> p a t", a=4)))
    DV.wait(tcs)
    XH, XL = alloc(st, [P, 8, T], F32R), alloc(st, [P, 8, T], F32R)
    splits_begin(st, 2)
    will_use([(a, j) for a in ("oq", "ok", "ov", "odo") for j in range(4)])
    xh = lambda k, sg: (XH[:, k, :], XL[:, k, :])
    for k in range(8):
        t_x = split(XH[:, k, :], XL[:, k, :], X[:, k, :])
    Q8 = alloc(st, [P, 8, T])
    K8 = alloc(st, [P, 8, T])
    V8 = alloc(st, [P, 4, 1024])
    OM = alloc(st, [P, 8, T])
    st2 = ExitStack()
    TQ = [alloc(st2, [P, T]) for _ in range(4)]
    gemm3(8, 8, xh, [MAIN], rope_evac(Q8, 0, TQ), [t_x])
    fence()
    gemm3(8, 8, xh, [MAIN], rope_evac(K8, 0, TQ))
    gemm3_tok(8, xh, [MAIN], V8, st2)
    fence()
    st2.close()
    S4 = [alloc(st, [P, 4, T]) for _ in range(2)]
    P4 = [alloc(st, [P, 4, 512]) for _ in range(2)]
    NS = alloc(st, [P, 2, 4, 4])
    s4f, p4f = [None, None], [None, None]

    def dil_unit(g, qb, u):
        nk = (qb + 1) * P
        S, Pt, sm = S4[u], P4[u], NS[:, u, :, :]
        mk = MK[:, 3 - qb:4, :].rearrange("p a b -> p (a b)")
        ev = []
        for i in range(4):
            h = 4 * g + i
            rows = slice(64 * (h % 2), 64 * (h % 2) + 64)
            bi, B, fr = bank()
            t = mm(B[:, 0:nk], Q8[rows, h // 2, qb * P:qb * P + P], K8[rows, h // 2, 0:nk], True, True, [fr], True)
            r = stt(S[:, i, 0:nk], B[:, 0:nk], 0.125, mk, MUL, ADD, [t, s4f[u]])
            bfree[bi] = r
            ev.append(r)
        mx, ng, dn = sm[:, :, 0], sm[:, :, 1], sm[:, :, 2]
        t = rmax(mx, S[:, :, 0:nk], ev)
        t = ts(ng, mx, -1.0, None, MUL, w=[t])
        ee = [act(S[:, c, 0:nk], S[:, c, 0:nk], ACT.Exp, [t], bias=ng[:, c:c + 1], accum_out=dn[:, c:c + 1])
              for c in range(4)]
        t = recip(dn, dn, ee)
        pn = [ts(S[:, i, 0:nk], S[:, i, 0:nk], dn[:, i:i + 1], None, MUL, w=[t]) for i in range(4)]

        def back():
            pts = []
            for b in range(qb + 1):
                bi, B, fr = bank()
                for i in range(4):
                    t = tr(B[:, i * P:i * P + P], S[:, i, b * P:b * P + P], ID, [fr, pn], i == 3)
                r = cp(AC, Pt[:, b, :], B[:, :], [t, p4f[u]])
                bfree[bi] = r
                pts.append(r)
            s4f[u] = PE.last()
            bi, B, fr = bank()
            for i in range(4):
                h = 4 * g + i
                rows = slice(64 * (h % 2), 64 * (h % 2) + 64)
                col = (i // 2) * P
                for b in range(qb + 1):
                    t = mm(B[rows, col:col + P], V8[:, b, h * 64:h * 64 + 64], Pt[:, b, i * P:i * P + P], b == 0,
                           b == qb, [fr, pts], i == 3 and b == qb)
            p4f[u] = t
            bfree[bi] = cp(AC, OM[:, 2 * g:2 * g + 2, qb * P:qb * P + P],
                           B[:, 0:256].rearrange("p (a b) -> p a b", b=P), [t])
        return back

    pend = None
    n = 0
    for qb in range(4):
        for g in range(4):
            nxt = dil_unit(g, qb, n % 2)
            n += 1
            if pend:
                pend()
            pend = nxt
    pend()
    t_o = AC.last()
    for k in range(8):
        t_o = split(XH[:, k, :], XL[:, k, :], OM[:, k, :], [t_o])
    gemm3(8, 8, xh, [MAIN], ev_mix, [t_o])
    fence()
    st.close()
    ffn_ple(1)

    t = dma(SP, "out", out_d, X[:, :, :].rearrange("p k t -> p (k t)"))
    SP.wait([t])

    block = ctx.enter_context(nc.Block())

    @block.tensor
    def _(e):
        PE.emit(e)

    @block.vector
    def _(e):
        DV.emit(e)

    @block.scalar
    def _(e):
        AC.emit(e)

    @block.gpsimd
    def _(e):
        PO.emit(e)

    @block.sync
    def _(e):
        SP.emit(e)

    ctx.close()


def constants():
    f = np.float32
    c = {}
    i = np.arange(P)
    cst = np.zeros((P, 5, P), f)
    cst[:, 0] = np.eye(P)
    cst[:, 1] = 1
    cst[:, 2] = (i[:, None] // 64 == i[None, :] // 64)
    for m in range(P):
        r = m % 32
        if r < 16:
            cst[m + 16, 3, m] = -1
        else:
            cst[m - 16, 3, m] = 1
        r = m % 64
        if r < 8:
            cst[m + 8, 4, m] = -1
        elif r < 16:
            cst[m - 8, 4, m] = 1
    c["cst"] = cst.reshape(P, -1)
    t = np.arange(T)
    fr = f(10000.0) ** (-np.arange(16, dtype=f) / f(16))
    pos = np.where((i % 64 < 32)[:, None], (t // 64)[None, :], (t % 64)[None, :]).astype(f)
    ang = (pos * fr[i % 16][:, None]).astype(f)
    c["cs0"] = np.concatenate([np.cos(ang), np.sin(ang)], 1).astype(f)
    inv = f(500000.0) ** (-np.arange(0, 16, 2, dtype=f) / f(16))
    ang = (t[None, :].astype(f) * inv[i % 8][:, None]).astype(f)
    rot = (i % 64 < 16)[:, None]
    c["cs1"] = np.concatenate([np.where(rot, np.cos(ang), 1), np.where(rot, np.sin(ang), 0)], 1).astype(f)
    q, k = i[:, None], i[None, :]
    z = np.zeros((P, P))
    c["wm"] = np.concatenate([np.where(k >= q, 0, NEG), z, np.where(k <= q, 0, NEG)], 1).astype(f)

    def mult(off):
        d = q - k + off
        ok = d >= 0
        n = (ok & (d <= 128)).astype(int) + (ok & (d % 4 == 0)) + (ok & (d % 16 == 0))
        return np.where(n > 0, np.log(np.maximum(n, 1)), NEG)
    c["mk"] = np.concatenate([mult(384), mult(256), mult(128), mult(0)], 1).astype(f)
    c["ck"] = np.concatenate([z, z, z, np.where(k <= q, 0, NEG)], 1).astype(f)
    s64, t64 = (i % 64)[:, None], np.arange(64)[None, :]
    c["cz"] = np.concatenate([np.where(k <= q, 0, NEG), np.tile(s64 <= t64, (1, 2)).astype(f), z], 1).astype(f)
    c["scn"] = np.tile((np.arange(TT) % CH != 0).astype(f), (P, 1))
    c["mg"] = np.concatenate([s64 < t64, s64 <= t64, s64 > t64, s64 >= t64], 1).astype(f)
    ml = []
    for d in range(2):
        for lev in range(6):
            n = 1 << lev
            a, b = (s64, t64) if d == 0 else (t64, s64)
            ml.append((a // (2 * n) == b // (2 * n)) & (a // n % 2 == 0) & (b // n % 2 == 1))
    c["ml"] = np.concatenate(ml, 1).astype(f)
    c["e64"] = (s64 == t64).astype(f)
    return {k_: np.ascontiguousarray(v, dtype=f) for k_, v in c.items()}


def _cols(v):
    return np.ascontiguousarray(np.asarray(v).reshape(-1, P).T)


def _fm(a):
    a = np.asarray(a)
    return np.ascontiguousarray(a.T.reshape(a.shape[1] // P, P, a.shape[0]).transpose(1, 0, 2).reshape(P, -1))


def _panel(W):
    K, N = W.shape
    return W.reshape(K // P, P, N).transpose(1, 0, 2).reshape(P, -1)


def lay_out(inp):
    f = np.float32
    g = {k: np.asarray(v) for k, v in inp.items()}
    vec = np.zeros((P, NVEC), f)

    def put(name, a):
        s, n = VCOLS[name]
        vec[:a.shape[0], s:s + n] = a
    for l in range(2):
        put(f"adab{l}", _cols(g["ada_b"][l]))
        put(f"n1{l}", _cols(g["norm1_g"][l]))
        put(f"n2{l}", _cols(g["norm2_g"][l]))
        put(f"ln1g{l}", _cols(g["ln1_g_2"][l]))
        put(f"ln1b{l}", _cols(g["ln1_b_2"][l]))
        put(f"ln2g{l}", _cols(g["ln2_g_2"][l]))
        put(f"ln2b{l}", _cols(g["ln2_b_2"][l]))
        put(f"plg{l}", _cols(g["ple_norm_g_2"][l]))
    put("qg", np.tile(g["att_q_gain"][0], 2)[:, None])
    put("kg", np.tile(g["att_k_gain"][0], 2)[:, None])
    put("sink", np.tile(g["att_sink"][0][None, :], (P, 1)))
    put("mu", _cols(g["rwkv_mu"][0]))
    put("w0", _cols(g["rwkv_w0"][0]))
    put("a0", _cols(g["rwkv_a0"][0]))
    put("kk", _cols(g["rwkv_k_k"][0]))
    put("ka", _cols(g["rwkv_k_a"][0]))
    put("rk", _cols(g["rwkv_r_k"][0]))
    put("gng", _cols(g["rwkv_gn_g"][0]))
    put("gnb", _cols(g["rwkv_gn_b"][0]))
    put("c", np.stack([_cols(g["c"][0]), _cols(g["c_ctx"])], 2).reshape(P, 16))
    put("subg", g["da_subln_g_2"][0][:, None])
    put("hgg", g["hg_norm_g_2"][0][:, None])
    put("lb", _cols(g["hg_lb_logits_2"]))
    put("lam", g["da_lambda_2"][0].T)
    for name, v in (("e6", 1e-6), ("e5", 1e-5), ("egn", 64e-5), ("l10", 10 * np.log(2.0))):
        put(name, np.full((P, 1), v, f))
    qcols = np.concatenate([np.arange(64) + 64 * h for pr in PAIRS for h in pr])
    wqkv = g["att_w_qkv"][0]
    evi, odi = g["ev_w_in_2"][0], g["od_w_in_2"][0]

    def cut(W, j):
        return _panel(W[:, 256 * j:256 * j + 256])

    def one(key):
        if key == "loraA":
            return _panel(np.concatenate([g["rwkv_w1"][0, 0], g["rwkv_w1"][0, 1], g["rwkv_a1"][0],
                                          np.zeros((1024, 64), f)], 1))
        if key == "loraB":
            a = np.zeros((P, 2048), f)
            a[0:64, 0:1024] = g["rwkv_w2"][0, 0]
            a[64:128, 0:1024] = g["rwkv_w2"][0, 1]
            a[0:64, 1024:2048] = g["rwkv_a2"][0]
            return a
        if key == "g1":
            return _panel(np.concatenate([g["rwkv_g1"][0, 0], g["rwkv_g1"][0, 1]], 1))
        if key == "g2":
            return np.concatenate([g["rwkv_g2"][0, 0], g["rwkv_g2"][0, 1]], 1)
        k, j = key[0], key[-1]
        if k == "ada":
            return cut(g["ada_w"][key[1]], j)
        if k == "q":
            return cut(wqkv[:, qcols], j)
        if k == "k":
            return cut(wqkv[:, 1024:], 0)
        if k == "v":
            return cut(wqkv[:, 1280:], 0)
        if k == "wo":
            return cut(g["att_w_o"][0][qcols], j)
        if k in ("m1", "f1"):
            return cut(g["mlp_w1" if k == "m1" else "ffn_w1_2"][key[1]], j)
        if k in ("m2", "f2"):
            w = g["mlp_w2" if k == "m2" else "ffn_w2_2"][key[1]]
            q, c = j // 2, j % 2
            return _panel(w[512 * q:512 * q + 512, 512 * c:512 * c + 512])
        if k in ("r", "kr", "vr"):
            return cut(g["rwkv_w_rkv"][0, ("r", "kr", "vr").index(k)], j)
        if k == "wor":
            return cut(g["rwkv_w_o"][0], j)
        if k in ("qa", "ka", "va", "hq", "hf", "hi", "hg"):
            return cut(evi[:, 512 * ("qa", "ka", "va", "hq", "hf", "hi", "hg").index(k):], j)
        if k == "evo":
            return cut(g["ev_w_out_2"][0], j)
        if k in ("oq", "ok", "ov"):
            return cut(odi[:, 1024 * ("oq", "ok", "ov").index(k):], j)
        if k == "odo":
            return cut(g["od_w_out_2"][0], j)
        if k == "pp":
            return _panel(g["ple_w_proj_2"][key[1]])
        if k == "pg":
            return cut(g["ple_w_gate_2"][key[1]], j)
        raise ValueError(key)

    arrays = dict(constants())
    arrays["vec"] = vec
    arrays["xT"] = _fm(g["x"][0])
    arrays["ctxT"] = _fm(g["ctx"][0])
    arrays["p0"] = _fm(g["p_2"][0, 0])
    arrays["p1"] = _fm(g["p_2"][1, 0])
    return arrays, one


NPANELS = 250


def kernel(**inputs):
    import concourse.bacc as _bacc
    from concourse.bass_utils import run_bass_kernel_spmd as _run

    arrays, one = lay_out(inputs)
    nc = _bacc.Bacc("TRN2", target_bir_lowering=False, num_devices=1)
    dt = mybir.dt.float32
    ins = {}
    for name, a in arrays.items():
        ins[name] = nc.dram_tensor("in_" + name, a.shape, dt, kind="ExternalInput").ap()
    ins["w"] = nc.dram_tensor("in_w", (NPANELS, P, 2048), dt, kind="ExternalInput").ap()
    scratch = {
        "fe": nc.dram_tensor("s_fe", (12, P, 9, 8, CH), dt, kind="Internal").ap(),
        "bon": nc.dram_tensor("s_bon", (P, 8, T), dt, kind="Internal").ap(),
        "ys": nc.dram_tensor("s_ys", (2, 8, P, 8 * CH), dt, kind="Internal").ap(),
    }
    out = nc.dram_tensor("out_0", (P, 8 * T), dt, kind="ExternalOutput").ap()
    order = []
    program(nc, ins, out, scratch, NPANELS, order)
    assert len(order) == NPANELS, len(order)
    arrays["w"] = np.stack([one(k) for k in order])
    r = _run(nc, [{("in_" + k): v for k, v in arrays.items()}], core_ids=[0])
    got = r.results[0]["out_0"]
    return np.ascontiguousarray(got.reshape(P, 8, T).transpose(2, 1, 0).reshape(1, T, 1024))
```

```python
from contextlib import ExitStack

import numpy as np

import concourse.bass as bass
from concourse import mybir

P = 128
F32 = mybir.dt.float32
F32R = mybir.dt.float32r
ALU = mybir.AluOpType
ACT = mybir.ActivationFunctionType
AX = mybir.AxisListType
T = 512
TC = 256
TT = T + TC
CH = 64
RING = 3
NEG = -1e30
ALPHA = 4 ** 0.25

PAIRS = [(0, 4), (1, 5), (2, 6), (3, 7), (8, 12), (9, 13), (10, 14), (11, 15)]

VCOLS = {}


def _vec_layout():
    at = 0
    for name, n in [("adab0", 48), ("adab1", 48), ("n10", 8), ("n11", 8), ("n20", 8), ("n21", 8),
                    ("qg", 1), ("kg", 1), ("sink", 16), ("mu", 48), ("w0", 16), ("a0", 8), ("kk", 8),
                    ("ka", 8), ("rk", 8), ("gng", 8), ("gnb", 8), ("c", 16),
                    ("ln1g0", 8), ("ln1b0", 8), ("ln2g0", 8), ("ln2b0", 8), ("plg0", 8),
                    ("ln1g1", 8), ("ln1b1", 8), ("ln2g1", 8), ("ln2b1", 8), ("plg1", 8),
                    ("subg", 1), ("hgg", 1), ("lb", 8), ("lam", 4), ("e6", 1), ("e5", 1), ("egn", 1),
                    ("l10", 1)]:
        VCOLS[name] = (at, n)
        at += n
    return at


NVEC = _vec_layout()


class Engine:

    def __init__(self, name, sem):
        self.name, self.sem, self.count, self.items, self.seen = name, sem, 0, [], {}

    def wait(self, toks):
        need = {}
        flat = [toks]
        while flat:
            t = flat.pop()
            if t is None:
                continue
            if isinstance(t, list) or not _is_tok(t):
                flat += list(t)
                continue
            sem, v, key = t
            if v > self.seen.get(key, 0) and v > need.get(key, (None, 0))[1]:
                need[key] = (sem, v)
        for key, (sem, v) in need.items():
            self.seen[key] = v
            self.items.append((None, sem, v))

    def do(self, w, f, s=True):
        self.wait([w])
        if s:
            self.count += 1
            self.items.append((f, self.sem, 1))
            return (self.sem, self.count, self.name)
        self.items.append((f, None, 0))
        return None

    def last(self):
        return (self.sem, self.count, self.name) if self.count else None

    def emit(self, eng):
        for f, sem, v in self.items:
            if f is None:
                eng.wait_ge(sem, v)
            else:
                ins = f(eng)
                if sem is not None:
                    ins.then_inc(sem, v)


def _is_tok(t):
    return isinstance(t, tuple) and len(t) == 3 and isinstance(t[2], str)


def program(nc, ins, out_d, scratch, npanels, order):
    ctx = ExitStack()
    uid = [0]

    def alloc(stack, shape, dt=F32):
        uid[0] += 1
        return stack.enter_context(nc.sbuf_tensor(f"t{uid[0]}", shape, dt))

    def new_sem(name):
        return ctx.enter_context(nc.semaphore(name))

    PE = Engine("pe", new_sem("s_pe"))
    DV = Engine("dv", new_sem("s_dv"))
    AC = Engine("ac", new_sem("s_ac"))
    PO = Engine("po", new_sem("s_po"))
    SP = Engine("sp", None)
    dmas = {}

    def dma(q, name, dst, src, w=()):
        if name not in dmas:
            dmas[name] = [new_sem("d_" + name), 0]
        d = dmas[name]
        q.wait(list(w))
        d[1] += 16
        sem = d[0]
        q.items.append((lambda e: e.dma_start(dst, src), sem, 16))
        return (sem, d[1], "d_" + name)


    def mm(out, lhsT, rhs, start=True, stop=True, w=(), s=False):
        return PE.do(w, lambda e: e.matmul(out, lhsT, rhs, start=start, stop=stop), s)

    def tr(out, in_, ident, w=(), s=False):
        return PE.do(w, lambda e: e.transpose(out, in_, ident), s)

    def tt(out, a, b, op, w=(), E=None):
        if E is PO:
            w = [w, PO.last()]
        return (E or DV).do(w, lambda e: e.tensor_tensor(out, a, b, op))

    def ts(out, a, s1, s2, op0, op1=None, w=(), E=None):
        if op1 is None:
            return (E or DV).do(w, lambda e: e.tensor_scalar(out, a, s1, None, op0))
        return (E or DV).do(w, lambda e: e.tensor_scalar(out, a, s1, s2, op0, op1))

    def stt(out, a, sc, b, op0, op1, w=()):
        return DV.do(w, lambda e: e.scalar_tensor_tensor(out=out, in0=a, scalar=sc, in1=b, op0=op0, op1=op1))

    def act(out, a, f, w=(), **k):
        return AC.do(w, lambda e: e.activation(out, a, f, **k))

    def cp(E, out, a, w=()):
        if E is AC:
            return act(out, a, ACT.Copy, w)
        if E is PO:
            w = [w, PO.last()]
        return E.do(w, lambda e: e.tensor_copy(out, a))

    def recip(out, a, w=()):
        return DV.do(w, lambda e: e.reciprocal(out, a))

    def rmax(out, a, w=()):
        return DV.do(w, lambda e: e.tensor_reduce(out, a, AX.X, ALU.max))

    MUL, ADD, SUB, MAX, MIN = ALU.mult, ALU.add, ALU.subtract, ALU.max, ALU.min

    banks = [ctx.enter_context(nc.psum_tensor(f"ps{i}", [P, 512], F32)) for i in range(8)]
    bfree = [None] * 8
    bturn = [0]

    def bank():
        i = bturn[0] % 8
        bturn[0] += 1
        return i, banks[i], bfree[i]


    def fence():
        toks = [e.last() for e in (PE, DV, AC, PO)]
        for e in (PE, DV, AC, PO, SP):
            e.wait(list(toks))
        return toks

    CST = alloc(ctx, [P, 5, P])
    VEC = alloc(ctx, [P, NVEC])
    X = alloc(ctx, [P, 8, T])
    RW = [alloc(ctx, [P, 2048]) for _ in range(RING)]
    ADA = alloc(ctx, [P, 2, 6, 8, 2])
    MOD = alloc(ctx, [P, 2, 2, 8, 2])
    SC = alloc(ctx, [P, 8, 2])
    SM = alloc(ctx, [P, 64])
    AROW = [alloc(ctx, [2, 256]) for _ in range(2)]
    arow = [0]
    ID, ONES, BONES = CST[:, 0, :], CST[:, 1, :], CST[:, 2, :]
    PERM = [CST[:, 3, :], CST[:, 4, :]]

    def vec(name, i=0, n=1, rows=slice(0, P)):
        a = VCOLS[name][0] + i
        return VEC[rows, a:a + n]

    d_cst = [dma(AC, "c0", CST[:, :, :], ins["cst"].rearrange("p (a b) -> p a b", a=5)),
             dma(AC, "c1", VEC[:, :], ins["vec"])]
    d_x = dma(AC, "x", X[:, :, :], ins["xT"].rearrange("p (k t) -> p k t", k=8))
    for e in (PE, DV, AC, PO):
        e.wait(d_cst)

    wp = ins["w"]
    rfree = {}
    issued = [0]
    wtok = {}

    def issue():
        while issued[0] < npanels and (issued[0] < RING or issued[0] - RING in rfree):
            n = issued[0]
            wtok[n] = dma(SP, f"w{n % RING}", RW[n % RING][:, :], wp[n], [rfree.get(n - RING)])
            issued[0] += 1

    issue()
    used = [0]

    def panel(key):
        n = used[0]
        used[0] += 1
        order.append(key)
        assert n in wtok, key
        return n, RW[n % RING], wtok[n]

    def release(n, tok):
        rfree[n] = tok
        issue()

    WS = {"bufs": None, "free": None, "turn": 0}
    plan = []
    ready = []
    open_panel = {}

    def splits_begin(st, n=3):
        WS["bufs"] = [(alloc(st, [P, 8, P], F32R), alloc(st, [P, 8, P], F32R)) for _ in range(n)]
        WS["free"] = [None] * n
        WS["turn"] = 0

    def will_use(keys, kc=8):
        nm = 16 // kc
        for key in keys:
            for m in range(nm):
                plan.append((key, kc, m, nm))
        ahead()

    def ahead():
        while plan and len(ready) < len(WS["bufs"]) - 1:
            key, kc, m, nm = plan.pop(0)
            if m == 0:
                open_panel["n"], open_panel["W"], open_panel["t"] = panel(key)
            W = open_panel["W"][:, :].rearrange("p (k n) -> p k n", k=kc)[:, :, m * P:m * P + P]
            i = WS["turn"] % len(WS["bufs"])
            WS["turn"] += 1
            hi, lo = WS["bufs"][i]
            a = act(hi[:, 0:kc, :], W, ACT.Copy, [open_panel["t"], WS["free"][i]])
            b = tt(lo[:, 0:kc, :], W, hi[:, 0:kc, :].bitcast(F32), SUB, [a])
            if m == nm - 1:
                release(open_panel["n"], b)
            ready.append((i, hi, lo, b))

    def unit_of(kc):
        ahead()
        u = ready.pop(0)
        ahead()
        return u

    def unit_done(i, tok):
        WS["free"][i] = tok
        ahead()

    def mm3(out, whi, wlo, xhi, xlo, start, stop, w=(), s=False):
        mm(out, whi, xhi, start, False, w)
        mm(out, wlo, xhi, False, False)
        return mm(out, whi, xlo, False, stop, (), s)

    deferred = []

    def run_deferred():
        now = deferred[:]
        deferred.clear()
        for f in now:
            f()

    def interleave(gens, width):
        gens, live = list(gens), []
        while gens or live:
            while gens and len(live) < width:
                live.append(gens.pop(0))
            for g in list(live):
                if next(g, "end") == "end":
                    live.remove(g)

    live = []

    def attend(g):
        next(g)
        if len(live) == 2:
            next(live.pop(0), None)
        if live:
            next(live[-1])
        live.append(g)

    def attend_end():
        next(live.pop(0), None)
        next(live[0])
        next(live.pop(0), None)

    def gemm3(nunits, kc, src, segs, evac, w=(), tick=None, ready=None, free=None, every=1):
        for m in range(nunits):
            i, hi, lo, wt = unit_of(kc)
            tok = None
            for sg in segs:
                bi, B, fr = bank()
                for k in range(kc):
                    xh, xl = src(k, sg)
                    if ready is not None and m == 0:
                        PE.wait([ready[k]])
                    last = free is not None and m == nunits - 1
                    tok = mm3(B[:, 0:sg[1]], hi[:, k, :], lo[:, k, :], xh, xl, k == 0, k == kc - 1,
                              [wt, fr, list(w)] if k == 0 else (), k == kc - 1 or last)
                    if last:
                        free[k] = tok
                run_deferred()
                bfree[bi] = evac(m, sg, B[:, 0:sg[1]], tok)
            unit_done(i, tok)
            if tick and m % 2 >= 2 - every:
                tick()
        while deferred:
            run_deferred()

    def gemm3_tok(nunits, src, segs, dst, st, w=()):
        VT_ = [alloc(st, [P, T]) for _ in range(2)]
        vf = [None, None]
        n_ = [0]
        later = []

        def turn(v, m, sg, t0, i):
            bi, B, fr = bank()
            cnt = sg[1] // P
            for b in range(cnt):
                t = tr(B[:, b * P:b * P + P], v[:, b * P:b * P + P], ID, [fr, t0], b == cnt - 1)
            vf[i] = t
            bfree[bi] = cp(DV, dst[:, sg[0] // P:sg[0] // P + cnt, m * P:m * P + P],
                           B[:, 0:sg[1]].rearrange("p (a b) -> p a b", b=P), [t])

        def ev(m, sg, B, tok):
            i = n_[0] % 2
            n_[0] += 1
            t = cp(AC, VT_[i][:, 0:sg[1]], B, [tok, vf[i]])
            if later:
                turn(*later.pop())
            later.append((VT_[i], m, sg, t, i))
            return t
        gemm3(nunits, 8, src, segs, ev, w)
        turn(*later.pop())

    def gemm(keys, src, segs, evac, w=(), tick=None):
        for pi, key in enumerate(keys):
            s, W, wt = panel(key)
            tok = None
            for m in range(2):
                for sg in segs:
                    bi, B, fr = bank()
                    for k in range(8):
                        tok = mm(B[:, 0:sg[1]], W[:, k * 256 + m * P:k * 256 + m * P + P], src(k, sg),
                                 k == 0, k == 7, [wt, fr, list(w)] if k == 0 else (), k == 7)
                    bfree[bi] = evac(pi * 2 + m, sg, B[:, 0:sg[1]], tok)
            release(s, tok)
            if tick:
                tick()

    def split(hi, lo, a, w=()):
        t = act(hi, a, ACT.Copy, w)
        return tt(lo, a, hi.bitcast(F32), SUB, [t])

    def rstd(out, B, scale, eps, w):
        t = act(out, B, ACT.Ln, w, scale=scale, bias=vec(eps))
        return t, act(out, out, ACT.Exp, [t], scale=-0.5)

    MAIN, CTX = (0, T, 0), (T, TC, 1)

    e0 = act(SC[:, :, :], vec("c", 0, 16).rearrange("p (k c) -> p k c", c=2), ACT.Exp, scale=-1.0)
    e1 = ts(SC[:, :, :], SC[:, :, :], 1.0, None, ADD, w=[e0])
    e2 = recip(SC[:, :, :], SC[:, :, :], [e1])
    t_sc = tt(SC[:, :, :], SC[:, :, :], vec("c", 0, 16).rearrange("p (k c) -> p k c", c=2), MUL, [e2])

    def ada(layer, parts):
        for part in parts:
            tok = None
            for pj in range(4):
                s, W, wt = panel(("ada", layer, part * 4 + pj))
                bi, B, fr = bank()
                for k in range(8):
                    t = mm(B[0:2, 0:256], SC[:, k, :], W[:, k * 256:k * 256 + 256], k == 0, k == 7, [wt, fr, t_sc],
                           k == 7)
                release(s, t)
                r_ = AROW[arow[0] % 2]
                arow[0] += 1
                bfree[bi] = t1 = act(r_[:, :], B[0:2, 0:256], ACT.Copy, [t])
                yield
                bi, B, fr = bank()
                for m in range(2):
                    t = tr(B[:, 2 * m:2 * m + 2], r_[:, m * P:m * P + P], ID[0:2, 0:2], [t1, fr], m == 1)
                a = VCOLS[f"adab{layer}"][0] + part * 8 + pj * 2
                bfree[bi] = tok = tt(ADA[:, layer, part, pj * 2:pj * 2 + 2, :],
                                     B[:, 0:4].rearrange("p (a b) -> p a b", b=2),
                                     VEC[:, a:a + 2].unsqueeze(2).broadcast_to([P, 2, 2]), ADD, [t])
            if part in (1, 4):
                which = 0 if part == 1 else 1
                g = vec(f"n{which + 1}{layer}", 0, 8).unsqueeze(2).broadcast_to([P, 8, 2])
                tok = ts(MOD[:, layer, which, :, :], ADA[:, layer, part, :, :], 1.0, None, ADD, w=[tok])
                tok = tt(MOD[:, layer, which, :, :], MOD[:, layer, which, :, :], g, MUL, [tok])
                for e in (AC, DV):
                    e.wait([tok])

    def run(g):
        for _ in g:
            pass

    def rms_mod(srcf, HH, HL, segs, layer, which, st, w=()):
        outs = []
        AC.wait([DV.last()])
        Q = [alloc(st, [P, T]) for _ in range(4)]
        qf = [None] * 4
        later = []
        R = alloc(st, [P, T])
        n_ = 0
        for sg in segs:
            o, n, c = sg
            bi, B, fr = bank()
            for k in range(8):
                i = n_ % 4
                n_ += 1
                t = act(Q[i][:, 0:n], srcf(k, sg), ACT.Square, [list(w), qf[i]])
                qf[i] = t = mm(B[:, 0:n], ONES, Q[i][:, 0:n], k == 0, k == 7, [t, fr], True)
            t1, t2 = rstd(R[:, 0:n], B[:, 0:n], 1.0 / 1024, "e6", [t, outs])
            bfree[bi] = t1
            for k in range(10):
                if k < 8:
                    i = n_ % 4
                    n_ += 1
                    t3 = tt(Q[i][:, 0:n], srcf(k, sg), R[:, 0:n], MUL, [t2, qf[i]])
                    t4 = act(Q[i][:, 0:n], Q[i][:, 0:n], ACT.Identity, [t3],
                             scale=MOD[:, layer, which, k, c:c + 1], bias=ADA[:, layer, 3 * which, k, c:c + 1])
                    later.append((i, k, act(HH[:, k, o:o + n], Q[i][:, 0:n], ACT.Copy, [t4])))
                if k > 1:
                    i1, k1, th = later.pop(0)
                    qf[i1] = tt(HL[:, k1, o:o + n], Q[i1][:, 0:n], HH[:, k1, o:o + n].bitcast(F32), SUB, [th])
            outs = [t3, qf[i1]]
        return outs

    def mlp_keys(a, b, layer):
        k1 = lambda q: ([(a, layer, 2 * q + j) for j in range(2)], 8)
        k2 = lambda q: ([(b, layer, 2 * q + j) for j in range(2)], 4)
        seq = [k1(0)]
        for q in range(8):
            if q < 7:
                seq.append(k1(q + 1))
            seq.append(k2(q))
        return seq

    def mlp(srcf, segs, st, seq, HH, HL, gate, tick=None, alpha=None, w=()):
        n_all = sum(s[1] for s in segs)
        HD = [(alloc(st, [P, 4, n_all], F32R), alloc(st, [P, 4, n_all], F32R)) for _ in range(2)]
        R = [alloc(st, [P, T]) for _ in range(2)]
        rfr = [None, None]
        hfr = [None, None]
        xt = {}
        cnt = [0]
        hts = {}
        for keys, kc in seq:
            for key in keys:
                will_use([key], kc)

        def first(q):
            DH, DL = HD[q % 2]
            hts[q] = []

            def ev1(m, sg, B, tok):
                i = cnt[0] % 2
                cnt[0] += 1
                r = R[i][:, 0:sg[1]]
                t = act(r, B, ACT.Relu, [tok, rfr[i]])
                t2 = tt(r, r, r, MUL, [t])
                rfr[i] = split(DH[:, m, sg[0]:sg[0] + sg[1]], DL[:, m, sg[0]:sg[0] + sg[1]], r, [t2, hfr[q % 2]])
                hts[q].append(rfr[i])
                return t
            gemm3(4, 8, lambda k, sg: (HH[:, k, sg[0]:sg[0] + sg[1]], HL[:, k, sg[0]:sg[0] + sg[1]]), segs, ev1, w,
                  tick)

        def second(q):
            DH, DL = HD[q % 2]

            def ev2(m, sg, B, tok):
                dst = srcf(m, sg)
                key = (m, sg[2])
                pre = xt.get(key)
                if alpha is not None and q == 0:
                    t = stt(dst, dst, alpha, B, MUL, ADD, [tok, pre])
                elif gate is None:
                    t = tt(dst, B, dst, ADD, [tok, pre])
                else:
                    t = stt(dst, B, gate(m, sg), dst, MUL, ADD, [tok, pre])
                xt[key] = t
                return t
            gemm3(8, 4, lambda k, sg: (DH[:, k, sg[0]:sg[0] + sg[1]], DL[:, k, sg[0]:sg[0] + sg[1]]), segs, ev2,
                  [hts[q]], tick)
            hfr[q % 2] = PE.last()

        first(0)
        for q in range(8):
            if q < 7:
                first(q + 1)
            second(q)

    stS = ExitStack()
    SG = alloc(stS, [P, 2, T])
    stC = ExitStack()
    CR = alloc(stC, [P, 8, TC])
    d_c = dma(AC, "x", CR[:, :, :], ins["ctxT"].rearrange("p (k t) -> p k t", k=8))
    for e in (DV, AC):
        e.wait([d_x, d_c])

    def res(k, sg):
        return X[:, k, :] if sg[2] == 0 else CR[:, k, :]

    run(ada(0, [0, 1]))
    st = ExitStack()
    KT = alloc(st, [P, 2, TT])
    VT = alloc(st, [P, 6, 256])
    QT = alloc(st, [P, 8, TT])
    CS = alloc(st, [P, 2, T])
    WM = alloc(st, [P, 3, P])
    d_cs = [dma(AC, "cs", CS[:, :, :], ins["cs0"].rearrange("p (a t) -> p a t", a=2)),
            dma(AC, "cs", WM[:, :, :], ins["wm"].rearrange("p (a t) -> p a t", a=3))]
    DV.wait(d_cs)
    st2 = ExitStack()
    splits_begin(st2)
    will_use([("q", j) for j in range(4)] + [("k", 0), ("v", 0)])
    HH, HL = alloc(st2, [P, 8, TT], F32R), alloc(st2, [P, 8, TT], F32R)
    st3 = ExitStack()
    hh = rms_mod(res, HH, HL, [MAIN, CTX], 0, 0, st3)
    fence()
    st3.close()
    SQ = [alloc(st2, [P, T]) for _ in range(2)]
    QR = [alloc(st2, [P, T]) for _ in range(2)]
    RR = [alloc(st2, [P, T]) for _ in range(2)]
    turn = [0]
    busy = [[None], [None]]

    def qk_evac(dst, gain):
        def f(m, sg, B, tok):
            i = turn[0] % 2
            turn[0] += 1
            o, n, c = sg
            q, sq, rr = QR[i][:, 0:n], SQ[i][:, 0:n], RR[i][:, 0:n]
            t0 = act(q, B, ACT.Copy, [tok] + busy[i])
            t1 = act(sq, q, ACT.Square, [t0])

            def norm():
                bi, S, fr = bank()
                t2 = mm(S[:, 0:n], BONES, sq, True, True, [t1, fr], True)
                t3, t4 = rstd(rr, S[:, 0:n], 1.0 / 64, "e6", [t2])
                bfree[bi] = t3
                d = dst[:, m, o:o + n]
                if c:
                    busy[i] = [stt(d, q, vec(gain), rr, MUL, MUL, [t4])]
                    return
                t5 = stt(q, q, vec(gain), rr, MUL, MUL, [t4])
                deferred.append(lambda: rope(d, t5))

            def rope(d, t5):
                bi, S, fr = bank()
                t6 = mm(S[:, 0:n], PERM[0], q, True, True, [t5, fr], True)
                t7 = tt(d, q, CS[:, 0, :], MUL, [t5])
                t8 = tt(sq, S[:, 0:n], CS[:, 1, :], MUL, [t6])
                bfree[bi] = t8
                t9 = tt(d, d, sq, ADD, [t7, t8])
                busy[i] = [t9, t6]

            deferred.append(norm)
            return t0
        return f

    hsrc = lambda k, sg: (HH[:, k, sg[0]:sg[0] + sg[1]], HL[:, k, sg[0]:sg[0] + sg[1]])
    gemm3(8, 8, hsrc, [MAIN, CTX], qk_evac(QT, "qg"), hh)
    gemm3(2, 8, hsrc, [MAIN, CTX], qk_evac(KT, "kg"), hh)
    gemm3_tok(2, hsrc, [MAIN, CTX], VT, st2, hh)
    fence()
    st2.close()
    O = alloc(st, [P, 8, TT])
    stA = ExitStack()
    S4 = [alloc(stA, [P, 4, 640]) for _ in range(3)]
    PT = [alloc(stA, [P, 5, 512]) for _ in range(2)]
    sfree = [None] * 3
    pfree = [None, None]
    ada_rest = ada(0, [2, 3, 4, 5])
    un = [0]
    NSM = alloc(stA, [P, 3, 4, 8])

    def att_unit(g, q0, blocks, masks):
        u, v = un[0] % 3, un[0] % 2
        un[0] += 1
        S, PTu, nb, half, sm = S4[u], PT[v], len(blocks), g % 2, NSM[:, u, :, :]
        rows = slice(64 * half, 64 * half + 64)
        runs = []
        for i, b in enumerate(blocks):
            if runs and runs[-1][1] + runs[-1][2] == b and b != 4:
                runs[-1][2] += 1
            else:
                runs.append([i, b, 1])
        ev = []
        for i in range(4):
            tile = 4 * (g // 2) + i
            for (i0, b0, cnt) in runs:
                bi, B, fr = bank()
                t = mm(B[:, 0:cnt * P], QT[rows, tile, q0:q0 + P], KT[rows, g // 2, b0 * P:(b0 + cnt) * P],
                       True, True, [fr], True)
                if b0 >= 4:
                    r = act(S[:, i, i0 * P:(i0 + cnt) * P], B[:, 0:cnt * P], ACT.Copy, [t, sfree[u]], scale=0.125)
                else:
                    r = stt(S[:, i, i0 * P:(i0 + cnt) * P], B[:, 0:cnt * P], 0.125,
                            WM[:, masks:masks + cnt, :].rearrange("p a b -> p (a b)"), MUL, ADD, [t, sfree[u]])
                bfree[bi] = r
                ev.append(r)
        mx, ng, dn, es = sm[:, :, 0], sm[:, :, 1], sm[:, :, 2], sm[:, :, 3]
        t = rmax(mx, S[:, :, 0:nb * P], ev)
        sk = VCOLS["sink"][0] + 4 * g
        t = tt(ng, mx, VEC[:, sk:sk + 4], MAX, [t])
        t = ts(ng, ng, -1.0, None, MUL, w=[t])
        yield
        ee = []
        for i in range(4):
            ee.append(act(S[:, i, 0:nb * P], S[:, i, 0:nb * P], ACT.Exp, [t], bias=ng[:, i:i + 1],
                          accum_out=dn[:, i:i + 1]))
        t = tt(es, ng, VEC[:, sk:sk + 4], ADD, [t])
        t = act(es, es, ACT.Exp, [t])
        t = tt(dn, dn, es, ADD, [t, ee])
        t = recip(dn, dn, [t])
        pn = [ts(S[:, i, 0:nb * P], S[:, i, 0:nb * P], dn[:, i:i + 1], None, MUL, w=[t]) for i in range(4)]

        yield
        pts = []
        for b in range(nb):
            bi, B, fr = bank()
            for i in range(4):
                t = tr(B[:, i * P:i * P + P], S[:, i, b * P:b * P + P], ID, [fr, pn], i == 3)
            E = (AC, DV)[b % 2]
            r = cp(E, PTu[:, b, :], B[:, :], [t, pfree[v]])
            bfree[bi] = r
            pts.append(r)
        sfree[u] = PE.last()
        bi, B, fr = bank()
        for b in range(nb):
            t = mm(B[rows, :], VT[:, blocks[b], 64 * g:64 * g + 64], PTu[:, b, :], b == 0, b == nb - 1,
                   [fr, pts[b]], b == nb - 1)
        pfree[v] = t
        bfree[bi] = cp(DV, O[rows, 4 * (g // 2):4 * (g // 2) + 4, q0:q0 + P],
                       B[rows, :].rearrange("p (a b) -> p a b", a=4), [t])

    for qb in range(6):
        for g in range(4):
            if qb < 4:
                blk = [b for b in (qb - 1, qb, qb + 1) if 0 <= b < 4]
                attend(att_unit(g, qb * P, blk + [4, 5], 1 if qb == 0 else 0))
            else:
                attend(att_unit(g, qb * P, [4, 5], 0))
            next(ada_rest, None)
    attend_end()
    run(ada_rest)
    fence()
    stA.close()
    splits_begin(st)
    will_use([("wo", j) for j in range(4)])
    OH, OL = alloc(st, [P, 8, TT], F32R), alloc(st, [P, 8, TT], F32R)
    for k in range(8):
        t_o = split(OH[:, k, :], OL[:, k, :], O[:, k, :])

    def resid(layer, part):
        def f(m, sg, B, tok):
            d = res(m, sg)
            return stt(d, B, ADA[:, layer, part, m, sg[2]:sg[2] + 1], d, MUL, ADD, [tok])
        return f

    gemm3(8, 8, lambda k, sg: (OH[:, k, sg[0]:sg[0] + sg[1]], OL[:, k, sg[0]:sg[0] + sg[1]]), [MAIN, CTX],
          resid(0, 2), [t_o])
    fence()
    st.close()

    st = ExitStack()
    ada1 = ada(1, range(6))
    splits_begin(st)
    HH, HL = alloc(st, [P, 8, TT], F32R), alloc(st, [P, 8, TT], F32R)
    st3 = ExitStack()
    hh = rms_mod(res, HH, HL, [MAIN, CTX], 0, 1, st3)
    fence()
    st3.close()
    mlp(res, [MAIN, CTX], st, mlp_keys("m1", "m2", 0), HH, HL,
        lambda m, sg: ADA[:, 0, 5, m, sg[2]:sg[2] + 1], lambda: next(ada1, None), None, hh)
    run(ada1)
    fence()
    st.close()

    FE = scratch["fe"]
    BON = scratch["bon"]
    YS = scratch["ys"]

    def fe_store(name, idx, tile_ap, m, seg, w):
        o, n, c = seg
        c0, cn = o // CH, n // CH
        dst = FE[c0:c0 + cn, :, idx, m, :].rearrange("c p t -> p c t")
        return dma(SP, "fe" + name, dst, tile_ap.rearrange("p (c t) -> p c t", t=CH), w)

    st = ExitStack()
    splits_begin(st, 2)
    will_use(["loraA", "g1"] + [("r", j) for j in range(4)] + [("kr", j) for j in range(4)] + [("vr", j) for j in range(4)])
    H = alloc(st, [P, 8, TT])
    XX = alloc(st, [P, 8, TT])
    XMH, XML = alloc(st, [P, 8, TT], F32R), alloc(st, [P, 8, TT], F32R)
    BS = alloc(st, [P, 8, T])
    stR = ExitStack()
    rs = alloc(stR, [P, T])
    outs = []
    AC.wait([DV.last()])
    for sg in (MAIN, CTX):
        o, n, c = sg
        R = rs[:, 0:n]
        bi, B, fr = bank()
        for k in range(8):
            t = act(H[:, k, o:o + n], res(k, sg), ACT.Square)
            t = mm(B[:, 0:n], ONES, H[:, k, o:o + n], k == 0, k == 7, [t, fr], True)
        t1, t2 = rstd(R, B[:, 0:n], 1.0 / 1024, "e6", [t, outs])
        bfree[bi] = t1
        for k in range(8):
            t3 = tt(H[:, k, o:o + n], res(k, sg), R, MUL, [t2])
            t4 = act(H[:, k, o:o + n], H[:, k, o:o + n], ACT.Identity, [t3],
                     scale=MOD[:, 1, 0, k, c:c + 1], bias=ADA[:, 1, 0, k, c:c + 1])
        outs += [t3, t4]
    for sg in (MAIN, CTX):
        o, n, c = sg
        e = o + n
        t = tt(XX[:, :, o + 1:e - 1], H[:, :, o:e - 2], H[:, :, o + 2:e], ADD, [outs])
        a = cp(DV, XX[:, :, o:o + 1], H[:, :, o + 1:o + 2])
        b = cp(DV, XX[:, :, e - 1:e], H[:, :, e - 2:e - 1])
        t = stt(XX[:, :, o:e], XX[:, :, o:e], 0.5, H[:, :, o:e], MUL, SUB, [t, a, b])
    t_xx = t
    fence()
    stR.close()
    XD = YS[0].rearrange("c p t -> p c t")
    spill = dma(SP, "x", XD, X[:, :, :])
    TM = [X[:, i, :] for i in range(8)]
    TM += [CR[:, 2 * i:2 * i + 2, :].rearrange("p a b -> p (a b)") for i in range(4)]
    SCN = alloc(st, [P, T])
    MX = [alloc(st, [P, TT]) for _ in range(2)]
    mxf = [None, None]
    xready, xfree = [None] * 8, [None] * 8

    def mix(m, segs):
        a, e = segs[0][0], segs[-1][0] + segs[-1][1]
        for k in range(9):
            if k < 8:
                x = MX[k % 2][:, a:e]
                t = stt(x, XX[:, k, a:e], vec("mu", m * 8 + k), H[:, k, a:e], MUL, ADD, [t_xx, mxf[k % 2]])
                th = act(XMH[:, k, a:e], x, ACT.Copy, [t, xfree[k]])
            if k:
                mxf[(k - 1) % 2] = xready[k - 1] = tt(XML[:, k - 1, a:e], px, XMH[:, k - 1, a:e].bitcast(F32), SUB, [pth])
            px, pth = x, th

    xsrc = lambda k, sg: (XMH[:, k, sg[0]:sg[0] + sg[1]], XML[:, k, sg[0]:sg[0] + sg[1]])
    BOTH = [MAIN, CTX]
    LR = [alloc(st, [P, TT]), alloc(st, [64, TT])]
    A2 = alloc(st, [64, 1024])
    AT = alloc(st, [P, T])
    NB = alloc(st, [P, 24])
    DV.wait([dma(AC, "cs", SCN[:, :], ins["scn"][:, 0:T])])
    a = VCOLS["w0"][0]
    tnb = cp(DV, NB[:, 0:24], VEC[:, a:a + 24])
    lr = {}

    def ev_w(m, sg, B, tok):
        lr["w", sg[2]] = t = act(LR[0][:, sg[0]:sg[0] + sg[1]], B, ACT.Tanh, [tok])
        return t

    def ev_a(m, sg, B, tok):
        lr["a", sg[2]] = t = cp(AC, LR[1][:, sg[0]:sg[0] + sg[1]], B[0:64, :], [tok])
        return t

    def ev_g(m, sg, B, tok):
        return act(SG[:, m, :], B, ACT.Sigmoid, [tok])

    mix(1, BOTH)
    gemm3(1, 8, xsrc, BOTH, ev_w, (), None, xready, xfree)
    mix(4, BOTH)
    gemm3(1, 8, xsrc, BOTH, ev_a, (), None, xready, xfree)
    mix(5, [MAIN])
    gemm3(2, 8, xsrc, [MAIN], ev_g, (), None, xready, xfree)
    sB, WB, wtB = panel("loraB")
    tA2 = cp(AC, A2[:, :], WB[0:64, 1024:2048], [wtB])
    for h in range(2):
        tW2 = cp(AC, TM[10 + h], WB[:, h * T:h * T + T], [wtB])
    release(sB, tW2)
    tfree = [spill] * 8 + [None] * 4

    def decays():
        q = 0
        for d in range(2):
            rows = slice(64 * d, 64 * d + 64)
            for m in range(8):
                for sg in BOTH:
                    o, n, c = sg
                    i = q % 5
                    q += 1
                    L, C = TM[2 * i][:, 0:n], TM[2 * i + 1][:, 0:n]
                    bi, B, fr = bank()
                    t = mm(B[:, 0:n], TM[10 + m // 4][rows, m % 4 * P:m % 4 * P + P], LR[0][rows, o:o + n], True, True,
                           [tW2, fr, lr["w", c]], True)
                    bfree[bi] = t2 = act(L, B[:, 0:n], ACT.Sigmoid, [t, tfree[2 * i], tnb],
                                         bias=NB[:, 8 * d + m:8 * d + m + 1])
                    t3 = act(L, L, ACT.Copy, [t2], scale=-float(np.exp(-0.5)))
                    sc = SCN[:, 0:n]
                    t4 = DV.do([t3, tfree[2 * i + 1]], lambda e, sc=sc, L=L, C=C: e.tensor_tensor_scan(
                        C, sc, L, 0.0, MUL, ADD))
                    tfree[2 * i] = [fe_store(f"t{2 * i}", 1 if d == 0 else 8, L, m, sg, [t3]), t4]
                    tfree[2 * i + 1] = [fe_store(f"t{2 * i + 1}", 0 if d == 0 else 7, C, m, sg, [t4])]
                    yield
    dec = decays()

    def some(n_):
        def f():
            for _ in range(n_):
                next(dec, None)
        return f

    rts = []

    def ev_r(m, sg, B, tok):
        t = cp(AC, BS[:, m, :], B, [tok])
        rts.append(t)
        rts.append(fe_store("r", 2, BS[:, m, :], m, sg, [t]))
        return t
    mix(0, [MAIN])
    gemm3(8, 8, xsrc, [MAIN], ev_r, (), some(4), xready, xfree, 2)
    run(dec)
    tfree[10] = tfree[11] = [PE.last()]
    mix(2, BOTH)
    kb = [0]
    atf = [None]

    def ev_k(m, sg, B, tok):
        o, n, c = sg
        s0 = 4 * (kb[0] % 3)
        kb[0] += 1
        k, kk, b, nr = [TM[s0 + x][:, 0:n] for x in range(4)]
        t0 = act(k, B, ACT.Copy, [tok, tfree[s0]])
        t1 = ts(kk, k, vec("kk", m), None, MUL, w=[t0, tfree[s0 + 1]])
        t2 = act(nr, kk, ACT.Square, [t1, tfree[s0 + 3]])

        def norm():
            bi, S, fr = bank()
            t3 = mm(S[:, 0:n], BONES, nr, True, True, [t2, fr], True)
            bj, S2_, fr2 = bank()
            ta = mm(S2_[:, 0:n], A2[:, m * P:m * P + P], LR[1][:, o:o + n], True, True, [fr2, tA2, lr["a", c]], True)
            t4 = ts(nr, S[:, 0:n], 1e-24, 2.0 ** 20, MAX, MUL, w=[t3])
            bfree[bi] = t4
            deferred.append(lambda: rest(bj, S2_, ta, t4))

        def rest(bj, S2_, ta, t4):
            bfree[bj] = ta = act(AT[:, 0:n], S2_[:, 0:n], ACT.Sigmoid, [ta, atf[0], tnb], bias=NB[:, 16 + m:17 + m])
            t5 = act(nr, nr, ACT.Ln, [t4])
            t6 = act(nr, nr, ACT.Exp, [t5], scale=-0.5, bias=vec("l10"))
            t7 = tt(kk, kk, nr, MUL, [t6])
            t8 = tt(b, kk, AT[:, 0:n], MUL, [t7, ta, tfree[s0 + 2]])
            t9 = ts(nr, AT[:, 0:n], 1.0, vec("ka", m), SUB, MUL, w=[t7])
            atf[0] = [t8, t9]
            t10 = stt(k, nr, 1.0, k, ADD, MUL, [t9])
            tfree[s0 + 1] = [fe_store(f"t{s0 + 1}", 5, kk, m, sg, [t7]), t8]
            tfree[s0 + 2] = [fe_store(f"t{s0 + 2}", 6, b, m, sg, [t8])]
            tfree[s0] = [fe_store(f"t{s0}", 3, k, m, sg, [t10])]
            tfree[s0 + 3] = [t10]
            if c == 0:
                t11 = tt(BS[:, m, :], BS[:, m, :], k, MUL, [t10, rts])
                t12 = ts(BS[:, m, :], BS[:, m, :], vec("rk", m), None, MUL, w=[t11])
                tfree[s0].append(t11)

                def bonus():
                    bi, S, fr = bank()
                    t13 = mm(S[:, 0:n], BONES, BS[:, m, :], True, True, [t12, fr], True)
                    bfree[bi] = cp(AC, BS[:, m, :], S[:, 0:n], [t13])
                deferred.append(bonus)
        deferred.append(norm)
        return t0
    gemm3(8, 8, xsrc, BOTH, ev_k, (), None, xready, xfree)
    mix(3, BOTH)
    DV.wait([AC.last()])
    vc = [0]
    bon = []

    def ev_v(m, sg, B, tok):
        o, n, c = sg
        i = vc[0] % 12
        vc[0] += 1
        v = TM[i][:, 0:n]
        t0 = act(v, B, ACT.Copy, [tok, tfree[i]])
        tfree[i] = [fe_store(f"t{i}", 4, v, m, sg, [t0])]
        if c == 0:
            t1 = tt(BS[:, m, :], BS[:, m, :], v, MUL, [t0])
            tfree[i].append(t1)
            bon.append(dma(SP, "bon", BON[:, m, :], BS[:, m, :], [t1]))
        return t0
    gemm3(8, 8, xsrc, BOTH, ev_v, (), None, xready, xfree)
    fe_done = [tfree, bon[-1], rts]
    for e in (PE, DV, AC, PO, SP):
        e.wait(fe_done)
    fence()
    st.close()
    stC.close()
    back = dma(SP, "x", X[:, :, :], XD)

    st = ExitStack()
    MG = alloc(st, [P, 2, P])
    ML = alloc(st, [P, 2, 6, CH])
    E64 = alloc(st, [P, CH])
    tmk = [dma(AC, "cs", MG[:, :, :], ins["mg"].rearrange("p (a t) -> p a t", a=2)),
           dma(AC, "cs", ML[:, :, :, :], ins["ml"].rearrange("p (a b t) -> p a b t", a=2, b=6)),
           dma(AC, "cs", E64[:, :], ins["e64"])]
    DV.wait(tmk)
    PO.wait(tmk)
    NA = 7
    LD = [alloc(st, [P, NA, 8, CH]) for _ in range(2)]
    AR = [[alloc(st, [P, 8, 2, CH]) for _ in range(2)] for _ in range(2)]
    BK = [alloc(st, [P, 8, 3, CH]) for _ in range(2)]
    GG = [alloc(st, [P, 16, P]) for _ in range(2)]
    OB = [[alloc(st, [P, 8, P]) for _ in range(2)] for _ in range(2)]
    XD = [alloc(st, [P, 8, P]) for _ in range(2)]
    AU = [alloc(st, [P, 8, CH]) for _ in range(2)]
    XA = [alloc(st, [P, 8, CH]) for _ in range(2)]
    PP = [alloc(st, [P, 8, CH]) for _ in range(2)]
    UV = [alloc(st, [P, 16, CH]) for _ in range(2)]
    BT = [alloc(st, [P, 16, CH]) for _ in range(2)]
    EE = [alloc(st, [P, 8, CH]) for _ in range(2)]
    SS = [alloc(st, [P, 8, CH]) for _ in range(2)]
    YY = [alloc(st, [P, 8, CH]) for _ in range(2)]
    GM = [[alloc(st, [P, 3, 8]) for _ in range(2)] for _ in range(2)]
    for d in range(2):
        DV.do((), lambda e, d=d: e.memset(SS[d][:, :, :], 0.0))
        for j in range(2):
            DV.do((), lambda e, d=d, j=j: e.memset(AR[d][j][:, :, :, :], 0.0))
            DV.do((), lambda e, d=d, j=j: e.memset(OB[d][j][:, :, :], 0.0))
        DV.do((), lambda e, d=d: e.memset(XD[d][:, :, :], 0.0))
    tms = DV.last()
    for e in (PE, DV, AC, PO, SP):
        e.wait([tms])

    seqs = [[8, 9, 10, 11] + list(range(8)), [11, 10, 9, 8] + list(range(7, -1, -1))]
    ldf = [[None], [None]]
    yfree = [back, back]
    prev = [dict(), dict()]
    ys_tok = []

    def load(d, i):
        c = seqs[d][i]
        L = LD[d]
        if c >= 8:
            if d == 0:
                a = dma(SP, f"l{d}", L[:, 0:2, :, :], FE[c, :, 0:2, :, :], ldf[d])
                return dma(SP, f"l{d}", L[:, 3:7, :, :], FE[c, :, 3:7, :, :])
            return dma(SP, f"l{d}", L[:, 1:7, :, :], FE[c, :, 3:9, :, :], ldf[d])
        a0 = 0 if d == 0 else 2
        return dma(SP, f"l{d}", L[:, :, :, :], FE[c, :, a0:a0 + 7, :, :], ldf[d])

    ldt = [load(0, 0), load(1, 0)]
    

    def half(par):
        return slice(64 * par, 64 * par + 64)

    fl = lambda B: B[:, :].rearrange("p (a t) -> p a t", t=CH)

    def tilde(d, i):
        c = seqs[d][i]
        main = c < 8
        L, lt, pv = LD[d], ldt[d], prev[d]
        if d == 0:
            pf, lf, r, k, v, kk, b = [L[:, j, :, :] for j in range(7)]
        else:
            r, k, v, kk, b, pf, lf = [L[:, j, :, :] for j in range(7)]
        ar, bk, E, gm = AR[d][i % 2], BK[d], EE[d], GM[d][i % 2]
        last, mid = CH - 1, CH // 2 - 1
        if d == 0:
            t = tt(lf, pf, lf, SUB, [lt])
            gi, ge = pf, lf
        else:
            gl = gm[:, 2, :]
            t = cp(DV, gl, pf[:, :, last], [lt, pv.get(("gm", i % 2))])
            t = tt(pf, gl.unsqueeze(2).broadcast_to([P, 8, CH]), pf, SUB, [t])
            t = tt(lf, pf, lf, ADD, [t])
            gi, ge = lf, pf
        m_ix = mid if d == 0 else CH - 1 - mid
        l_ix = last if d == 0 else 0
        newf = gm[:, 0, :]
        tm = cp(DV, newf, gi[:, :, m_ix], [t, pv.get(("gm", i % 2))])
        mb = newf.unsqueeze(2).broadcast_to([P, 8, CH])
        sl0, sl1 = ar[:, :, 0, :], ar[:, :, 1, :]
        arf = pv.get(("ar", i % 2))
        tb = tt(sl0, ge, mb, SUB, [tm, arf])
        ta = tt(E[:, :, :], gi, mb, SUB, [tm, pv.get("bk")])
        tf = tt(gm[:, 1, :], gi[:, :, l_ix], newf, SUB, [tm])
        ea = act(sl0, sl0, ACT.Exp, [tb])
        if main:
            eb = act(sl1, E[:, :, :], ACT.Exp, [ta, arf])
        ec = act(E[:, :, :], E[:, :, :], ACT.Exp, [ta], scale=-1.0)
        t1 = stt(sl0, sl0, -1.0, kk, MUL, MUL, [ea])
        t3 = tt(bk[:, :, 0, :], E[:, :, :], b, MUL, [ec, pv.get("bk")])
        t4 = tt(bk[:, :, 1, :], E[:, :, :], k, MUL, [ec])
        t2 = tt(sl1, sl1, r, MUL, [eb]) if main else None
        t5 = cp(PO, bk[:, :, 2, :], bk[:, :, 0, :], [t3])
        pv["feats"] = [t1, t2, t3, t4, t5]
        pv["tm"], pv["tf"] = tm, tf

    def unit(d, i):
        c = seqs[d][i]
        main = c < 8
        L, lt, pv = LD[d], ldt[d], prev[d]
        v = L[:, 4, :, :] if d == 0 else L[:, 2, :, :]
        ar, bk, G, gm = AR[d][i % 2], BK[d], GG[d], GM[d][i % 2]
        Xt, Xd, Pm, A = XA[d], XD[d], PP[d], AU[d]
        feats, tm, tf = pv["feats"], pv["tm"], pv["tf"]
        bi, B, fr = bank()
        for h in range(16):
            rows = half(h % 2)
            t = mm(B[rows, (h // 2) * CH:(h // 2) * CH + CH], ar[rows, h // 2, 0, :], bk[rows, h // 2, 0, :],
                   True, True, [fr, feats], h == 15)
        a_t = tt(A[:, :, :], fl(B), MG[:, 1 - d:2 - d, 0:CH].broadcast_to([P, 8, CH]), MUL, [t, pv.get("inv")])
        bfree[bi] = a_t
        n2 = P if main else CH
        gts = []
        for hf in range(2):
            two = [bank(), bank()]
            for j in range(4):
                for par in range(2):
                    bi, B, fr = two[par]
                    h = 8 * hf + 2 * j + par
                    rows = half(par)
                    lhs = bk[rows, h // 2, par:par + 2, :].rearrange("p a t -> p (a t)")
                    t = mm(B[:, j * P:j * P + n2], lhs, ar[rows, h // 2, 0:(2 if main else 1), :].rearrange(
                        "p a t -> p (a t)"), True, True, [fr, feats], j == 3)
            for par in range(2):
                bi, B, fr = two[par]
                h0 = 8 * hf + par
                gts.append(tt(G[:, h0:h0 + 7:2, 0:n2], B[:, :].rearrange("p (j n) -> p j n", j=4)[:, :, 0:n2],
                              MG[:, d:d + 1, 0:n2].broadcast_to([P, 4, n2]), MUL, [t, pv.get("gfree")]))
                bfree[bi] = gts[-1]
        xs = []
        for par in range(2):
            rows = half(par)
            gv = G[rows, par:16:2, 0:CH]
            x1 = tt(Xt[rows, :, :], gv, ML[rows, d, 0:1, :].broadcast_to([64, 8, CH]), MUL, [gts, pv.get("inv")])
            xs.append(x1)
        tx = tt(Xt[:, :, :], Xt[:, :, :], E64[:, :].unsqueeze(1).broadcast_to([P, 8, CH]), ADD, [xs])

        def omask(lev):
            O, key = OB[d][lev % 2], ("o", lev % 2)
            return [tt(O[half(par), :, 64 * par:64 * par + 64], A[half(par), :, :],
                       ML[half(par), 1 - d, lev:lev + 1, :].broadcast_to([64, 8, CH]), MUL, [a_t, pv.get(key)], E=PO)
                    for par in range(2)]
        ot = omask(1)
        yield
        ev_v = []
        for hf in range(2):
            bi, B, fr = bank()
            for j in range(4):
                t = tr(B[0:64, j * 128:j * 128 + 128], v[:, 4 * hf + j, :], ID, [fr, lt], j == 3)
            src = B[0:64, :].rearrange("p (j a c) -> p j a c", j=4, a=2)
            dsto = UV[d][0:64, 8 * hf + 1:8 * hf + 8:2, :]
            dste = UV[d][64:128, 8 * hf:8 * hf + 8:2, :]
            x1 = cp(AC, dsto, src[:, :, 1, :], [t, pv.get("uv")])
            x2 = cp(AC, dste, src[:, :, 0, :], [t, pv.get("uv")])
            bfree[bi] = [x1, x2]
            ev_v += [x1, x2]
        bts = []
        two = [bank(), bank()]
        for j in range(8):
            for par in range(2):
                bi, B, fr = two[par]
                lhs = bk[half(par), j, par:par + 2, :].rearrange("p a t -> p (a t)")
                t = tr(B[:, j * CH:j * CH + CH], lhs, ID[half(par), 64 * par:64 * par + 64], [fr], j == 7)
        for par in range(2):
            bi, B, fr = two[par]
            bts.append(cp((AC, DV)[par], BT[d][:, par:16:2, :], fl(B), [t, pv.get("s_mm")]))
            bfree[bi] = bts[-1]
        pv["bk"] = PE.last()
        ldf[d] = [DV.last(), PE.last(), PO.last(), AC.last()]
        if i + 1 < 12:
            ldt[d] = load(d, i + 1)
        yield
        for lev in range(1, 6):
            if lev < 5:
                on = omask(lev + 1)
            xd = []
            for q in range(2):
                bi, B, fr = bank()
                for p in range(4):
                    t = tr(B[0:64, p * P:p * P + P], Xt[:, 4 * q + p, :], ID, [fr, tx], p == 3)
                src = B[0:64, :].rearrange("p (j a c) -> p j a c", j=4, a=2)
                for par in range(2):
                    xd.append(cp((AC, DV)[q], Xd[half(par), 4 * q:4 * q + 4, 64 * par:64 * par + 64], src[:, :, par, :],
                                 [t, pv.get("xd")]))
                bfree[bi] = xd[-2:]
            bi, B, fr = bank()
            O = OB[d][lev % 2]
            for p in range(8):
                t = mm(B[:, p * CH:p * CH + CH], O[:, p, :], Xt[:, p, :], True, True, [fr, ot], p == 7)
            pv[("o", lev % 2)] = t
            tp = cp(DV if lev % 2 else AC, Pm[:, :, :], fl(B), [t, pv.get("pm")])
            bfree[bi] = tp
            yield
            bi, B, fr = bank()
            for p in range(8):
                t = mm(B[:, p * CH:p * CH + CH], Xd[:, p, :], Pm[:, p, :], True, True, [fr, tp, xd], p == 7)
            pv["pm"] = pv["xd"] = t
            if lev < 5:
                tx = tt(Xt[:, :, :], Xt[:, :, :], fl(B), ADD, [t])
                ot = on
            else:
                tx = [tt(Xd[half(par), :, 64 * par:64 * par + 64], Xt[half(par), :, :], fl(B)[half(par), :, :], ADD,
                         [t]) for par in range(2)]
                pv["inv"] = tx
            bfree[bi] = tx
            yield
        pv["inv"] = [tx, PE.last(), PO.last()]
        S, uv, fx = SS[d], UV[d], pv["fx"]
        te = act(fx[:, 0, :], gm[:, 0, :], ACT.Exp, [tm, pv.get("s_upd")])
        tex = act(fx[:, 1, :], gm[:, 1, :], ACT.Exp, [tf, pv.get("s_upd")])
        tS = tt(S[:, :, :], S[:, :, :], fx[:, 0, :].unsqueeze(2).broadcast_to([P, 8, CH]), MUL, [te, pv.get("s_upd")])
        zb = []
        for which in range(2):
            bi, B, fr = bank()
            for h in range(16):
                par = h % 2
                rows = half(par)
                oth = half(1 - par)
                col = (h // 2) * CH
                if which == 0:
                    t = mm(B[rows, col:col + CH], G[oth, h, 0:CH], uv[oth, h, :], True, True, [fr, ev_v, gts], h == 15)
                else:
                    t = mm(B[rows, col:col + CH], ar[rows, h // 2, 0, :], S[rows, h // 2, :], True, True, [fr, tS],
                           h == 15)
            zb.append((bi, B, t))
        z = Pm
        z0 = cp(AC, z[:, :, :], fl(zb[0][1]), [zb[0][2], pv["pm"]])
        bfree[zb[0][0]] = z0
        zt = tt(z[:, :, :], z[:, :, :], fl(zb[1][1]), ADD, [z0, zb[1][2]])
        bfree[zb[1][0]] = zt
        if i + 1 < 12:
            tilde(d, i + 1)
        yield
        bi, B, fr = bank()
        for p in range(8):
            t = mm(B[:, p * CH:p * CH + CH], Xd[:, p, :], z[:, p, :], True, True, [fr, zt, tx], p == 7)
        pv["pm"] = pv["xd"] = t
        ut = []
        for par in range(2):
            ut.append(cp((AC, DV)[par], uv[half(par), par:16:2, :], fl(B)[half(par), :, :], [t]))
        bfree[bi] = ut
        yield
        bi, B, fr = bank()
        for h in range(16):
            t = mm(B[half(h % 2), (h // 2) * CH:(h // 2) * CH + CH], BT[d][:, h, :], uv[:, h, :], True, True,
                   [fr, bts, ut], h == 15)
        pv["s_mm"] = pv["uv"] = t
        pv["gfree"] = [t, PO.last()]
        bs, BS_ = bi, B
        if main:
            bi, B, fr = bank()
            for h in range(16):
                rows = half(h % 2)
                col = (h // 2) * CH
                mm(B[rows, col:col + CH], S[rows, h // 2, :], ar[rows, h // 2, 1, :], True, False, [fr])
                t = mm(B[rows, col:col + CH], uv[:, h, :], G[:, h, CH:P], False, True, (), h == 15)
            ty = cp(AC, YY[d][:, :, :], fl(B), [t, yfree[d]])
            bfree[bi] = ty
            yfree[d] = dma(SP, f"y{d}", YS[d, c].rearrange("p (a t) -> p a t", t=CH), YY[d][:, :, :], [ty])
            pv["uv"] = t
            pv["gfree"] = [t, PO.last()]
        pv[("ar", i % 2)] = PE.last()
        t = tt(S[:, :, :], S[:, :, :], fl(BS_), ADD, [t])
        bfree[bs] = t
        t = tt(S[:, :, :], S[:, :, :], fx[:, 1, :].unsqueeze(2).broadcast_to([P, 8, CH]), MUL, [t, tex])
        pv["s_upd"] = [t, tex, te]
        pv[("gm", i % 2)] = [tex, te, t]
        yield

    for d in range(2):
        prev[d]["fx"] = alloc(st, [P, 2, 8])
        tilde(d, 0)
    def direction(d):
        for i in range(12):
            yield from unit(d, i)

    gens = [direction(0), direction(1)]
    for _ in range(2):
        next(gens[0])
    interleave(gens, 2)
    for e in (PE, DV, AC, PO, SP):
        e.wait(list(yfree))
    fence()
    st.close()

    st = ExitStack()
    YA = [alloc(st, [P, 8, 8, CH]) for _ in range(2)]
    BO = alloc(st, [P, 8, T])
    splits_begin(st)
    OH, OL = alloc(st, [P, 8, T], F32R), alloc(st, [P, 8, T], F32R)
    tl = [dma(SP, "rd", YA[d][:, :, :, :], YS[d].rearrange("c p (a t) -> p c a t", t=CH)) for d in range(2)]
    tl.append(dma(SP, "rd", BO[:, :, :], BON))
    will_use([("wor", 0)])
    TR = [[alloc(st, [P, T]) for _ in range(2)] for _ in range(4)]
    trf = [None] * 4
    sG, WG, wtG = panel("g2")
    v3 = lambda z: z[:, :].rearrange("p (c t) -> p c t", t=CH)
    oo = {}

    def read_tile(n_):
        m, d = n_ // 2, n_ % 2
        i = n_ % 4
        a, b = TR[i]
        t0 = cp(PO, v3(a), YA[d][:, :, m, :], [tl, trf[i]])
        yield
        bi, B, fr = bank()
        t = mm(B[:, :], BONES, a[:, :], True, True, [t0, fr], True)
        t1 = stt(a[:, :], B[:, :], -1.0 / 64, a[:, :], MUL, ADD, [t])
        bfree[bi] = t1
        t2 = act(b[:, :], a[:, :], ACT.Square, [t1, trf[i]])
        yield
        bi, B, fr = bank()
        t = mm(B[:, :], BONES, b[:, :], True, True, [t2, fr], True)
        t3, t4 = rstd(b[:, :], B[:, :], 1.0 / 64, "egn", [t])
        bfree[bi] = t3
        yield
        t5 = tt(a[:, :], a[:, :], b[:, :], MUL, [t4])
        t6 = act(a[:, :], a[:, :], ACT.Identity, [t5], scale=vec("gng", m), bias=vec("gnb", m))
        yield
        t7 = tt(a[:, :], a[:, :], BO[:, m, :], ADD, [t6])
        bi, B, fr = bank()
        t = mm(B[:, :], WG[:, d * 1024 + m * P:d * 1024 + m * P + P], SG[:, d, :], True, True, [wtG, fr], True)
        t8 = tt(a[:, :], a[:, :], B[:, :], MUL, [t, t7])
        bfree[bi] = t8
        if d == 0:
            oo[m] = (a, t8, i)
        else:
            a0, t0_, i0 = oo[m]
            t9 = tt(a0[:, :], a0[:, :], a[:, :], ADD, [t8, t0_])
            oo["last"] = split(OH[:, m, :], OL[:, m, :], a0[:, :], [t9])
            trf[i] = [t9]
            trf[i0] = [oo["last"]]

    interleave([read_tile(n_) for n_ in range(16)], 4)
    t_o = oo["last"]
    release(sG, PE.last())
    will_use([("wor", j) for j in range(1, 4)])
    gemm3(8, 8, lambda k, sg: (OH[:, k, :], OL[:, k, :]), [MAIN], resid(1, 2), [t_o])
    fence()
    st.close()
    stS.close()

    st = ExitStack()
    splits_begin(st)
    HH, HL = alloc(st, [P, 8, T], F32R), alloc(st, [P, 8, T], F32R)
    hh = rms_mod(res, HH, HL, [MAIN], 1, 1, st)
    mlp(res, [MAIN], st, mlp_keys("m1", "m2", 1), HH, HL,
        lambda m, sg: ADA[:, 1, 5, m, 0:1], None, None, hh)
    fence()
    st.close()

    def layer_norm(g, b, XH, XL):
        st = ExitStack()
        Q = [alloc(st, [P, T]) for _ in range(3)]
        R = alloc(st, [P, T])
        M = alloc(st, [P, T])
        PE.wait([DV.last()])
        bi, B, fr = bank()
        for k in range(8):
            t = mm(B[:, :], ONES, X[:, k, :], k == 0, k == 7, [fr], k == 7)
        t = act(M[:, :], B[:, :], ACT.Copy, [t], scale=1.0 / 1024)
        bfree[bi] = t
        bi, B, fr = bank()
        qf = [None] * 3
        for k in range(8):
            t1 = tt(X[:, k, :], X[:, k, :], M[:, :], SUB, [t])
            t2 = act(Q[k % 3][:, :], X[:, k, :], ACT.Square, [t1, qf[k % 3]])
            t3 = qf[k % 3] = mm(B[:, :], ONES, Q[k % 3][:, :], k == 0, k == 7, [fr, t2], True)
        t4, t5 = rstd(R[:, :], B[:, :], 1.0 / 1024, "e5", [t3])
        bfree[bi] = t4
        for k in range(10):
            if k < 8:
                t6 = tt(X[:, k, :], X[:, k, :], R[:, :], MUL, [t5])
                act(X[:, k, :], X[:, k, :], ACT.Identity, [t6], scale=vec(g, k), bias=vec(b, k))
                qf.append(act(XH[:, k, :], X[:, k, :], ACT.Copy, [AC.last()]))
            if k > 1:
                j = k - 2
                t8 = tt(XL[:, j, :], X[:, j, :], XH[:, j, :].bitcast(F32), SUB, [qf[3 + j]])
        fence()
        st.close()
        return t8

    def ffn_ple(l):
        st = ExitStack()
        splits_begin(st)
        XH, XL = alloc(st, [P, 8, T], F32R), alloc(st, [P, 8, T], F32R)
        xh = lambda k, sg: (XH[:, k, :], XL[:, k, :])
        layer_norm(f"ln1g{l}", f"ln1b{l}", XH, XL)
        st2 = ExitStack()
        mlp(lambda k, sg: X[:, k, :], [MAIN], st2, mlp_keys("f1", "f2", l), XH, XL, None, None, ALPHA)
        fence()
        st2.close()
        PTt = alloc(st, [P, 2, T])
        tp = dma(AC, "cs", PTt[:, :, :], ins[f"p{l}"].rearrange("p (k t) -> p k t", k=2))
        EM = alloc(st, [P, 8, T])
        SQ = [alloc(st, [P, T]) for _ in range(2)]
        R = alloc(st, [P, T])
        s, W, wt = panel(("pp", l))
        for m in range(8):
            bi, B, fr = bank()
            for k in range(2):
                t = mm(B[:, :], W[:, k * 1024 + m * P:k * 1024 + m * P + P], PTt[:, k, :], k == 0, k == 1,
                       [wt, fr, tp], k == 1)
            t1 = cp(AC, EM[:, m, :], B[:, :], [t])
            bfree[bi] = t1
        release(s, t)
        bi, B, fr = bank()
        sf = [None, None]
        for m in range(8):
            t2 = act(SQ[m % 2][:, :], EM[:, m, :], ACT.Square, [t1, sf[m % 2]])
            t3 = mm(B[:, :], ONES, SQ[m % 2][:, :], m == 0, m == 7, [fr, t2], True)
            sf[m % 2] = t3
        t4, t5 = rstd(R[:, :], B[:, :], 1.0 / 1024, "e5", [t3])
        bfree[bi] = t4
        for m in range(8):
            t6 = stt(EM[:, m, :], EM[:, m, :], vec(f"plg{l}", m), R[:, :], MUL, MUL, [t5])
        layer_norm(f"ln2g{l}", f"ln2b{l}", XH, XL)
        will_use([("pg", l, j) for j in range(4)])
        Gt = [alloc(st, [P, T]) for _ in range(2)]
        gf = [None, None]

        def ev(m, sg, B, tok):
            g = Gt[m % 2][:, :]
            t = act(g, B, ACT.Sigmoid, [tok, gf[m % 2]])
            t1 = tt(g, g, EM[:, m, :], MUL, [t, t6])
            gf[m % 2] = tt(X[:, m, :], g, X[:, m, :], ADD, [t1])
            return t
        gemm3(8, 8, xh, [MAIN], ev)
        fence()
        st.close()

    st = ExitStack()
    splits_begin(st)
    will_use([(a, j) for a in ("qa", "ka", "va", "hq", "hf", "hi", "hg", "evo") for j in range(4 if a == "evo" else 2)])
    XH, XL = alloc(st, [P, 8, T], F32R), alloc(st, [P, 8, T], F32R)
    xh = lambda k, sg: (XH[:, k, :], XL[:, k, :])
    xht = lambda k, tb: (XH[:, k, tb * P:tb * P + P], XL[:, k, tb * P:tb * P + P])
    for k in range(8):
        t_x = split(XH[:, k, :], XL[:, k, :], X[:, k, :])
    CS = alloc(st, [P, 2, T])
    tcs = dma(AC, "cs", CS[:, :, :], ins["cs1"].rearrange("p (a t) -> p a t", a=2))
    MK = alloc(st, [P, 4, P])
    CZ = alloc(st, [P, 3, P])
    tcs = [tcs, dma(AC, "cs", MK[:, :, :], ins["ck"].rearrange("p (a t) -> p a t", a=4)),
           dma(AC, "cs", CZ[:, :, :], ins["cz"].rearrange("p (a t) -> p a t", a=3))]
    for e in (DV, PO):
        e.wait(tcs)
    Q4 = alloc(st, [P, 4, T])
    K4 = alloc(st, [P, 4, T])
    VA = alloc(st, [P, 4, 512])
    OM = alloc(st, [P, 8, T])
    TQ = [alloc(st, [P, T]) for _ in range(4)]

    def rope_evac(dst, m0, TQ):
        fr2 = [[None], [None]]
        n = [0]

        def f(m, sg, B, tok):
            i = n[0] % 2
            n[0] += 1
            a, b = TQ[2 * i][:, :], TQ[2 * i + 1][:, :]
            t0 = act(a, B, ACT.Copy, [tok] + fr2[i])

            def rope():
                bi, S, fr = bank()
                t1 = mm(S[:, :], PERM[1], a, True, True, [t0, fr], True)
                t2 = tt(b, S[:, :], CS[:, 1, :], MUL, [t1] + fr2[i])
                bfree[bi] = t2
                t3 = tt(dst[:, m, :], a, CS[:, 0, :], MUL, [t0])
                t4 = tt(dst[:, m, :], dst[:, m, :], b, ADD, [t3, t2])
                fr2[i] = [t4, t1]
            deferred.append(rope)
            return t0
        return f

    gemm3(4, 8, xh, [MAIN], rope_evac(Q4, 0, TQ), [t_x])
    fence()
    gemm3(4, 8, xh, [MAIN], rope_evac(K4, 0, TQ))
    st_v = ExitStack()
    gemm3_tok(4, xh, [MAIN], VA, st_v)
    fence()
    st_v.close()
    t = tt(SM[0:64, 0:1], vec("lam", 0, 1, slice(0, 64)), vec("lam", 1, 1, slice(0, 64)), MUL)
    t = [t, tt(SM[0:64, 1:2], vec("lam", 2, 1, slice(0, 64)), vec("lam", 3, 1, slice(0, 64)), MUL)]
    bi, B, fr = bank()
    t = mm(B[:, 0:2], ONES[0:64, :], SM[0:64, 0:2], True, True, [t, fr], True)
    t = act(SM[:, 2:4], B[:, 0:2], ACT.Exp, [t])
    bfree[bi] = t
    t = tt(SM[:, 4:5], SM[:, 3:4], SM[:, 2:3], SUB, [t])
    t_lam = ts(SM[:, 4:5], SM[:, 4:5], -(0.8 - 0.6), None, ADD, w=[t])
    fence()
    stD = ExitStack()
    S2 = [alloc(stD, [P, 2, T]) for _ in range(3)]
    P2 = [alloc(stD, [P, 4, P]) for _ in range(3)]
    NS = alloc(stD, [P, 3, 2, 4])
    s2f, p2f = [None] * 3, [None] * 3
    un2 = 0

    def diff_unit(h, qb, u):
        nk = (qb + 1) * P
        S, Pt, sm = S2[u], P2[u], NS[:, u, :, :]
        ev = []
        for c in range(2):
            rows = slice(64 * c, 64 * c + 64)
            bi, B, fr = bank()
            t = mm(B[:, 0:nk], Q4[rows, h, qb * P:qb * P + P], K4[rows, h, 0:nk], True, True, [fr], True)
            r = stt(S[:, c, 0:nk], B[:, 0:nk], 0.125, MK[:, 3 - qb:4, :].rearrange("p a b -> p (a b)"), MUL, ADD,
                    [t, s2f[u]])
            bfree[bi] = r
            ev.append(r)
        mx, ng, dn = sm[:, :, 0], sm[:, :, 1], sm[:, :, 2]
        t = rmax(mx, S[:, :, 0:nk], ev)
        t = ts(ng, mx, -1.0, None, MUL, w=[t])
        yield
        ee = [act(S[:, c, 0:nk], S[:, c, 0:nk], ACT.Exp, [t], bias=ng[:, c:c + 1], accum_out=dn[:, c:c + 1])
              for c in range(2)]
        t = recip(dn, dn, ee)
        t = tt(dn[:, 1:2], dn[:, 1:2], SM[:, 4:5], MUL, [t])
        a = ts(S[:, 0, 0:nk], S[:, 0, 0:nk], dn[:, 0:1], None, MUL, w=[t])
        pn = stt(S[:, 0, 0:nk], S[:, 1, 0:nk], dn[:, 1:2], S[:, 0, 0:nk], MUL, ADD, [a])

        yield
        bi, B, fr = bank()
        for b in range(qb + 1):
            t = tr(B[:, b * P:b * P + P], S[:, 0, b * P:b * P + P], ID, [fr, pn], b == qb)
        s2f[u] = t
        r = cp(AC, Pt[:, 0:qb + 1, :], B[:, 0:nk].rearrange("p (a b) -> p a b", b=P), [t, p2f[u]])
        bfree[bi] = r
        bi, B, fr = bank()
        for b in range(qb + 1):
            t = mm(B[:, 0:P], VA[:, b, h * P:h * P + P], Pt[:, b, :], b == 0, b == qb, [fr, r], b == qb)
        p2f[u] = t
        bfree[bi] = cp(DV, OM[:, h, qb * P:qb * P + P], B[:, 0:P], [t])

    for qb in range(4):
        for h in range(4):
            attend(diff_unit(h, qb, un2 % 3))
            un2 += 1
    attend_end()

    fence()
    tq_ = [act(TQ[h][:, :], OM[:, h, :], ACT.Square) for h in range(4)]
    for h in range(4):
        bi, B, fr = bank()
        t = mm(B[:, :], ONES, TQ[h][:, :], True, True, [tq_[h], fr], True)
        bfree[bi], t = rstd(TQ[h][:, :], B[:, :], 1.0 / 128, "e5", [t])
        t = stt(OM[:, h, :], OM[:, h, :], vec("subg"), TQ[h][:, :], MUL, MUL, [t])
        ts(OM[:, h, :], OM[:, h, :], 1.0 - (0.8 - 0.6), None, MUL, w=[t])
    fence()
    stD.close()
    LF = alloc(st, [P, 4, T])
    SCN = alloc(st, [P, T])
    DV.wait([dma(AC, "cs", SCN[:, :], ins["scn"][:, 0:T])])
    LB = alloc(st, [P, 2, 4])
    lb2 = vec("lb", 0, 8).rearrange("p (a b) -> p a b", a=2)
    L3 = alloc(st, [P, 3, 4])
    t = tt(L3[:, 0, :], lb2[:, 0, :], lb2[:, 1, :], MAX)
    ta_ = tt(L3[:, 1, :], lb2[:, 0, :], L3[:, 0, :], SUB, [t])
    tb_ = tt(L3[:, 2, :], lb2[:, 1, :], L3[:, 0, :], SUB, [t])
    t = act(L3[:, 1:3, :], L3[:, 1:3, :], ACT.Exp, [ta_, tb_])
    t = tt(L3[:, 0, :], L3[:, 1, :], L3[:, 2, :], ADD, [t])
    t = recip(L3[:, 0, :], L3[:, 0, :], [t])
    t = tt(LB[:, 0, :], L3[:, 1, :], L3[:, 0, :], MUL, [t])
    t_lb = ts(LB[:, 1, :], LB[:, 0, :], -1.0, 1.0, MUL, ADD, w=[t])
    fr4 = [[None]] * 4

    def ev_silu(dst, T0):
        fr = [[None], [None]]

        def f(m, sg, B, tok):
            i = m % 2
            a = T0[2 * i][:, :]
            t0 = act(a, B, ACT.Sigmoid, [tok] + fr[i])
            t1 = tt(dst[:, m, :], B, a, MUL, [t0])
            fr[i] = [t1]
            return t1
        return f

    def ev_f(m, sg, B, tok):
        t2 = t0 = act(K4[:, m, :], B, ACT.Sigmoid, [tok])
        t3 = ts(LF[:, m, :], K4[:, m, :], LB[:, 1, m:m + 1], LB[:, 0, m:m + 1], MUL, ADD, w=[t2, t_lb])
        t4 = ts(K4[:, m, :], LF[:, m, :], -1.0, 1.0, MUL, ADD, w=[t3])
        lf_toks.append((m, t4))
        return t0
    lf_toks = []
    gemm3(4, 8, xh, [MAIN], ev_silu(Q4, TQ))
    gemm3(4, 8, xh, [MAIN], ev_f)
    for m, t4 in lf_toks:
        act(LF[:, m, :], LF[:, m, :], ACT.Ln, [t4])
    st_v = ExitStack()
    gemm3_tok(4, xh, [MAIN], VA, st_v)
    fence()
    st_v.close()
    fence()
    HG = alloc(st, [P, 4, T])
    gemm3(4, 8, xh, [MAIN], ev_silu(HG, TQ))
    CB = alloc(st, [P, 4, T])
    W2 = [[TQ[0], TQ[1], TQ[2], TQ[3]], [alloc(st, [P, T]) for _ in range(4)]]
    KSTs = [alloc(st, [P, 4, P]) for _ in range(2)]
    AAs = [[alloc(st, [P, CH]) for _ in range(2)] for _ in range(2)]
    DCs = [alloc(st, [P, 8]) for _ in range(2)]
    SHs = [alloc(st, [P, P]) for _ in range(2)]
    MU = alloc(st, [P, CH], mybir.dt.uint32)
    tmu = ts(MU[:, :], CZ[:, 1, 0:CH], 1.0, None, MUL)
    fence()
    c3 = lambda z: z.rearrange("p (c t) -> p c t", t=CH)
    hdone = [None, None]

    def hgrn_head(h):
        x = h % 2
        QP, KP, QO, KS = W2[x]
        KST, AA, DC, SH = KSTs[x], AAs[x], DCs[x], SHs[x]
        b_, l_ = CB[:, h, :], LF[:, h, :]
        t0 = DV.do([hdone[x]], lambda e: e.tensor_tensor_scan(b_, SCN[:, :], l_, 0.0, MUL, ADD))
        bc = c3(b_)
        mid = bc[:, :, CH // 2 - 1:CH // 2].broadcast_to([P, 8, CH])
        las = bc[:, :, CH - 1:CH].broadcast_to([P, 8, CH])
        q_, k_ = Q4[:, h, :], K4[:, h, :]
        t1 = tt(c3(QP[:, :]), bc, mid, SUB, [t0])
        t5 = tt(c3(KS[:, :]), las, bc, SUB, [t0])
        t2 = act(KP[:, :], QP[:, :], ACT.Exp, [t1], scale=-1.0)
        t3 = act(QP[:, :], QP[:, :], ACT.Exp, [t1])
        t4 = act(QO[:, :], b_, ACT.Exp, [t0])
        t6 = act(KS[:, :], KS[:, :], ACT.Exp, [t5])
        t7 = act(DC[:, :], bc[:, :, CH - 1], ACT.Exp, [t0])
        u = [tt(QP[:, :], QP[:, :], q_, MUL, [t3, t2]), tt(KP[:, :], KP[:, :], k_, MUL, [t2]),
             tt(KS[:, :], KS[:, :], k_, MUL, [t6]), tt(QO[:, :], QO[:, :], q_, MUL, [t4])]
        tS = DV.do([hdone[x]], lambda e: e.memset(SH[:, :], 0.0))
        for i in range(2):
            tz = DV.do([hdone[x]], lambda e, i=i: e.memset(AA[i][:, :], 0.0))
        yield
        bi, B, fr = bank()
        for tb in range(4):
            t = tr(B[:, tb * P:tb * P + P], KS[:, tb * P:tb * P + P], ID, [fr, u], tb == 3)
        tk = cp(AC, KST[:, :, :], B[:, :].rearrange("p (a b) -> p a b", b=P), [t])
        bfree[bi] = tk
        aaf = [None, None]
        atok = {}

        def intra(c):
            rows = slice(64 * (c % 2), 64 * (c % 2) + 64)
            A = AA[(c // 2) % 2]
            bi, B, fr = bank()
            cc = slice(c * CH, c * CH + CH)
            r0, c0, hf = rows.start, c * CH, CH // 2
            mm(B[r0:r0 + hf, 0:CH], KP[:, c0:c0 + hf], QP[:, cc], True, True, [fr, u])
            t = mm(B[r0 + hf:r0 + CH, hf:CH], KP[:, c0 + hf:c0 + CH], QP[:, c0 + hf:c0 + CH], True, True, (), True)
            w = [t, aaf[(c // 2) % 2], tmu, tz]
            q4 = []
            for r, co in ((r0, 0), (r0 + hf, hf)):
                am, bm, mm_ = A[r:r + hf, co:CH], B[r:r + hf, co:CH], MU[r:r + hf, co:CH]
                q4.append(DV.do(w, lambda e, am=am, bm=bm, mm_=mm_: e.copy_predicated(am, mm_, bm)))
            atok[c] = q4
            bfree[bi] = atok[c]
        intra(0)
        intra(1)
        yield
        for c in range(8):
            rows = slice(64 * (c % 2), 64 * (c % 2) + 64)
            A = AA[(c // 2) % 2]
            cc = slice(c * CH, c * CH + CH)
            v_ = VA[rows, c // 2, h * P:h * P + P]
            if c < 7:
                bj, B2, fr2 = bank()
                t2 = mm(B2[:, 0:P], KST[rows, c // 2, :], v_, True, True, [fr2, tk], True)
            bi, B, fr = bank()
            mm(B[:, 0:CH], v_, A[rows, :], True, False, [fr, atok[c]])
            t = mm(B[:, 0:CH], SH[:, :], QO[:, cc], False, True, [tS], True)
            aaf[(c // 2) % 2] = t
            bfree[bi] = to = cp(AC, OM[:, 4 + h, cc], B[:, 0:CH], [t])
            if c < 7:
                tS = stt(SH[:, :], SH[:, :], DC[:, c:c + 1], B2[:, 0:P], MUL, ADD, [t2, tS, t7, t])
                bfree[bj] = tS
            if c % 2 == 1 and c < 7:
                intra(c + 1)
                intra(c + 2)
            yield
        ap = OM[:, 4 + h, :]
        t = act(QP[:, :], ap, ACT.Square, [to, PE.last()])
        yield
        bi, B, fr = bank()
        t = mm(B[:, :], ONES, QP[:, :], True, True, [t, fr], True)
        bfree[bi], t = rstd(KP[:, :], B[:, :], 1.0 / 128, "e5", [t])
        t = stt(ap, ap, vec("hgg"), KP[:, :], MUL, MUL, [t])
        hdone[x] = [tt(ap, ap, HG[:, h, :], MUL, [t]), PE.last(), AC.last()]

    interleave([hgrn_head(h) for h in range(4)], 2)
    fence()

    def ev_mix(m, sg, B, tok):
        return stt(X[:, m, :], X[:, m, :], ALPHA, B, MUL, ADD, [tok])
    for k in range(8):
        t_o = split(XH[:, k, :], XL[:, k, :], OM[:, k, :])
    gemm3(8, 8, xh, [MAIN], ev_mix, [t_o])
    fence()
    st.close()
    ffn_ple(0)

    st = ExitStack()
    CS = alloc(st, [P, 2, T])
    tcs = [dma(AC, "cs", CS[:, :, :], ins["cs1"].rearrange("p (a t) -> p a t", a=2))]
    MK = alloc(st, [P, 4, P])
    tcs.append(dma(AC, "cs", MK[:, :, :], ins["mk"].rearrange("p (a t) -> p a t", a=4)))
    DV.wait(tcs)
    XH, XL = alloc(st, [P, 8, T], F32R), alloc(st, [P, 8, T], F32R)
    splits_begin(st, 2)
    will_use([(a, j) for a in ("oq", "ok", "ov", "odo") for j in range(4)])
    xh = lambda k, sg: (XH[:, k, :], XL[:, k, :])
    for k in range(8):
        t_x = split(XH[:, k, :], XL[:, k, :], X[:, k, :])
    Q8 = alloc(st, [P, 8, T])
    K8 = alloc(st, [P, 8, T])
    V8 = alloc(st, [P, 4, 1024])
    OM = alloc(st, [P, 8, T])
    st2 = ExitStack()
    TQ = [alloc(st2, [P, T]) for _ in range(4)]
    gemm3(8, 8, xh, [MAIN], rope_evac(Q8, 0, TQ), [t_x])
    fence()
    gemm3(8, 8, xh, [MAIN], rope_evac(K8, 0, TQ))
    gemm3_tok(8, xh, [MAIN], V8, st2)
    fence()
    st2.close()
    S4 = [alloc(st, [P, 4, T]) for _ in range(3)]
    P4 = [alloc(st, [P, 4, 512]) for _ in range(2)]
    NS = alloc(st, [P, 3, 4, 4])
    s4f, p4f = [None] * 3, [None, None]

    def dil_unit(g, qb, u, v):
        nk = (qb + 1) * P
        S, Pt, sm = S4[u], P4[v], NS[:, u, :, :]
        mk = MK[:, 3 - qb:4, :].rearrange("p a b -> p (a b)")
        ev = []
        for i in range(4):
            h = 4 * g + i
            rows = slice(64 * (h % 2), 64 * (h % 2) + 64)
            bi, B, fr = bank()
            t = mm(B[:, 0:nk], Q8[rows, h // 2, qb * P:qb * P + P], K8[rows, h // 2, 0:nk], True, True, [fr], True)
            r = stt(S[:, i, 0:nk], B[:, 0:nk], 0.125, mk, MUL, ADD, [t, s4f[u]])
            bfree[bi] = r
            ev.append(r)
        mx, ng, dn = sm[:, :, 0], sm[:, :, 1], sm[:, :, 2]
        t = rmax(mx, S[:, :, 0:nk], ev)
        t = ts(ng, mx, -1.0, None, MUL, w=[t])
        yield
        ee = [act(S[:, c, 0:nk], S[:, c, 0:nk], ACT.Exp, [t], bias=ng[:, c:c + 1], accum_out=dn[:, c:c + 1])
              for c in range(4)]
        t = recip(dn, dn, ee)
        pn = [ts(S[:, i, 0:nk], S[:, i, 0:nk], dn[:, i:i + 1], None, MUL, w=[t]) for i in range(4)]

        yield
        pts = []
        for b in range(qb + 1):
            bi, B, fr = bank()
            for i in range(4):
                t = tr(B[:, i * P:i * P + P], S[:, i, b * P:b * P + P], ID, [fr, pn], i == 3)
            r = cp(AC, Pt[:, b, :], B[:, :], [t, p4f[v]])
            bfree[bi] = r
            pts.append(r)
        s4f[u] = PE.last()
        bi, B, fr = bank()
        for i in range(4):
            h = 4 * g + i
            rows = slice(64 * (h % 2), 64 * (h % 2) + 64)
            col = (i // 2) * P
            for b in range(qb + 1):
                t = mm(B[rows, col:col + P], V8[:, b, h * 64:h * 64 + 64], Pt[:, b, i * P:i * P + P], b == 0,
                       b == qb, [fr, pts], i == 3 and b == qb)
        p4f[v] = t
        bfree[bi] = cp(AC, OM[:, 2 * g:2 * g + 2, qb * P:qb * P + P],
                       B[:, 0:256].rearrange("p (a b) -> p a b", b=P), [t])

    n = 0
    for qb in range(4):
        for g in range(4):
            attend(dil_unit(g, qb, n % 3, n % 2))
            n += 1
    attend_end()
    t_o = AC.last()
    for k in range(8):
        t_o = split(XH[:, k, :], XL[:, k, :], OM[:, k, :], [t_o])
    gemm3(8, 8, xh, [MAIN], ev_mix, [t_o])
    fence()
    st.close()
    ffn_ple(1)

    t = dma(SP, "out", out_d, X[:, :, :].rearrange("p k t -> p (k t)"))
    SP.wait([t])

    block = ctx.enter_context(nc.Block())

    @block.tensor
    def _(e):
        PE.emit(e)

    @block.vector
    def _(e):
        DV.emit(e)

    @block.scalar
    def _(e):
        AC.emit(e)

    @block.gpsimd
    def _(e):
        PO.emit(e)

    @block.sync
    def _(e):
        SP.emit(e)

    ctx.close()


def constants():
    f = np.float32
    c = {}
    i = np.arange(P)
    cst = np.zeros((P, 5, P), f)
    cst[:, 0] = np.eye(P)
    cst[:, 1] = 1
    cst[:, 2] = (i[:, None] // 64 == i[None, :] // 64)
    for m in range(P):
        r = m % 32
        if r < 16:
            cst[m + 16, 3, m] = -1
        else:
            cst[m - 16, 3, m] = 1
        r = m % 64
        if r < 8:
            cst[m + 8, 4, m] = -1
        elif r < 16:
            cst[m - 8, 4, m] = 1
    c["cst"] = cst.reshape(P, -1)
    t = np.arange(T)
    fr = f(10000.0) ** (-np.arange(16, dtype=f) / f(16))
    pos = np.where((i % 64 < 32)[:, None], (t // 64)[None, :], (t % 64)[None, :]).astype(f)
    ang = (pos * fr[i % 16][:, None]).astype(f)
    c["cs0"] = np.concatenate([np.cos(ang), np.sin(ang)], 1).astype(f)
    inv = f(500000.0) ** (-np.arange(0, 16, 2, dtype=f) / f(16))
    ang = (t[None, :].astype(f) * inv[i % 8][:, None]).astype(f)
    rot = (i % 64 < 16)[:, None]
    c["cs1"] = np.concatenate([np.where(rot, np.cos(ang), 1), np.where(rot, np.sin(ang), 0)], 1).astype(f)
    q, k = i[:, None], i[None, :]
    z = np.zeros((P, P))
    c["wm"] = np.concatenate([np.where(k >= q, 0, NEG), z, np.where(k <= q, 0, NEG)], 1).astype(f)

    def mult(off):
        d = q - k + off
        ok = d >= 0
        n = (ok & (d <= 128)).astype(int) + (ok & (d % 4 == 0)) + (ok & (d % 16 == 0))
        return np.where(n > 0, np.log(np.maximum(n, 1)), NEG)
    c["mk"] = np.concatenate([mult(384), mult(256), mult(128), mult(0)], 1).astype(f)
    c["ck"] = np.concatenate([z, z, z, np.where(k <= q, 0, NEG)], 1).astype(f)
    s64, t64 = (i % 64)[:, None], np.arange(64)[None, :]
    c["cz"] = np.concatenate([np.where(k <= q, 0, NEG), np.tile(s64 <= t64, (1, 2)).astype(f), z], 1).astype(f)
    c["scn"] = np.tile((np.arange(TT) % CH != 0).astype(f), (P, 1))
    c["mg"] = np.concatenate([s64 < t64, s64 <= t64, s64 > t64, s64 >= t64], 1).astype(f)
    ml = []
    for d in range(2):
        for lev in range(6):
            n = 1 << lev
            a, b = (s64, t64) if d == 0 else (t64, s64)
            ml.append((a // (2 * n) == b // (2 * n)) & (a // n % 2 == 0) & (b // n % 2 == 1))
    c["ml"] = np.concatenate(ml, 1).astype(f)
    c["e64"] = (s64 == t64).astype(f)
    return {k_: np.ascontiguousarray(v, dtype=f) for k_, v in c.items()}


def _cols(v):
    return np.ascontiguousarray(np.asarray(v).reshape(-1, P).T)


def _fm(a):
    a = np.asarray(a)
    return np.ascontiguousarray(a.T.reshape(a.shape[1] // P, P, a.shape[0]).transpose(1, 0, 2).reshape(P, -1))


def _panel(W):
    K, N = W.shape
    return W.reshape(K // P, P, N).transpose(1, 0, 2).reshape(P, -1)


def lay_out(inp):
    f = np.float32
    g = {k: np.asarray(v) for k, v in inp.items()}
    vec = np.zeros((P, NVEC), f)

    def put(name, a):
        s, n = VCOLS[name]
        vec[:a.shape[0], s:s + n] = a
    for l in range(2):
        put(f"adab{l}", _cols(g["ada_b"][l]))
        put(f"n1{l}", _cols(g["norm1_g"][l]))
        put(f"n2{l}", _cols(g["norm2_g"][l]))
        put(f"ln1g{l}", _cols(g["ln1_g_2"][l]))
        put(f"ln1b{l}", _cols(g["ln1_b_2"][l]))
        put(f"ln2g{l}", _cols(g["ln2_g_2"][l]))
        put(f"ln2b{l}", _cols(g["ln2_b_2"][l]))
        put(f"plg{l}", _cols(g["ple_norm_g_2"][l]))
    put("qg", np.tile(g["att_q_gain"][0], 2)[:, None])
    put("kg", np.tile(g["att_k_gain"][0], 2)[:, None])
    put("sink", np.tile(g["att_sink"][0][None, :], (P, 1)))
    put("mu", _cols(g["rwkv_mu"][0]))
    put("w0", _cols(g["rwkv_w0"][0]))
    put("a0", _cols(g["rwkv_a0"][0]))
    put("kk", _cols(g["rwkv_k_k"][0]))
    put("ka", _cols(g["rwkv_k_a"][0]))
    put("rk", _cols(g["rwkv_r_k"][0]))
    put("gng", _cols(g["rwkv_gn_g"][0]))
    put("gnb", _cols(g["rwkv_gn_b"][0]))
    put("c", np.stack([_cols(g["c"][0]), _cols(g["c_ctx"])], 2).reshape(P, 16))
    put("subg", g["da_subln_g_2"][0][:, None])
    put("hgg", g["hg_norm_g_2"][0][:, None])
    put("lb", _cols(g["hg_lb_logits_2"]))
    put("lam", g["da_lambda_2"][0].T)
    for name, v in (("e6", 1e-6), ("e5", 1e-5), ("egn", 64e-5), ("l10", 10 * np.log(2.0))):
        put(name, np.full((P, 1), v, f))
    qcols = np.concatenate([np.arange(64) + 64 * h for pr in PAIRS for h in pr])
    wqkv = g["att_w_qkv"][0]
    evi, odi = g["ev_w_in_2"][0], g["od_w_in_2"][0]

    def cut(W, j):
        return _panel(W[:, 256 * j:256 * j + 256])

    def one(key):
        if key == "loraA":
            return _panel(np.concatenate([g["rwkv_w1"][0, 0], g["rwkv_w1"][0, 1], g["rwkv_a1"][0],
                                          np.zeros((1024, 64), f)], 1))
        if key == "loraB":
            a = np.zeros((P, 2048), f)
            a[0:64, 0:1024] = g["rwkv_w2"][0, 0]
            a[64:128, 0:1024] = g["rwkv_w2"][0, 1]
            a[0:64, 1024:2048] = g["rwkv_a2"][0]
            return a
        if key == "g1":
            return _panel(np.concatenate([g["rwkv_g1"][0, 0], g["rwkv_g1"][0, 1]], 1))
        if key == "g2":
            return np.concatenate([g["rwkv_g2"][0, 0], g["rwkv_g2"][0, 1]], 1)
        k, j = key[0], key[-1]
        if k == "ada":
            return cut(g["ada_w"][key[1]], j)
        if k == "q":
            return cut(wqkv[:, qcols], j)
        if k == "k":
            return cut(wqkv[:, 1024:], 0)
        if k == "v":
            return cut(wqkv[:, 1280:], 0)
        if k == "wo":
            return cut(g["att_w_o"][0][qcols], j)
        if k in ("m1", "f1"):
            return cut(g["mlp_w1" if k == "m1" else "ffn_w1_2"][key[1]], j)
        if k in ("m2", "f2"):
            w = g["mlp_w2" if k == "m2" else "ffn_w2_2"][key[1]]
            q, c = j // 2, j % 2
            return _panel(w[512 * q:512 * q + 512, 512 * c:512 * c + 512])
        if k in ("r", "kr", "vr"):
            return cut(g["rwkv_w_rkv"][0, ("r", "kr", "vr").index(k)], j)
        if k == "wor":
            return cut(g["rwkv_w_o"][0], j)
        if k in ("qa", "ka", "va", "hq", "hf", "hi", "hg"):
            return cut(evi[:, 512 * ("qa", "ka", "va", "hq", "hf", "hi", "hg").index(k):], j)
        if k == "evo":
            return cut(g["ev_w_out_2"][0], j)
        if k in ("oq", "ok", "ov"):
            return cut(odi[:, 1024 * ("oq", "ok", "ov").index(k):], j)
        if k == "odo":
            return cut(g["od_w_out_2"][0], j)
        if k == "pp":
            return _panel(g["ple_w_proj_2"][key[1]])
        if k == "pg":
            return cut(g["ple_w_gate_2"][key[1]], j)
        raise ValueError(key)

    arrays = dict(constants())
    arrays["vec"] = vec
    arrays["xT"] = _fm(g["x"][0])
    arrays["ctxT"] = _fm(g["ctx"][0])
    arrays["p0"] = _fm(g["p_2"][0, 0])
    arrays["p1"] = _fm(g["p_2"][1, 0])
    return arrays, one


NPANELS = 250


def kernel(**inputs):
    import concourse.bacc as _bacc
    from concourse.bass_utils import run_bass_kernel_spmd as _run

    arrays, one = lay_out(inputs)
    nc = _bacc.Bacc("TRN2", target_bir_lowering=False, num_devices=1)
    dt = mybir.dt.float32
    ins = {}
    for name, a in arrays.items():
        ins[name] = nc.dram_tensor("in_" + name, a.shape, dt, kind="ExternalInput").ap()
    ins["w"] = nc.dram_tensor("in_w", (NPANELS, P, 2048), dt, kind="ExternalInput").ap()
    scratch = {
        "fe": nc.dram_tensor("s_fe", (12, P, 9, 8, CH), dt, kind="Internal").ap(),
        "bon": nc.dram_tensor("s_bon", (P, 8, T), dt, kind="Internal").ap(),
        "ys": nc.dram_tensor("s_ys", (2, 8, P, 8 * CH), dt, kind="Internal").ap(),
    }
    out = nc.dram_tensor("out_0", (P, 8 * T), dt, kind="ExternalOutput").ap()
    order = []
    program(nc, ins, out, scratch, NPANELS, order)
    assert len(order) == NPANELS, len(order)
    arrays["w"] = np.stack([one(k) for k in order])
    r = _run(nc, [{("in_" + k): v for k, v in arrays.items()}], core_ids=[0])
    got = r.results[0]["out_0"]
    return np.ascontiguousarray(got.reshape(P, 8, T).transpose(2, 1, 0).reshape(1, T, 1024))
```
